# Optimizing a Trainium2 kernel written in Bass

```python
import math
import jax, jax.numpy as jnp
from jax import lax
import numpy as np

D_MODEL = 1024
BATCH = 1
SEQ = 1024
DEPTH = 1

SB_HEADS = 8
SB_HEAD_DIM = 64
SB_WIDTH = SB_HEADS * SB_HEAD_DIM
SB_BLOCK = 128
HG_HEADS = 4
HG_DK = 128
HG_DV = 128
HG_WIDTH_K = HG_HEADS * HG_DK
HG_WIDTH_V = HG_HEADS * HG_DV
HG_CHUNK = 64
HG_F_FLOOR = 1e-30
SSD_HEADS = 8
SSD_HEAD_DIM = 64
SSD_WIDTH = SSD_HEADS * SSD_HEAD_DIM
SSD_GROUPS = 2
SSD_STATE = 64
SSD_CONV = 4
SSD_CHUNK = 128
SSD_CONV_DIM = SSD_WIDTH + 2 * SSD_GROUPS * SSD_STATE
N_BRANCHES = 3
IN_SIZES = (SB_WIDTH, SB_WIDTH, SB_WIDTH,
            HG_WIDTH_K, HG_WIDTH_K, HG_WIDTH_V, HG_WIDTH_V,
            SSD_WIDTH, SSD_CONV_DIM, SSD_HEADS,
            D_MODEL, D_MODEL, D_MODEL)
IN_COLS = 3 * SB_WIDTH + 2 * HG_WIDTH_K + 2 * HG_WIDTH_V + SSD_WIDTH + SSD_CONV_DIM + SSD_HEADS + N_BRANCHES * D_MODEL
PEER_HEADS = 8
PEER_NKEYS = 128
PEER_EXPERTS = PEER_NKEYS * PEER_NKEYS
PEER_QDIM = 256
PEER_TOPK = 16
PEER_TOKEN_BLOCK = 128
EPS = 1e-6
NEG_BIG = -1e30

kernel_name = 'sb_hgrn2_ssd_peer_hybrid'

def rmsnorm(x, w):
    xf = x.astype(jnp.float32)
    y = xf * lax.rsqrt(jnp.mean(xf * xf, axis=-1, keepdims=True) + EPS)
    return (y * w.astype(jnp.float32)).astype(x.dtype)

def stick_breaking_attention(q, k, v):
    Bsz, S, H, Dh = q.shape
    nb = S // SB_BLOCK
    scale = Dh ** -0.5
    kf = k.astype(jnp.float32)
    vf = v.astype(jnp.float32)
    qb = q.astype(jnp.float32).reshape(Bsz, nb, SB_BLOCK, H, Dh).transpose(1, 0, 2, 3, 4)
    key_pos = jnp.arange(S)

    def block(args):
        q_blk, blk = args
        q_pos = blk * SB_BLOCK + jnp.arange(SB_BLOCK)
        z = jnp.einsum('bqhd,bkhd->bhqk', q_blk, kf) * scale
        before = key_pos[None, :] < q_pos[:, None]
        log_beta = jax.nn.log_sigmoid(z)
        log_rest = jnp.where(before, jax.nn.log_sigmoid(-z), 0.0)
        tail = lax.cumsum(log_rest, axis=3, reverse=True) - log_rest
        a = jnp.exp(jnp.where(before, log_beta + tail, NEG_BIG))
        return jnp.einsum('bhqk,bkhd->bqhd', a, vf)

    out = lax.map(block, (qb, jnp.arange(nb)))
    return out.transpose(1, 0, 2, 3, 4).reshape(Bsz, S, H * Dh).astype(q.dtype)

def hgrn2_mixer(q_raw, f_raw, i_raw, g_raw, lb, norm_w):
    Bsz, S, _ = q_raw.shape
    nc = S // HG_CHUNK
    f32 = jnp.float32
    lb = lb.astype(f32).reshape(HG_HEADS, HG_DK)
    f_logit = f_raw.astype(f32).reshape(Bsz, S, HG_HEADS, HG_DK)
    f = lb + (1.0 - lb) * jax.nn.sigmoid(f_logit)
    log_f = jnp.log(jnp.maximum(f, HG_F_FLOOR))
    key = (1.0 - lb) * jax.nn.sigmoid(-f_logit)
    q = jax.nn.silu(q_raw.astype(f32)).reshape(Bsz, S, HG_HEADS, HG_DK) * (HG_DK ** -0.5)
    val = i_raw.astype(f32).reshape(Bsz, S, HG_HEADS, HG_DV)

    def chunks(t):
        return t.reshape(Bsz, nc, HG_CHUNK, HG_HEADS, t.shape[-1]).transpose(1, 0, 3, 2, 4)

    causal = jnp.tril(jnp.ones((HG_CHUNK, HG_CHUNK), dtype=bool))

    def step(state, inp):
        qc, kc, vc, gc = inp
        b = jnp.cumsum(gc, axis=2)
        diff = b[:, :, :, None, :] - b[:, :, None, :, :]
        decay = jnp.exp(jnp.where(causal[:, :, None], diff, NEG_BIG))
        scores = jnp.einsum('bhtk,bhtsk,bhsk->bhts', qc, decay, kc)
        o = jnp.einsum('bhts,bhsv->bhtv', scores, vc) + jnp.einsum('bhtk,bhkv->bhtv', qc * jnp.exp(b), state)
        b_last = b[:, :, -1, :]
        new_state = jnp.exp(b_last)[..., None] * state + jnp.einsum('bhsk,bhsv->bhkv', kc * jnp.exp(b_last[:, :, None, :] - b), vc)
        return new_state, o

    state0 = jnp.zeros((Bsz, HG_HEADS, HG_DK, HG_DV), f32)
    _, o = lax.scan(step, state0, (chunks(q), chunks(key), chunks(val), chunks(log_f)))
    o = o.transpose(1, 0, 3, 2, 4).reshape(Bsz, S, HG_HEADS, HG_DV)
    gate = jax.nn.silu(g_raw.astype(f32)).reshape(Bsz, S, HG_HEADS, HG_DV)
    o = rmsnorm(o, norm_w) * gate
    return o.reshape(Bsz, S, HG_WIDTH_V).astype(q_raw.dtype)

def causal_depthwise_conv(x, w, b):
    K, C = w.shape
    y = lax.conv_general_dilated(x, w[:, None, :].astype(x.dtype), window_strides=(1,),
                                 padding=[(K - 1, 0)], dimension_numbers=('NWC', 'WIO', 'NWC'),
                                 feature_group_count=C)
    return y + b.astype(x.dtype)

def segsum(a):
    T = a.shape[-1]
    rep = jnp.broadcast_to(a[..., :, None], a.shape + (T,))
    rep = jnp.where(jnp.tril(jnp.ones((T, T), dtype=bool), -1), rep, 0.0)
    ss = jnp.cumsum(rep, axis=-2)
    return jnp.where(jnp.tril(jnp.ones((T, T), dtype=bool)), ss, NEG_BIG)

def ssd_chunked(x, a, b_h, c_h):
    Bsz, S, H, P = x.shape
    N = b_h.shape[-1]
    L = SSD_CHUNK
    nc = S // L
    x = x.reshape(Bsz, nc, L, H, P)
    b_h = b_h.reshape(Bsz, nc, L, H, N)
    c_h = c_h.reshape(Bsz, nc, L, H, N)
    a = a.reshape(Bsz, nc, L, H).transpose(0, 3, 1, 2)
    a_cum = jnp.cumsum(a, axis=-1)
    seg = jnp.exp(segsum(a))
    scores = jnp.einsum('bclhn,bcshn->bhcls', c_h, b_h) * seg
    y_diag = jnp.einsum('bhcls,bcshp->bclhp', scores, x)
    decay_states = jnp.exp(a_cum[..., -1:] - a_cum)
    states = jnp.einsum('bclhn,bhcl,bclhp->bchpn', b_h, decay_states, x)
    states = jnp.concatenate([jnp.zeros_like(states[:, :1]), states], axis=1)
    chunk_tot = jnp.pad(a_cum[..., -1], ((0, 0), (0, 0), (1, 0)))
    decay_chunk = jnp.exp(segsum(chunk_tot))
    states = jnp.einsum('bhzc,bchpn->bzhpn', decay_chunk, states)[:, :-1]
    y_off = jnp.einsum('bclhn,bchpn,bhcl->bclhp', c_h, states, jnp.exp(a_cum))
    return (y_diag + y_off).reshape(Bsz, S, H, P)

def ssd_mixer(z, xbc, dt_raw, conv_w, conv_b, dt_bias, a_log, d_skip, norm_w):
    Bsz, S, _ = z.shape
    f32 = jnp.float32
    xbc = jax.nn.silu(causal_depthwise_conv(xbc, conv_w, conv_b))
    xs, b_in, c_in = jnp.split(xbc, [SSD_WIDTH, SSD_WIDTH + SSD_GROUPS * SSD_STATE], axis=-1)
    rep = SSD_HEADS // SSD_GROUPS
    xs = xs.astype(f32).reshape(Bsz, S, SSD_HEADS, SSD_HEAD_DIM)
    b_h = jnp.repeat(b_in.astype(f32).reshape(Bsz, S, SSD_GROUPS, SSD_STATE), rep, axis=2)
    c_h = jnp.repeat(c_in.astype(f32).reshape(Bsz, S, SSD_GROUPS, SSD_STATE), rep, axis=2)
    dt = jax.nn.softplus(dt_raw.astype(f32) + dt_bias.astype(f32))
    a = -jnp.exp(a_log.astype(f32)) * dt
    y = ssd_chunked(xs * dt[..., None], a, b_h, c_h)
    y = y + d_skip.astype(f32)[:, None] * xs
    y = y.reshape(Bsz, S, SSD_WIDTH) * jax.nn.silu(z.astype(f32))
    y = rmsnorm(y.reshape(Bsz, S, SSD_GROUPS, SSD_WIDTH // SSD_GROUPS), norm_w.reshape(SSD_GROUPS, -1))
    return y.reshape(Bsz, S, SSD_WIDTH).astype(z.dtype)

def hybrid_mixer(h, lb, w_in, hg_norm_w, conv_w, conv_b, dt_bias, a_log, d_skip, ssd_norm_w,
                 w_branch_sb, w_branch_hg, w_branch_ssd, w_out):
    Bsz, S, _ = h.shape
    proj = h @ w_in
    points = [int(p) for p in np.cumsum(IN_SIZES)[:-1]]
    (sb_q, sb_k, sb_v, hg_f, hg_q, hg_i, hg_g, ssd_z, ssd_xbc, ssd_dt,
     gate_sb, gate_hg, gate_ssd) = jnp.split(proj, points, axis=-1)
    heads = lambda t: t.reshape(Bsz, S, SB_HEADS, SB_HEAD_DIM)
    y_sb = stick_breaking_attention(heads(sb_q), heads(sb_k), heads(sb_v))
    y_hg = hgrn2_mixer(hg_q, hg_f, hg_i, hg_g, lb, hg_norm_w)
    y_ssd = ssd_mixer(ssd_z, ssd_xbc, ssd_dt, conv_w, conv_b, dt_bias, a_log, d_skip, ssd_norm_w)
    merged = (jax.nn.sigmoid(gate_sb) * (y_sb @ w_branch_sb)
              + jax.nn.sigmoid(gate_hg) * (y_hg @ w_branch_hg)
              + jax.nn.sigmoid(gate_ssd) * (y_ssd @ w_branch_ssd))
    return merged @ w_out

def peer_ffn(x, w_q, sub_keys, u, v):
    Bsz, S, D = x.shape
    T = Bsz * S
    xt = x.reshape(T, D)
    q = (xt @ w_q).reshape(T, PEER_HEADS, 2, PEER_QDIM // 2)
    s = jnp.einsum('thpd,hpkd->thpk', q, sub_keys).astype(jnp.float32)
    s1, i1 = lax.top_k(s[:, :, 0], PEER_TOPK)
    s2, i2 = lax.top_k(s[:, :, 1], PEER_TOPK)
    cand_s = (s1[..., :, None] + s2[..., None, :]).reshape(T, PEER_HEADS, PEER_TOPK * PEER_TOPK)
    cand_i = (i1[..., :, None] * PEER_NKEYS + i2[..., None, :]).reshape(T, PEER_HEADS, PEER_TOPK * PEER_TOPK)
    top_s, pos = lax.top_k(cand_s, PEER_TOPK)
    expert_idx = jnp.take_along_axis(cand_i, pos, axis=-1)
    gates = jax.nn.softmax(top_s, axis=-1)
    nb = T // PEER_TOKEN_BLOCK
    HK = PEER_HEADS * PEER_TOPK

    def block(args):
        xb, idx, g = args
        ub = u[idx]
        vb = v[idx]
        act = jax.nn.gelu(jnp.einsum('td,tjd->tj', xb, ub).astype(jnp.float32), approximate=False)
        return jnp.einsum('tj,tjd->td', (g * act).astype(xb.dtype), vb)

    out = lax.map(block, (xt.reshape(nb, PEER_TOKEN_BLOCK, D),
                          expert_idx.reshape(nb, PEER_TOKEN_BLOCK, HK),
                          gates.reshape(nb, PEER_TOKEN_BLOCK, HK)))
    return out.reshape(Bsz, S, D)

def setup_inputs(seed: int = 0) -> dict:
    key = jax.random.key(seed)
    ks = jax.random.split(key, 24)
    f32 = jnp.float32
    nrm = lambda k, shape, scale: jax.random.normal(k, shape, f32) * scale
    dt = jnp.exp(jax.random.uniform(ks[7], (DEPTH, SSD_HEADS), f32, math.log(1e-3), math.log(1e-1)))
    return {
        'x': jax.random.normal(ks[0], (BATCH, SEQ, D_MODEL), f32),
        'norm1_w': 1.0 + nrm(ks[1], (DEPTH, D_MODEL), 0.02),
        'w_in': nrm(ks[2], (DEPTH, D_MODEL, IN_COLS), D_MODEL ** -0.5),
        'hg_lb_logits': nrm(ks[3], (DEPTH, HG_WIDTH_K), 1.0),
        'hg_norm_w': 1.0 + nrm(ks[4], (DEPTH, HG_DV), 0.02),
        'ssd_conv_w': nrm(ks[5], (DEPTH, SSD_CONV, SSD_CONV_DIM), SSD_CONV ** -0.5),
        'ssd_conv_b': nrm(ks[6], (DEPTH, SSD_CONV_DIM), 0.02),
        'ssd_dt_bias': dt + jnp.log(-jnp.expm1(-dt)),
        'ssd_a_log': jnp.log(jax.random.uniform(ks[8], (DEPTH, SSD_HEADS), f32, 1.0, 16.0)),
        'ssd_d': 1.0 + nrm(ks[9], (DEPTH, SSD_HEADS), 0.1),
        'ssd_norm_w': 1.0 + nrm(ks[10], (DEPTH, SSD_WIDTH), 0.02),
        'w_branch_sb': nrm(ks[11], (DEPTH, SB_WIDTH, D_MODEL), SB_WIDTH ** -0.5),
        'w_branch_hg': nrm(ks[12], (DEPTH, HG_WIDTH_V, D_MODEL), HG_WIDTH_V ** -0.5),
        'w_branch_ssd': nrm(ks[13], (DEPTH, SSD_WIDTH, D_MODEL), SSD_WIDTH ** -0.5),
        'w_out': nrm(ks[14], (DEPTH, D_MODEL, D_MODEL), D_MODEL ** -0.5),
        'norm2_w': 1.0 + nrm(ks[15], (DEPTH, D_MODEL), 0.02),
        'peer_w_q': nrm(ks[16], (DEPTH, D_MODEL, PEER_HEADS * PEER_QDIM), D_MODEL ** -0.5),
        'peer_sub_keys': nrm(ks[17], (DEPTH, PEER_HEADS, 2, PEER_NKEYS, PEER_QDIM // 2), (PEER_QDIM // 2) ** -0.5),
        'peer_u': nrm(ks[18], (DEPTH, PEER_EXPERTS, D_MODEL), D_MODEL ** -0.5),
        'peer_v': nrm(ks[19], (DEPTH, PEER_EXPERTS, D_MODEL), PEER_HEADS ** -0.5),
        'final_norm_w': 1.0 + nrm(ks[20], (D_MODEL,), 0.02),
    }

def reference(x, norm1_w, w_in, hg_lb_logits, hg_norm_w, ssd_conv_w, ssd_conv_b, ssd_dt_bias,
              ssd_a_log, ssd_d, ssd_norm_w, w_branch_sb, w_branch_hg, w_branch_ssd, w_out,
              norm2_w, peer_w_q, peer_sub_keys, peer_u, peer_v, final_norm_w):
    gamma = jax.nn.softmax(hg_lb_logits.astype(jnp.float32), axis=0)
    lower_bounds = jnp.cumsum(gamma, axis=0) - gamma[0]
    for l in range(DEPTH):
        h = rmsnorm(x, norm1_w[l])
        x = x + hybrid_mixer(h, lower_bounds[l], w_in[l], hg_norm_w[l], ssd_conv_w[l], ssd_conv_b[l],
                             ssd_dt_bias[l], ssd_a_log[l], ssd_d[l], ssd_norm_w[l],
                             w_branch_sb[l], w_branch_hg[l], w_branch_ssd[l], w_out[l])
        h = rmsnorm(x, norm2_w[l])
        x = x + peer_ffn(h, peer_w_q[l], peer_sub_keys[l], peer_u[l], peer_v[l])
    return rmsnorm(x, final_norm_w)


_drawn_inputs = setup_inputs


def setup_inputs(seed=0):
    import zlib

    import numpy as np

    out = dict(_drawn_inputs(seed))
    spreads = {}
    factors = {'hg_norm_w': 56.522, 'ssd_norm_w': 32.706, 'final_norm_w': 25.736, 'norm2_w': 18.463}
    for name, (base, spread) in spreads.items():
        noise = np.random.default_rng([zlib.crc32(name.encode()), seed]).standard_normal(out[name].shape)
        drawn = base * np.exp(spread * noise) if base else spread * noise
        out[name] = __import__('jax').numpy.asarray(drawn.astype(out[name].dtype))
    for name, factor in factors.items():
        out[name] = (out[name] * factor).astype(out[name].dtype)
    return out
```

```python
from contextlib import ExitStack

import concourse.bass as bass
from concourse import mybir

F32 = mybir.dt.float32
U32 = mybir.dt.uint32
ALU = mybir.AluOpType
ACT = mybir.ActivationFunctionType
AXX = mybir.AxisListType.X

P = 128
T = 1024
D = 1024
KC = D // P
TB = T // P
HALF = 512
EPS = 1e-6

SB_HEADS, SB_DIM = 8, 64
HG_HEADS, HG_DIM = 4, 128
SSD_HEADS, SSD_DIM, SSD_GROUPS, SSD_STATE, SSD_CONV = 8, 64, 2, 64, 4
SSD_HPG = SSD_HEADS // SSD_GROUPS
SSD_GW = SSD_HPG * SSD_DIM
SB_W = SB_HEADS * SB_DIM
HG_W = HG_HEADS * HG_DIM
SSD_W = SSD_HEADS * SSD_DIM
COL_Q = 0
COL_K = COL_Q + SB_W
COL_V = COL_K + SB_W
COL_HF = COL_V + SB_W
COL_HQ = COL_HF + HG_W
COL_HI = COL_HQ + HG_W
COL_HG = COL_HI + HG_W
COL_Z = COL_HG + HG_W
COL_X = COL_Z + SSD_W
COL_B = COL_X + SSD_W
COL_C = COL_B + SSD_GROUPS * SSD_STATE
COL_DT = COL_C + SSD_GROUPS * SSD_STATE
COL_G = COL_DT + SSD_HEADS

PEER_HEADS, KEYS, TOPK = 8, 128, 16
NEG = -1e30
LOG_EXP = "natural_log_exp_and_others"

CONSTS = ("ident", "neg_from", "neg_before", "causal_bias", "upto", "beyond", "ones", "iota")
LEVELS = [64, 32, 16, 8, 4, 2, 1]
C_AT = {name: P * i for i, name in enumerate(CONSTS)}
C_LEVEL = P * len(CONSTS)
C_RESET = C_LEVEL + P * (len(LEVELS) + 1)
C_COLS = C_RESET + T


class Steps:

    def __init__(self, *names):
        self.at = {name: i + 1 for i, name in enumerate(names)}
        self.per = len(names)
        assert len(self.at) == self.per

    def after(self, name, n=0):
        return n * self.per + self.at[name]

    def passes(self, n):
        return n * self.per


def kc_view(w):
    return w.rearrange("(k p) c -> p k c", p=P)


def bc(ap, axis, shape):
    return ap.unsqueeze(axis).broadcast_to(shape)


class Core:

    def __init__(self, nc, ctx):
        self.nc = nc
        self.ctx = ctx
        self.consts = ctx.enter_context(nc.sbuf_tensor("consts", [P, C_COLS], F32))
        self.eps = ctx.enter_context(nc.sbuf_tensor("eps", [P, 1], F32))

    def const(self, name):
        at = C_AT[name]
        return self.consts[:, at:at + P]

    def level_mask(self, n):
        return self.consts[:, C_LEVEL + P * n:C_LEVEL + P * (n + 1)]


def stage_tools(nc, ctx, prefix):

    def sb(name, shape, dt=F32):
        return ctx.enter_context(nc.sbuf_tensor(f"{prefix}_{name}", shape, dt))

    def ps(name, shape):
        return ctx.enter_context(nc.psum_tensor(f"{prefix}_{name}", shape, F32))

    def sem(name):
        return ctx.enter_context(nc.semaphore(f"{prefix}_{name}"))

    return sb, ps, sem


def norm_input(nc, core, x, norm_w, packed_consts, hT):
    with ExitStack() as ctx:
        sb, ps, sem = stage_tools(nc, ctx, "ni")
        xt = sb("x", [P, 2, D])
        squares = sb("squares", [P, D])
        xn = sb("xn", [P, 2, D])
        stat = sb("stat", [P, 3])
        wcol = sb("wcol", [P, KC])
        turned = ps("turned", [P, KC, P])
        consts_in, w_in = sem("consts_in"), sem("w_in")
        x_in = [sem(f"x_in{j}") for j in range(2)]
        scalar_done, vector_done, tensor_done = sem("scalar_done"), sem("vector_done"), sem("tensor_done")
        eps_set = sem("eps_set")
        A = Steps(*[(s, j) for j in range(2) for s in ("squares", "std")])
        V = Steps(*[(s, j) for j in range(2) for s in ("rstd", "xn", "turned0", "turned1")])
        E = Steps(("turned", 0), ("turned", 1))
        block = ctx.enter_context(nc.Block())
        xv = x.rearrange("(b p) d -> p b d", p=P)

        @block.sync
        def _(sp):
            sp.dma_start(core.consts[:, :], packed_consts).then_inc(consts_in, 16)
            sp.dma_start(wcol[:, :], norm_w).then_inc(w_in, 16)
            with sp.Fori(0, TB // 2) as i:
                for j in range(2):
                    sp.wait_ge(vector_done, V.passes(i))
                    sp.dma_start(xt[:, j, :], xv[:, bass.ds(i * 2 + j, 1), :].rearrange("p b d -> p (b d)")).then_inc(x_in[j], 16)

        @block.scalar
        def _(act):
            act.wait_ge(eps_set, 1)
            with act.Fori(0, TB // 2) as i:
                for j in range(2):
                    act.wait_ge(x_in[j], i * 16 + 16)
                    act.wait_ge(vector_done, V.passes(i) if j == 0 else V.after(("xn", 0), i))
                    nc.scalar.activation(squares[:, :], xt[:, j, :], ACT.Square, accum_out=stat[:, 0:1]).then_inc(scalar_done, 1)
                    act.wait_ge(scalar_done, A.after(("squares", j), i))
                    nc.scalar.activation(stat[:, 1:2], stat[:, 0:1], ACT.Sqrt, scale=1.0 / D, bias=core.eps[:, :]).then_inc(scalar_done, 1)

        @block.vector
        def _(dve):
            nc.vector.memset(core.eps[:, :], EPS).then_inc(eps_set, 1)
            dve.wait_ge(w_in, 16)
            with dve.Fori(0, TB // 2) as i:
                for j in range(2):
                    dve.wait_ge(scalar_done, A.after(("std", j), i))
                    nc.vector.reciprocal(stat[:, 2:3], stat[:, 1:2]).then_inc(vector_done, 1)
                    dve.wait_ge(vector_done, V.after(("rstd", j), i))
                    dve.wait_ge(tensor_done, E.passes(i))
                    nc.vector.tensor_scalar(xn[:, j, :], xt[:, j, :], stat[:, 2:3], None, ALU.mult).then_inc(vector_done, 1)
                    dve.wait_ge(tensor_done, E.after(("turned", j), i))
                    for b in range(2):
                        ks = slice(4 * b, 4 * b + 4)
                        nc.vector.tensor_tensor(hT[:, ks, bass.ts(i * 2 + j, P)], turned[:, ks, :],
                                                bc(wcol[:, ks], 2, [P, 4, P]), ALU.mult).then_inc(vector_done, 1)

        @block.tensor
        def _(pe):
            pe.wait_ge(consts_in, 16)
            with pe.Fori(0, TB // 2) as i:
                for j in range(2):
                    pe.wait_ge(vector_done, V.after(("xn", j), i))
                    for k in range(KC):
                        last = nc.tensor.transpose(turned[:, k, :], xn[:, j, k * P:(k + 1) * P], core.const("ident"))
                    last.then_inc(tensor_done, 1)


def stick_breaking(nc, core, w_in, hT, ysbT):
    with ExitStack() as ctx:
        sb, ps, sem = stage_tools(nc, ctx, "sb")
        wq = sb("wq", [P, KC, P])
        wk = sb("wk", [P, KC, P])
        wv = sb("wv", [P, KC, P])
        qT = sb("qT", [P, T])
        kT = sb("kT", [P, T])
        v = sb("v", [P, TB, P])
        NZ = 5
        SOFT, TAIL, REST, EXP, Y = 1, 2, 3, 3, 4
        zs = sb("zs", [P, NZ, HALF])
        mag = sb("mag", [P, NZ, HALF])
        soft = sb("soft", [P, NZ, HALF])
        aT = sb("aT", [P, NZ, HALF])
        pz = [ps(f"pz{i}", [P, HALF]) for i in range(3)]
        pacc = [ps(f"pacc{i}", [P, HALF]) for i in range(2)]
        py = ps("py", [P, HALF])
        pp = [ps(f"pp{i}", [P, HALF]) for i in range(2)]
        w_in_sem = [sem(f"w{n}_in") for n in "qkv"]
        tensor_done, scalar_done, vector_done = sem("tensor_done"), sem("scalar_done"), sem("vector_done")

        tiles = []
        for half in range(2):
            for kb in reversed(range(4 * half + 4)):
                for head in range(2):
                    tiles.append((head, half, kb, max(0, kb - 4 * half) * P))
        N = len(tiles)
        diagonal = [kb >= 4 * half for _, half, kb, _ in tiles]
        ends = {max(i for i, t in enumerate(tiles) if t[1] == half): half for half in range(2)}
        units = [("q", 0), ("q", 1), ("k", 0), ("k", 1)] + [("v", n) for n in range(2)]

        e_names = [("proj", u) for u in units]
        for s in range(N + Y):
            e_names += [("z", s)] * (s < N) + [("rest", s - REST)] * (REST <= s < N + REST)
            e_names += [("tail", s - TAIL)] * (TAIL <= s < N + TAIL) + [("y", s - Y)] * (s >= Y)
        E = Steps(*e_names)
        v_names = []
        for s in range(N + TAIL):
            if s < N:
                v_names += [("zs", s)] + [("zd", s)] * (diagonal[s] and tiles[s][3] + P < HALF)
            v_names += [("soft", s - SOFT)] * (SOFT <= s < N + SOFT) + [("arg", s - TAIL)] * (s >= TAIL)
        V = Steps(*v_names)
        a_names = [("proj", u) for u in units]
        for s in range(N + EXP):
            a_names += [("mag", s), ("exp", s), ("ln", s)] * (s < N) + [("weights", s - EXP)] * (s >= EXP)
            a_names += [("out", ends[s - Y])] if s - Y in ends else []
        a_names += [("out", 1)]
        A = Steps(*a_names)
        block = ctx.enter_context(nc.Block())
        wv_ = kc_view(w_in)

        @block.sync
        def _(sp):
            with sp.Fori(0, SB_HEADS // 2) as c:
                sp.wait_ge(tensor_done, E.passes(c))
                for dst, col, s in ((wq, COL_Q, 0), (wk, COL_K, 1), (wv, COL_V, 2)):
                    sp.dma_start(dst[:, :, :], wv_[:, :, bass.ds(c * P + col, P)]).then_inc(w_in_sem[s], 16)

        @block.tensor
        def _(pe):
            with pe.Fori(0, SB_HEADS // 2) as c:
                for n, (kind, part) in enumerate(units):
                    pe.wait_ge(w_in_sem["qkv".index(kind)], c * 16 + 16)
                    pe.wait_ge(scalar_done, A.passes(c) if n < 2 else A.after(("proj", units[n - 2]), c))
                    if kind in "qk":
                        w = wq if kind == "q" else wk
                        for k in range(KC):
                            last = nc.tensor.matmul(pp[n % 2][:, :], w[:, k, :], hT[:, k, part * HALF:(part + 1) * HALF],
                                                    start=k == 0, stop=k == KC - 1)
                    else:
                        for tb in range(4):
                            for k in range(KC):
                                last = nc.tensor.matmul(pp[n % 2][:, tb * P:(tb + 1) * P],
                                                        hT[:, k, (4 * part + tb) * P:(4 * part + tb + 1) * P],
                                                        wv[:, k, :], start=k == 0, stop=k == KC - 1)
                    last.then_inc(tensor_done, 1)
                pe.wait_ge(scalar_done, A.after(("proj", units[-1]), c))
                for s in range(N + Y):
                    if s < N:
                        head, half, kb, q0 = tiles[s]
                        hp = slice(64 * head, 64 * head + 64)
                        if s >= 3:
                            pe.wait_ge(vector_done, V.after(("zd" if ("zd", s - 3) in V.at else "zs", s - 3), c))
                        nc.tensor.matmul(pz[s % 3][:, q0:HALF], kT[hp, kb * P:(kb + 1) * P],
                                         qT[hp, half * HALF + q0:(half + 1) * HALF],
                                         start=True, stop=True).then_inc(tensor_done, 1)
                    if REST <= s < N + REST:
                        r = s - REST
                        head, half, kb, q0 = tiles[r]
                        pe.wait_ge(vector_done, V.after(("arg", r), c))
                        nc.tensor.matmul(pacc[head][:, q0:HALF], core.const("neg_before"), soft[:, r % NZ, q0:HALF],
                                         start=False, stop=True, skip_group_check=True).then_inc(tensor_done, 1)
                    if TAIL <= s < N + TAIL:
                        r = s - TAIL
                        head, half, kb, q0 = tiles[r]
                        pe.wait_ge(vector_done, V.after(("soft", r), c))
                        nc.tensor.matmul(pacc[head][:, q0:HALF], core.const("neg_from"), soft[:, r % NZ, q0:HALF],
                                         start=kb == 4 * half + 3, stop=False, skip_group_check=True).then_inc(tensor_done, 1)
                    if s >= Y:
                        r = s - Y
                        head, half, kb, q0 = tiles[r]
                        pe.wait_ge(scalar_done, A.after(("weights", r), c))
                        if half == 1 and kb == 7:
                            pe.wait_ge(scalar_done, A.after(("out", 0), c))
                        nc.tensor.matmul(py[64 * head:64 * head + 64, q0:HALF], v[:, kb, 64 * head:64 * head + 64],
                                         aT[:, r % NZ, q0:HALF], start=kb == 4 * half + 3, stop=kb == 0,
                                         skip_group_check=True).then_inc(tensor_done, 1)

        @block.scalar
        def _(act):
            nc.scalar.preload_act_table_set(LOG_EXP)
            with act.Fori(0, SB_HEADS // 2) as c:
                for n, (kind, part) in enumerate(units):
                    act.wait_ge(tensor_done, E.after(("proj", units[n]), c))
                    if kind == "q":
                        nc.scalar.mul(qT[:, part * HALF:(part + 1) * HALF], pp[n % 2][:, :], SB_DIM ** -0.5).then_inc(scalar_done, 1)
                    elif kind == "k":
                        nc.scalar.copy(kT[:, part * HALF:(part + 1) * HALF], pp[n % 2][:, :]).then_inc(scalar_done, 1)
                    else:
                        nc.scalar.copy(v[:, 4 * part:4 * part + 4, :].rearrange("p b d -> p (b d)"), pp[n % 2][:, :]).then_inc(scalar_done, 1)

                def out(half):
                    last = max(i for i, t in enumerate(tiles) if t[1] == half)
                    act.wait_ge(tensor_done, E.after(("y", last), c))
                    nc.scalar.copy(ysbT[:, bass.ds(c, 1), half * HALF:(half + 1) * HALF].rearrange("p c t -> p (c t)"),
                                   py[:, :]).then_inc(scalar_done, 1)

                for s in range(N + EXP):
                    if s < N:
                        q0 = tiles[s][3]
                        act.wait_ge(vector_done, V.after(("zd" if ("zd", s) in V.at else "zs", s), c))
                        nc.scalar.activation(mag[:, s % NZ, q0:HALF], zs[:, s % NZ, q0:HALF], ACT.Abs).then_inc(scalar_done, 1)
                        act.wait_ge(scalar_done, A.after(("mag", s), c))
                        nc.scalar.activation(mag[:, s % NZ, q0:HALF], mag[:, s % NZ, q0:HALF], ACT.Exp, scale=-1.0).then_inc(scalar_done, 1)
                        act.wait_ge(scalar_done, A.after(("exp", s), c))
                        nc.scalar.activation(mag[:, s % NZ, q0:HALF], mag[:, s % NZ, q0:HALF], ACT.Ln, bias=1.0).then_inc(scalar_done, 1)
                    if s >= EXP:
                        r = s - EXP
                        q0 = tiles[r][3]
                        act.wait_ge(vector_done, V.after(("arg", r), c))
                        if r >= NZ:
                            act.wait_ge(tensor_done, E.after(("y", r - NZ), c))
                        nc.scalar.activation(aT[:, r % NZ, q0:HALF], zs[:, r % NZ, q0:HALF], ACT.Exp).then_inc(scalar_done, 1)
                    if s - Y in ends:
                        out(ends[s - Y])
                out(1)

        @block.vector
        def _(dve):
            with dve.Fori(0, SB_HEADS // 2) as c:
                for s in range(N + TAIL):
                    if s < N:
                        q0 = tiles[s][3]
                        dve.wait_ge(tensor_done, E.after(("z", s), c))
                        dve.wait_ge(scalar_done, A.after(("weights", s - NZ), c) if s >= NZ else A.passes(c))
                        if diagonal[s]:
                            nc.vector.tensor_tensor(zs[:, s % NZ, q0:q0 + P], pz[s % 3][:, q0:q0 + P],
                                                    core.const("causal_bias"), ALU.add).then_inc(vector_done, 1)
                            if q0 + P < HALF:
                                nc.vector.tensor_copy(zs[:, s % NZ, q0 + P:HALF], pz[s % 3][:, q0 + P:HALF]).then_inc(vector_done, 1)
                        else:
                            nc.vector.tensor_copy(zs[:, s % NZ, :], pz[s % 3][:, :]).then_inc(vector_done, 1)
                    if SOFT <= s < N + SOFT:
                        r = s - SOFT
                        q0 = tiles[r][3]
                        dve.wait_ge(scalar_done, A.after(("ln", r), c))
                        if r >= NZ:
                            dve.wait_ge(tensor_done, E.after(("rest", r - NZ), c))
                        nc.vector.scalar_tensor_tensor(soft[:, r % NZ, q0:HALF], zs[:, r % NZ, q0:HALF], 0.0,
                                                       mag[:, r % NZ, q0:HALF], ALU.max, ALU.add).then_inc(vector_done, 1)
                    if s >= TAIL:
                        r = s - TAIL
                        q0 = tiles[r][3]
                        dve.wait_ge(tensor_done, E.after(("tail", r), c))
                        nc.vector.tensor_tensor(zs[:, r % NZ, q0:HALF], zs[:, r % NZ, q0:HALF],
                                                pacc[tiles[r][0]][:, q0:HALF], ALU.add).then_inc(vector_done, 1)


def hgrn2(nc, core, w_in, lb_logits, norm_w, hT, yhgT):
    NL = len(LEVELS)
    with ExitStack() as ctx:
        sb, ps, sem = stage_tools(nc, ctx, "hg")
        w = sb("w", [P, 4, KC, P])
        logits = sb("lb_logits", [P, HG_HEADS])
        shifted = sb("shifted", [P, HG_HEADS])
        gamma_of = sb("gamma", [P, 2, HG_HEADS])
        lower = sb("lower", [P, HG_HEADS])
        upper = sb("upper", [P, HG_HEADS])
        lb = sb("lb", [P, 2])
        nw = sb("norm_w", [P, 1])
        ln_c = sb("ln_c", [P, 2])
        e1 = sb("e1", [P, T])
        e2 = sb("e2", [P, T])
        q = sb("q", [P, T])
        key = sb("key", [P, T])
        logf = sb("logf", [P, T])
        b = sb("b", [P, TB, P])
        ebl = sb("chunk_decay", [P, TB])
        x = sb("x", [P, 2, T])
        masked = sb("masked", [P, T])
        scores = sb("scores", [P, TB, P])
        v = sb("v", [P, TB, P])
        gate = sb("gate", [P, TB, P])
        kd = sb("kd", [P, TB, P])
        kdn = sb("kdn", [P, TB, P])
        qd = sb("qd", [P, TB, P])
        state = sb("state", [P, TB, P])
        y = sb("y", [P, TB, P])
        ss = sb("ss", [P, 3 * TB])
        big = [ps(f"big{i}", [P, 2, HALF]) for i in range(4)]
        w_sem = [sem(f"w{n}_in") for n in range(4)]
        small_in = sem("small_in")
        nw_in = sem("norm_w_in")
        tensor_done, scalar_done, vector_done = sem("tensor_done"), sem("scalar_done"), sem("vector_done")

        E = Steps("f", "q", "i", "g", "same", *[("level", n) for n in range(NL)], "kdn", "dstate", "o", "yT")
        L = Steps("shifted", "recip", "gamma", "lower", "upper")
        V = Steps("lb", "one_minus_lb", "e1p", "f", "e2p", "key", "f_lb", "key_lb", "f_hi", "f_lo", "logf", "b",
                  "qp", "qr", "q", "kd_arg", "kd", "qd",
                  "same_masked", *[(s, n) for n in range(NL) for s in ("diff", "left", "right", "masked", "sum")],
                  "gp", "gr", "gate", *[("state", n) for n in range(1, TB)], "ss", "rstd", "y_rstd", "y")
        A = Steps("e1", "e2", "eq", "v", "eg", "ln_hi", "ln_lo", "exp_b", "kd_exp", "chunk_decay",
                  *[(s, n) for n in range(NL) for s in ("decay_left", "decay_right")], "kdn", "square", "std", "yT")
        lnc_done, const_set = sem("ln_c_done"), sem("const_set")
        bound_done, bound_exp_done = sem("bound_done"), sem("bound_exp_done")
        block = ctx.enter_context(nc.Block())
        wv_ = kc_view(w_in)
        CUT, UP = 2.0 ** -40, 2.0 ** 60

        def flat(ap):
            return ap.rearrange("p b d -> p (b d)")

        @block.sync
        def _(sp):
            sp.dma_start(nw[:, :], norm_w).then_inc(nw_in, 16)
            sp.dma_start(logits[:, :], lb_logits).then_inc(small_in, 16)
            with sp.Fori(0, HG_HEADS) as h:
                sp.wait_ge(tensor_done, E.passes(h))
                for n, col in enumerate((COL_HF, COL_HQ, COL_HI, COL_HG)):
                    sp.dma_start(w[:, n, :, :], wv_[:, :, bass.ds(h * P + col, P)]).then_inc(w_sem[n], 16)

        @block.tensor
        def _(pe):
            with pe.Fori(0, HG_HEADS) as h:
                for n, name in enumerate(("f", "q")):
                    pe.wait_ge(w_sem[n], h * 16 + 16)
                    pe.wait_ge(scalar_done, A.passes(h))
                    pe.wait_ge(vector_done, V.passes(h))
                    for half in range(2):
                        for k in range(KC):
                            last = nc.tensor.matmul(big[n][:, half, :], w[:, n, k, :], hT[:, k, half * HALF:(half + 1) * HALF],
                                                    start=k == 0, stop=k == KC - 1)
                    last.then_inc(tensor_done, 1)
                for n, name in enumerate(("i", "g")):
                    pe.wait_ge(w_sem[2 + n], h * 16 + 16)
                    for tb in range(TB):
                        for k in range(KC):
                            last = nc.tensor.matmul(big[2 + n][:, tb // 4, (tb % 4) * P:(tb % 4 + 1) * P], hT[:, k, tb * P:(tb + 1) * P],
                                                    w[:, 2 + n, k, :], start=k == 0, stop=k == KC - 1)
                    last.then_inc(tensor_done, 1)
                pe.wait_ge(vector_done, V.after("q", h))
                for c in range(TB):
                    cs = slice(c * P, (c + 1) * P)
                    last = nc.tensor.matmul(big[0][:, c // 4, (c % 4) * P:(c % 4 + 1) * P], key[:, cs], q[:, cs], start=True, stop=True)
                last.then_inc(tensor_done, 1)
                for n in range(NL):
                    pe.wait_ge(vector_done, V.after(("right", n), h))
                    if n >= 1:
                        pe.wait_ge(vector_done, V.after("same_masked" if n == 1 else ("masked", n - 2), h))
                    for c in range(TB):
                        cs = slice(c * P, (c + 1) * P)
                        last = nc.tensor.matmul(big[(n + 1) % 2][:, c // 4, (c % 4) * P:(c % 4 + 1) * P], x[:, n % 2, cs], x[:, n % 2, cs],
                                                start=True, stop=True)
                    last.then_inc(tensor_done, 1)
                pe.wait_ge(scalar_done, A.after("v", h))
                pe.wait_ge(vector_done, V.after("kd", h))
                for c in range(TB):
                    last = nc.tensor.transpose(big[2][:, c // 4, (c % 4) * P:(c % 4 + 1) * P], kd[:, c, :], core.const("ident"))
                last.then_inc(tensor_done, 1)
                pe.wait_ge(scalar_done, A.after("kdn", h))
                pe.wait_ge(vector_done, V.after("gate", h))
                for c in range(TB):
                    last = nc.tensor.matmul(big[3][:, c // 4, (c % 4) * P:(c % 4 + 1) * P], kdn[:, c, :], v[:, c, :], start=True, stop=True)
                last.then_inc(tensor_done, 1)
                pe.wait_ge(vector_done, V.after(("state", TB - 1), h))
                pe.wait_ge(vector_done, V.after(("sum", NL - 1), h))
                for c in range(TB):
                    o = big[0][:, c // 4, (c % 4) * P:(c % 4 + 1) * P]
                    last = nc.tensor.matmul(o, scores[:, c, :], v[:, c, :], start=True, stop=c == 0)
                    if c:
                        last = nc.tensor.matmul(o, qd[:, c, :], state[:, c, :], start=False, stop=True)
                last.then_inc(tensor_done, 1)
                pe.wait_ge(vector_done, V.after("y", h))
                for c in range(TB):
                    last = nc.tensor.transpose(big[1][:, c // 4, (c % 4) * P:(c % 4 + 1) * P], y[:, c, :], core.const("ident"))
                last.then_inc(tensor_done, 1)

        @block.scalar
        def _(act):
            nc.scalar.preload_act_table_set(LOG_EXP)
            act.wait_ge(const_set, 1)
            nc.scalar.activation(ln_c[:, 1:2], ln_c[:, 0:1], ACT.Ln).then_inc(lnc_done, 1)
            act.wait_ge(bound_done, L.after("shifted"))
            nc.scalar.activation(gamma_of[:, 0, :], shifted[:, :], ACT.Exp).then_inc(bound_exp_done, 1)
            act.wait_ge(nw_in, 16)
            with act.Fori(0, HG_HEADS) as h:
                act.wait_ge(tensor_done, E.after("f", h))
                nc.scalar.activation(e1[:, :], flat(big[0][:, :, :]), ACT.Exp, scale=-1.0).then_inc(scalar_done, 1)
                nc.scalar.activation(e2[:, :], flat(big[0][:, :, :]), ACT.Exp).then_inc(scalar_done, 1)
                act.wait_ge(tensor_done, E.after("q", h))
                nc.scalar.activation(masked[:, :], flat(big[1][:, :, :]), ACT.Exp, scale=-1.0).then_inc(scalar_done, 1)
                act.wait_ge(tensor_done, E.after("i", h))
                nc.scalar.copy(flat(v[:, :, :]), flat(big[2][:, :, :])).then_inc(scalar_done, 1)
                act.wait_ge(tensor_done, E.after("g", h))
                nc.scalar.activation(flat(gate[:, :, :]), flat(big[3][:, :, :]), ACT.Exp, scale=-1.0).then_inc(scalar_done, 1)
                act.wait_ge(vector_done, V.after("f_lo", h))
                nc.scalar.activation(e1[:, :], e1[:, :], ACT.Ln).then_inc(scalar_done, 1)
                nc.scalar.activation(e2[:, :], e2[:, :], ACT.Ln, scale=UP).then_inc(scalar_done, 1)
                act.wait_ge(vector_done, V.after("b", h))
                nc.scalar.activation(flat(qd[:, :, :]), flat(b[:, :, :]), ACT.Exp).then_inc(scalar_done, 1)
                act.wait_ge(vector_done, V.after("kd_arg", h))
                nc.scalar.activation(flat(kd[:, :, :]), flat(kd[:, :, :]), ACT.Exp).then_inc(scalar_done, 1)
                nc.scalar.activation(ebl[:, :], b[:, :, P - 1], ACT.Exp).then_inc(scalar_done, 1)
                for n, m in enumerate(LEVELS):
                    act.wait_ge(vector_done, V.after(("diff", n), h))
                    xv = x[:, n % 2, :].rearrange("p (b s m) -> p b s m", s=2, m=m)
                    nc.scalar.activation(xv[:, :, 0, :], xv[:, :, 0, :], ACT.Exp, scale=-1.0).then_inc(scalar_done, 1)
                    nc.scalar.activation(xv[:, :, 1, :], xv[:, :, 1, :], ACT.Exp).then_inc(scalar_done, 1)
                act.wait_ge(tensor_done, E.after("kdn", h))
                nc.scalar.copy(flat(kdn[:, :, :]), flat(big[2][:, :, :])).then_inc(scalar_done, 1)
                act.wait_ge(tensor_done, E.after("o", h))
                nc.scalar.activation(e1[:, :], flat(big[0][:, :, :]), ACT.Square).then_inc(scalar_done, 1)
                act.wait_ge(vector_done, V.after("ss", h))
                nc.scalar.activation(ss[:, TB:2 * TB], ss[:, 0:TB], ACT.Sqrt, scale=1.0 / HG_DIM, bias=core.eps[:, :]).then_inc(scalar_done, 1)
                act.wait_ge(tensor_done, E.after("yT", h))
                nc.scalar.activation(yhgT[:, bass.ds(h, 1), :].rearrange("p c t -> p (c t)"), flat(big[1][:, :, :]),
                                     ACT.Copy, scale=nw[:, :]).then_inc(scalar_done, 1)

        @block.vector
        def _(dve):
            def chain(name, h):
                dve.wait_ge(vector_done, V.after(name, h))

            nc.vector.memset(ln_c[:, 0:1], CUT * UP).then_inc(const_set, 1)
            dve.wait_ge(small_in, 16)
            nc.vector.tensor_tensor(shifted[:, :], logits[:, :], logits[:, :], ALU.subtract).then_inc(bound_done, 1)
            dve.wait_ge(bound_exp_done, 1)
            nc.vector.reciprocal(gamma_of[:, 1, :], gamma_of[:, 0, :]).then_inc(bound_done, 1)
            dve.wait_ge(bound_done, L.after("recip"))
            nc.vector.tensor_tensor(shifted[:, :], gamma_of[:, 0, :], gamma_of[:, 1, :], ALU.mult).then_inc(bound_done, 1)
            dve.wait_ge(bound_done, L.after("gamma"))
            nc.vector.tensor_tensor(lower[:, :], shifted[:, :], shifted[:, :], ALU.subtract).then_inc(bound_done, 1)
            dve.wait_ge(bound_done, L.after("lower"))
            nc.vector.tensor_scalar(upper[:, :], lower[:, :], -1.0, 1.0, ALU.mult, ALU.add).then_inc(bound_done, 1)
            dve.wait_ge(bound_done, L.after("upper"))
            dve.wait_ge(lnc_done, 1)
            with dve.Fori(0, HG_HEADS) as h:
                nc.vector.tensor_copy(lb[:, 0:1], lower[:, bass.ds(h, 1)]).then_inc(vector_done, 1)
                nc.vector.tensor_copy(lb[:, 1:2], upper[:, bass.ds(h, 1)]).then_inc(vector_done, 1)
                dve.wait_ge(scalar_done, A.after("e1", h))
                nc.vector.tensor_scalar(e1[:, :], e1[:, :], 1.0, None, ALU.add).then_inc(vector_done, 1)
                chain("e1p", h)
                nc.vector.reciprocal(logf[:, :], e1[:, :]).then_inc(vector_done, 1)
                dve.wait_ge(scalar_done, A.after("e2", h))
                nc.vector.tensor_scalar(e2[:, :], e2[:, :], 1.0, None, ALU.add).then_inc(vector_done, 1)
                chain("e2p", h)
                nc.vector.reciprocal(key[:, :], e2[:, :]).then_inc(vector_done, 1)
                chain("one_minus_lb", h)
                nc.vector.tensor_scalar(logf[:, :], logf[:, :], lb[:, 1:2], lb[:, 0:1], ALU.mult, ALU.add).then_inc(vector_done, 1)
                chain("key", h)
                nc.vector.tensor_scalar(key[:, :], key[:, :], lb[:, 1:2], None, ALU.mult).then_inc(vector_done, 1)
                chain("f_lb", h)
                nc.vector.tensor_scalar(e1[:, :], logf[:, :], CUT, None, ALU.max).then_inc(vector_done, 1)
                nc.vector.tensor_scalar(e2[:, :], logf[:, :], 1e-30, CUT, ALU.max, ALU.min).then_inc(vector_done, 1)
                dve.wait_ge(scalar_done, A.after("ln_lo", h))
                nc.vector.scalar_tensor_tensor(logf[:, :], e2[:, :], ln_c[:, 1:2], e1[:, :], ALU.subtract, ALU.add).then_inc(vector_done, 1)
                chain("logf", h)
                nc.vector.tensor_tensor_scan(flat(b[:, :, :]), core.consts[:, C_RESET:C_RESET + T], logf[:, :], 0.0,
                                             ALU.mult, ALU.add).then_inc(vector_done, 1)
                dve.wait_ge(scalar_done, A.after("eq", h))
                nc.vector.tensor_scalar(masked[:, :], masked[:, :], 1.0, None, ALU.add).then_inc(vector_done, 1)
                chain("qp", h)
                nc.vector.reciprocal(q[:, :], masked[:, :]).then_inc(vector_done, 1)
                chain("qr", h)
                nc.vector.scalar_tensor_tensor(q[:, :], flat(big[1][:, :, :]), HG_DIM ** -0.5, q[:, :], ALU.mult, ALU.mult).then_inc(vector_done, 1)
                chain("b", h)
                nc.vector.tensor_tensor(kd[:, :, :], b[:, :, P - 1:P].broadcast_to([P, TB, P]), b[:, :, :], ALU.subtract).then_inc(vector_done, 1)
                dve.wait_ge(scalar_done, A.after("kd_exp", h))
                nc.vector.tensor_tensor(flat(kd[:, :, :]), flat(kd[:, :, :]), key[:, :], ALU.mult).then_inc(vector_done, 1)
                chain("q", h)
                nc.vector.tensor_tensor(flat(qd[:, :, :]), flat(qd[:, :, :]), q[:, :], ALU.mult).then_inc(vector_done, 1)
                dve.wait_ge(tensor_done, E.after("same", h))
                nc.vector.tensor_tensor(scores[:, :, :], big[0][:, :, :].rearrange("p a (b t) -> p (a b) t", t=P),
                                        bc(core.level_mask(NL), 1, [P, TB, P]), ALU.mult).then_inc(vector_done, 1)
                for n, m in enumerate(LEVELS):
                    xv = x[:, n % 2, :].rearrange("p (b s) -> p b s", s=2 * m)
                    bv = flat(b[:, :, :]).rearrange("p (b s) -> p b s", s=2 * m)
                    nc.vector.tensor_tensor(xv, bv, bv[:, :, m - 1:m].broadcast_to([P, T // (2 * m), 2 * m]), ALU.subtract).then_inc(vector_done, 1)
                    xs = x[:, n % 2, :].rearrange("p (b s m) -> p b s m", s=2, m=m)
                    ks = key[:, :].rearrange("p (b s m) -> p b s m", s=2, m=m)
                    qs = q[:, :].rearrange("p (b s m) -> p b s m", s=2, m=m)
                    dve.wait_ge(scalar_done, A.after(("decay_left", n), h))
                    nc.vector.tensor_tensor(xs[:, :, 0, :], xs[:, :, 0, :], ks[:, :, 0, :], ALU.mult).then_inc(vector_done, 1)
                    dve.wait_ge(scalar_done, A.after(("decay_right", n), h))
                    nc.vector.tensor_tensor(xs[:, :, 1, :], xs[:, :, 1, :], qs[:, :, 1, :], ALU.mult).then_inc(vector_done, 1)
                    dve.wait_ge(tensor_done, E.after(("level", n), h))
                    nc.vector.tensor_tensor(masked[:, :].rearrange("p (b t) -> p b t", t=P),
                                            big[(n + 1) % 2][:, :, :].rearrange("p a (b t) -> p (a b) t", t=P),
                                            bc(core.level_mask(n), 1, [P, TB, P]), ALU.mult).then_inc(vector_done, 1)
                    chain(("masked", n), h)
                    nc.vector.tensor_tensor(flat(scores[:, :, :]), flat(scores[:, :, :]), masked[:, :], ALU.add).then_inc(vector_done, 1)
                dve.wait_ge(scalar_done, A.after("eg", h))
                nc.vector.tensor_scalar(logf[:, :], flat(gate[:, :, :]), 1.0, None, ALU.add).then_inc(vector_done, 1)
                chain("gp", h)
                nc.vector.reciprocal(e2[:, :], logf[:, :]).then_inc(vector_done, 1)
                chain("gr", h)
                nc.vector.tensor_tensor(flat(gate[:, :, :]), flat(big[3][:, :, :]), e2[:, :], ALU.mult).then_inc(vector_done, 1)
                dve.wait_ge(tensor_done, E.after("dstate", h))
                dve.wait_ge(scalar_done, A.after("chunk_decay", h))
                for c in range(1, TB):
                    own = big[3][:, (c - 1) // 4, ((c - 1) % 4) * P:((c - 1) % 4 + 1) * P]
                    if c == 1:
                        nc.vector.tensor_copy(state[:, c, :], own).then_inc(vector_done, 1)
                    else:
                        chain(("state", c - 1), h)
                        nc.vector.scalar_tensor_tensor(state[:, c, :], state[:, c - 1, :], ebl[:, c - 1:c], own, ALU.mult, ALU.add).then_inc(vector_done, 1)
                dve.wait_ge(scalar_done, A.after("square", h))
                nc.vector.tensor_reduce(ss[:, 0:TB], e1[:, :].rearrange("p (b d) -> p b d", d=P), AXX, ALU.add).then_inc(vector_done, 1)
                dve.wait_ge(scalar_done, A.after("std", h))
                nc.vector.reciprocal(ss[:, 2 * TB:3 * TB], ss[:, TB:2 * TB]).then_inc(vector_done, 1)
                chain("rstd", h)
                nc.vector.tensor_tensor(y[:, :, :], big[0][:, :, :].rearrange("p a (b t) -> p (a b) t", t=P),
                                        bc(ss[:, 2 * TB:3 * TB], 2, [P, TB, P]), ALU.mult).then_inc(vector_done, 1)
                chain("y_rstd", h)
                nc.vector.tensor_tensor(y[:, :, :], y[:, :, :], gate[:, :, :], ALU.mult).then_inc(vector_done, 1)


def ssd(nc, core, w_in, conv_wb, head_rows, norm_w, hT, yssdT):
    HW, XC = SSD_HPG, SSD_GW // P
    GN = SSD_STATE
    NCV = XC + 2
    PAD = SSD_CONV - 1
    with ExitStack() as ctx:
        sb, ps, sem = stage_tools(nc, ctx, "ssd")
        wx = sb("wx", [P, KC, SSD_GW])
        wz = sb("wz", [P, KC, SSD_GW])
        wbc = sb("wbc", [P, 2, KC, GN])
        wdt = sb("wdt", [P, KC, HW])
        cw = sb("conv_w", [P, NCV, SSD_CONV + 1])
        cw_all = sb("conv_w_all", [P, SSD_GROUPS, NCV, SSD_CONV + 1])
        rows = sb("rows", [P, 3, HW])
        rows_all = sb("rows_all", [P, 3, SSD_HEADS])
        nw = sb("norm_w", [P, SSD_GROUPS * XC])
        raw = sb("raw", [P, NCV, T + PAD])
        conv = sb("conv", [P, NCV, T])
        sig = sb("sig", [P, NCV, T])
        xs = sb("xs", [P, TB, SSD_GW])
        xdt = sig[:, 0:XC, :].rearrange("p u (b h d) -> p (u b) h d", h=HW, d=SSD_DIM)
        xdd = sig[:, XC:NCV, :].rearrange("p u (b h d) -> p (u b) h d", h=HW, d=SSD_DIM)
        bn = sb("bn", [P, TB, GN])
        z = sb("z", [P, TB, SSD_GW])
        y = sb("y", [P, TB, HW, SSD_DIM])
        dt = sb("dt", [P, 3, TB, HW])
        a = sb("a", [P, TB, HW])
        decay = sb("decay", [P, 3, TB, HW])
        rate = sb("rate", [P, HW])
        seg = sb("seg", [P, 2, HW, P])
        cbm = sb("cbm", [P, TB, P])
        sc = sb("sc", [P, 2, HW, P])
        state = sb("state", [GN, TB, SSD_GW])
        ss = sb("ss", [P, 3, TB])
        bank = [ps(f"bank{i}", [P, HALF]) for i in range(8)]
        w_sem = {n: sem(f"w{n}_in") for n in ("x", "bc", "z", "dt")}
        rows_in = sem("rows_in")
        tensor_done, scalar_done, vector_done = sem("tensor_done"), sem("scalar_done"), sem("vector_done")
        pads_set = sem("pads_set")

        SMALL = 16 * (3 * SSD_GROUPS + 2)
        halves = [(u, half) for u in range(NCV) for half in range(2)]
        E = Steps(*[("in", u) for u in halves], "dt", *[("z", i) for i in range(4)], "sums",
                  *[("xs", i) for i in range(4)], "cb0", "cb1", "bn",
                  *[("own", i) for i in range(4)],
                  ("seg", 0), *[s for c in range(1, TB) for s in (("seg", c), ("y", c - 1))], ("y", TB - 1), *[("yT", i) for i in range(XC)])
        V = Steps("taps_x", "taps_bc", "rows", *[s for u in range(NCV) for s in [("tap", u, j) for j in range(SSD_CONV)]],
                  "dt_raw", "dt", "a",
                  *[s for u in range(NCV) for s in (("sp", u), ("sr", u), ("silu", u))],
                  "zp0", "zp1", "zp2", "zp3", "zr", "z0", "z1", "z2", "z3",
                  "cbm0", "cbm1", "xdt", "xdd",
                  *[s for c in range(1, TB) for s in (("state_decay", c), ("state", c))][1:],
                  *[("tri", 0, h) for h in range(HW)],
                  *[s for c in range(TB) for s in [("tri", c + 1, h) for h in range(HW) if c + 1 < TB] + [("sc", c)]
                    + [("y_off", c)] * (c > 0) + [("y", c)]],
                  "skip", "y_skip", "gated", "square", "ss", "rstd", "y_norm")
        A = Steps(*[("in", u) for u in halves], "rate", "dt_abs", "dt_exp", "dt_ln", *[("z", i) for i in range(4)],
                  "decay", *[("conv_exp", u) for u in range(NCV)],
                  *[("xs", i) for i in range(4)], "bn",
                  *[("seg", c) for c in range(TB)], "std", *[("yT", i) for i in range(XC)])
        block = ctx.enter_context(nc.Block())
        wv_ = kc_view(w_in)

        @block.sync
        def _(sp):
            for g in range(SSD_GROUPS):
                sp.dma_start(cw_all[:, g, 0:XC, :], conv_wb[g * SSD_GW:(g + 1) * SSD_GW, :].rearrange("(u p) j -> p u j", p=P)).then_inc(rows_in, 16)
                for n in range(2):
                    row = SSD_W + (n * SSD_GROUPS + g) * GN
                    sp.dma_start(cw_all[0:GN, g, XC + n, :], conv_wb[row:row + GN, :]).then_inc(rows_in, 16)
            sp.dma_start(rows_all[:, :, :], head_rows.broadcast_to([P, 3, SSD_HEADS])).then_inc(rows_in, 16)
            sp.dma_start(nw[:, :], norm_w).then_inc(rows_in, 16)
            with sp.Fori(0, SSD_GROUPS) as g:
                sp.wait_ge(tensor_done, E.passes(g))
                sp.dma_start(wx[:, :, :], wv_[:, :, bass.ds(g * SSD_GW + COL_X, SSD_GW)]).then_inc(w_sem["x"], 16)
                for n, col in enumerate((COL_B, COL_C)):
                    sp.dma_start(wbc[:, n, :, :], wv_[:, :, bass.ds(g * GN + col, GN)]).then_inc(w_sem["bc"], 16)
                sp.dma_start(wz[:, :, :], wv_[:, :, bass.ds(g * SSD_GW + COL_Z, SSD_GW)]).then_inc(w_sem["z"], 16)
                sp.dma_start(wdt[:, :, :], wv_[:, :, bass.ds(g * HW + COL_DT, HW)]).then_inc(w_sem["dt"], 16)

        @block.tensor
        def _(pe):
            with pe.Fori(0, SSD_GROUPS) as g:
                pe.wait_ge(scalar_done, A.passes(g))
                pe.wait_ge(vector_done, V.passes(g))
                for n, (u, half) in enumerate(halves):
                    m = P if u < XC else GN
                    if half == 0:
                        pe.wait_ge(w_sem["x" if u < XC else "bc"], g * 16 + 16 if u < XC else g * 32 + 32)
                    for k in range(KC):
                        w = wx[:, k, u * P:(u + 1) * P] if u < XC else wbc[:, u - XC, k, :]
                        last = nc.tensor.matmul(bank[n][0:m, :], w, hT[:, k, half * HALF:(half + 1) * HALF], start=k == 0, stop=k == KC - 1)
                    last.then_inc(tensor_done, 1)
                pe.wait_ge(w_sem["dt"], g * 16 + 16)
                pe.wait_ge(scalar_done, A.after(("in", halves[0]), g))
                for tb in range(TB):
                    for k in range(KC):
                        last = nc.tensor.matmul(bank[0][:, tb * HW:(tb + 1) * HW], hT[:, k, tb * P:(tb + 1) * P], wdt[:, k, :],
                                                start=k == 0, stop=k == KC - 1)
                last.then_inc(tensor_done, 1)
                pe.wait_ge(w_sem["z"], g * 16 + 16)
                for i in range(4):
                    pe.wait_ge(scalar_done, A.after(("in", halves[1 + i]), g))
                    for tb in (2 * i, 2 * i + 1):
                        for k in range(KC):
                            last = nc.tensor.matmul(bank[1 + i][:, (tb % 2) * SSD_GW:(tb % 2 + 1) * SSD_GW], hT[:, k, tb * P:(tb + 1) * P],
                                                    wz[:, k, :], start=k == 0, stop=k == KC - 1)
                    last.then_inc(tensor_done, 1)
                pe.wait_ge(vector_done, V.after("a", g))
                pe.wait_ge(scalar_done, A.after(("in", halves[7]), g))
                for n, tri in enumerate(("upto", "beyond", "ones")):
                    last = nc.tensor.matmul(bank[5][:, n * TB * HW:(n + 1) * TB * HW], core.const(tri),
                                            a[:, :, :].rearrange("p b h -> p (b h)"), start=True, stop=True)
                last.then_inc(tensor_done, 1)
                for i in range(4):
                    if i == 0:
                        pe.wait_ge(vector_done, V.after(("silu", XC - 1), g))
                    if i >= 2:
                        pe.wait_ge(scalar_done, A.after(("xs", i - 2), g))
                    for tb in (2 * i, 2 * i + 1):
                        for u in range(XC):
                            at = (tb % 2) * SSD_GW + u * P
                            last = nc.tensor.transpose(bank[6 + i % 2][:, at:at + P], conv[:, u, tb * P:(tb + 1) * P], core.const("ident"))
                    last.then_inc(tensor_done, 1)
                pe.wait_ge(vector_done, V.after(("silu", XC + 1), g))
                pe.wait_ge(vector_done, V.after("dt", g))
                for i in range(2):
                    pe.wait_ge(scalar_done, A.after(("xs", 2 + i), g))
                    for c in range(4 * i, 4 * i + 4):
                        last = nc.tensor.matmul(bank[6 + i][:, (c % 4) * P:(c % 4 + 1) * P], conv[0:GN, XC, c * P:(c + 1) * P],
                                                conv[0:GN, XC + 1, c * P:(c + 1) * P], start=True, stop=True)
                    last.then_inc(tensor_done, 1)
                for tb in range(TB):
                    last = nc.tensor.transpose(bank[0][:, tb * GN:(tb + 1) * GN], conv[0:GN, XC, tb * P:(tb + 1) * P], core.const("ident")[0:GN, 0:GN])
                last.then_inc(tensor_done, 1)
                pe.wait_ge(vector_done, V.after("xdd", g))
                pe.wait_ge(scalar_done, A.after("bn", g))
                for i in range(4):
                    for c in (2 * i, 2 * i + 1):
                        last = nc.tensor.matmul(bank[1 + i][0:GN, (c % 2) * SSD_GW:(c % 2 + 1) * SSD_GW], bn[:, c, :],
                                                xdd[:, c, :, :].rearrange("p h d -> p (h d)"), start=True, stop=True)
                    last.then_inc(tensor_done, 1)
                for c in range(TB + 1):
                    if c < TB:
                        if c >= 2:
                            pe.wait_ge(scalar_done, A.after(("seg", c - 2), g))
                        if c == 0:
                            pe.wait_ge(scalar_done, A.after("decay", g))
                        pe.wait_ge(vector_done, V.after(("tri", c, HW - 1), g))
                        for h in range(HW):
                            last = nc.tensor.matmul(bank[(0, 5)[c % 2]][:, h * P:(h + 1) * P], seg[:, c % 2, h, :], core.const("upto"), start=True, stop=True)
                        last.then_inc(tensor_done, 1)
                    if c >= 1:
                        r = c - 1
                        pe.wait_ge(vector_done, V.after(("sc", r), g))
                        if r >= 2:
                            pe.wait_ge(vector_done, V.after(("y", r - 2), g))
                        yb = bank[6 + r % 2]
                        for h in range(HW):
                            last = nc.tensor.matmul(yb[:, h * SSD_DIM:(h + 1) * SSD_DIM], sc[:, r % 2, h, :], xdt[:, r, h, :], start=True, stop=True)
                        if r >= 1:
                            last = nc.tensor.matmul(yb[:, SSD_GW:2 * SSD_GW], conv[0:GN, XC + 1, r * P:(r + 1) * P], state[:, r, :], start=True, stop=True)
                        last.then_inc(tensor_done, 1)
                pe.wait_ge(vector_done, V.after("y_norm", g))
                for u in range(XC):
                    for tb in range(TB):
                        last = nc.tensor.transpose(bank[1 + 2 * u + tb // 4][:, (tb % 4) * P:(tb % 4 + 1) * P],
                                                   y[:, tb, 2 * u:2 * u + 2, :].rearrange("p h d -> p (h d)"), core.const("ident"))
                    last.then_inc(tensor_done, 1)

        @block.scalar
        def _(act):
            nc.scalar.preload_act_table_set(LOG_EXP)
            act.wait_ge(pads_set, 1)
            act.wait_ge(rows_in, SMALL)
            with act.Fori(0, SSD_GROUPS) as g:
                for n, (u, half) in enumerate(halves):
                    m = P if u < XC else GN
                    act.wait_ge(tensor_done, E.after(("in", (u, half)), g))
                    nc.scalar.copy(raw[0:m, u, PAD + half * HALF:PAD + (half + 1) * HALF], bank[n][0:m, :]).then_inc(scalar_done, 1)
                act.wait_ge(vector_done, V.after("rows", g))
                nc.scalar.activation(rate[:, :], rows[:, 1, :], ACT.Exp).then_inc(scalar_done, 1)
                act.wait_ge(vector_done, V.after("dt_raw", g))
                nc.scalar.activation(dt[:, 1, :, :], dt[:, 0, :, :], ACT.Abs).then_inc(scalar_done, 1)
                act.wait_ge(scalar_done, A.after("dt_abs", g))
                nc.scalar.activation(dt[:, 1, :, :], dt[:, 1, :, :], ACT.Exp, scale=-1.0).then_inc(scalar_done, 1)
                act.wait_ge(scalar_done, A.after("dt_exp", g))
                nc.scalar.activation(dt[:, 1, :, :], dt[:, 1, :, :], ACT.Ln, bias=1.0).then_inc(scalar_done, 1)
                for i in range(4):
                    act.wait_ge(tensor_done, E.after(("z", i), g))
                    nc.scalar.activation(z[:, 2 * i:2 * i + 2, :].rearrange("p b d -> p (b d)"), bank[1 + i][:, :], ACT.Exp, scale=-1.0).then_inc(scalar_done, 1)
                act.wait_ge(tensor_done, E.after("sums", g))
                nc.scalar.activation(decay[:, :, :, :].rearrange("p s b h -> p (s b h)"), bank[5][:, 0:3 * TB * HW], ACT.Exp).then_inc(scalar_done, 1)
                for u in range(NCV):
                    m = P if u < XC else GN
                    act.wait_ge(vector_done, V.after(("tap", u, SSD_CONV - 1), g))
                    nc.scalar.activation(sig[0:m, u, :], conv[0:m, u, :], ACT.Exp, scale=-1.0).then_inc(scalar_done, 1)
                for i in range(4):
                    act.wait_ge(tensor_done, E.after(("xs", i), g))
                    nc.scalar.copy(xs[:, 2 * i:2 * i + 2, :].rearrange("p b d -> p (b d)"), bank[6 + i % 2][:, :]).then_inc(scalar_done, 1)
                act.wait_ge(tensor_done, E.after("bn", g))
                nc.scalar.copy(bn[:, :, :].rearrange("p b n -> p (b n)"), bank[0][:, :]).then_inc(scalar_done, 1)
                for c in range(TB):
                    act.wait_ge(tensor_done, E.after(("seg", c), g))
                    if c >= 2:
                        act.wait_ge(tensor_done, E.after(("y", c - 2), g))
                    nc.scalar.activation(sc[:, c % 2, :, :].rearrange("p h t -> p (h t)"), bank[(0, 5)[c % 2]][:, :], ACT.Exp).then_inc(scalar_done, 1)
                act.wait_ge(vector_done, V.after("ss", g))
                nc.scalar.activation(ss[:, 1, :], ss[:, 0, :], ACT.Sqrt, scale=1.0 / SSD_GW, bias=core.eps[:, :]).then_inc(scalar_done, 1)
                for u in range(XC):
                    act.wait_ge(tensor_done, E.after(("yT", u), g))
                    for half in range(2):
                        last = nc.scalar.activation(yssdT[:, bass.ds(g * XC + u, 1), half * HALF:(half + 1) * HALF].rearrange("p c t -> p (c t)"),
                                                    bank[1 + 2 * u + half][:, :], ACT.Copy, scale=nw[:, bass.ds(g * XC + u, 1)])
                    last.then_inc(scalar_done, 1)

        @block.vector
        def _(dve):
            nc.vector.memset(raw[:, :, 0:PAD], 0.0).then_inc(pads_set, 1)
            dve.wait_ge(rows_in, SMALL)
            with dve.Fori(0, SSD_GROUPS) as g:
                def chain(name):
                    dve.wait_ge(vector_done, V.after(name, g))

                nc.vector.tensor_copy(cw[:, 0:XC, :], cw_all[:, bass.ds(g, 1), 0:XC, :].rearrange("p g u j -> p (g u) j")).then_inc(vector_done, 1)
                nc.vector.tensor_copy(cw[0:GN, XC:NCV, :], cw_all[0:GN, bass.ds(g, 1), XC:NCV, :].rearrange("p g u j -> p (g u) j")).then_inc(vector_done, 1)
                nc.vector.tensor_copy(rows[:, :, :], rows_all[:, :, bass.ds(g * HW, HW)]).then_inc(vector_done, 1)
                chain("rows")
                for u in range(NCV):
                    m = P if u < XC else GN
                    dve.wait_ge(scalar_done, A.after(("in", (u, 1)), g))
                    for j in range(SSD_CONV):
                        if j == 0:
                            nc.vector.tensor_scalar(conv[0:m, u, :], raw[0:m, u, 0:T], cw[0:m, u, 0:1], cw[0:m, u, SSD_CONV:SSD_CONV + 1],
                                                    ALU.mult, ALU.add).then_inc(vector_done, 1)
                        else:
                            chain(("tap", u, j - 1))
                            nc.vector.scalar_tensor_tensor(conv[0:m, u, :], raw[0:m, u, j:j + T], cw[0:m, u, j:j + 1], conv[0:m, u, :],
                                                           ALU.mult, ALU.add).then_inc(vector_done, 1)
                dve.wait_ge(tensor_done, E.after("dt", g))
                nc.vector.tensor_tensor(dt[:, 0, :, :], bank[0][:, 0:TB * HW].rearrange("p (b h) -> p b h", h=HW),
                                        bc(rows[:, 0, :], 1, [P, TB, HW]), ALU.add).then_inc(vector_done, 1)
                dve.wait_ge(scalar_done, A.after("dt_ln", g))
                nc.vector.scalar_tensor_tensor(dt[:, 2, :, :], dt[:, 0, :, :], 0.0, dt[:, 1, :, :], ALU.max, ALU.add).then_inc(vector_done, 1)
                chain("dt")
                nc.vector.scalar_tensor_tensor(a[:, :, :], dt[:, 2, :, :], -1.0, bc(rate[:, :], 1, [P, TB, HW]), ALU.mult, ALU.mult).then_inc(vector_done, 1)
                for u in range(NCV):
                    m = P if u < XC else GN
                    dve.wait_ge(scalar_done, A.after(("conv_exp", u), g))
                    nc.vector.tensor_scalar(sig[0:m, u, :], sig[0:m, u, :], 1.0, None, ALU.add).then_inc(vector_done, 1)
                    chain(("sp", u))
                    nc.vector.reciprocal(sig[0:m, u, :], sig[0:m, u, :]).then_inc(vector_done, 1)
                    chain(("sr", u))
                    nc.vector.tensor_tensor(conv[0:m, u, :], conv[0:m, u, :], sig[0:m, u, :], ALU.mult).then_inc(vector_done, 1)
                zf = z[:, :, :].rearrange("p (i b) d -> p i (b d)", b=2)
                for i in range(4):
                    dve.wait_ge(scalar_done, A.after(("z", i), g))
                    nc.vector.tensor_scalar(zf[:, i, :], zf[:, i, :], 1.0, None, ALU.add).then_inc(vector_done, 1)
                chain("zp3")
                nc.vector.reciprocal(z[:, :, :], z[:, :, :]).then_inc(vector_done, 1)
                chain("zr")
                for i in range(4):
                    nc.vector.tensor_tensor(zf[:, i, :], zf[:, i, :], bank[1 + i][:, :], ALU.mult).then_inc(vector_done, 1)
                for i in range(2):
                    dve.wait_ge(tensor_done, E.after(f"cb{i}", g))
                    nc.vector.tensor_tensor(cbm[:, 4 * i:4 * i + 4, :], bank[6 + i][:, :].rearrange("p (c t) -> p c t", t=P),
                                            bc(core.const("upto"), 1, [P, 4, P]), ALU.mult).then_inc(vector_done, 1)
                dve.wait_ge(scalar_done, A.after(("xs", 3), g))
                nc.vector.tensor_tensor(xdt[:, :, :, :].rearrange("p b h d -> p (b h) d"), xs[:, :, :].rearrange("p b (h d) -> p (b h) d", d=SSD_DIM),
                                        bc(dt[:, 2, :, :].rearrange("p b h -> p (b h)"), 2, [P, TB * HW, SSD_DIM]), ALU.mult).then_inc(vector_done, 1)
                chain("xdt")
                nc.vector.tensor_tensor(xdd[:, :, :, :].rearrange("p b h d -> p (b h) d"), xdt[:, :, :, :].rearrange("p b h d -> p (b h) d"),
                                        bc(decay[:, 1, :, :].rearrange("p b h -> p (b h)"), 2, [P, TB * HW, SSD_DIM]), ALU.mult).then_inc(vector_done, 1)
                for c in range(1, TB):
                    own = bank[1 + (c - 1) // 2][0:GN, ((c - 1) % 2) * SSD_GW:((c - 1) % 2 + 1) * SSD_GW]
                    dve.wait_ge(tensor_done, E.after(("own", (c - 1) // 2), g))
                    if c == 1:
                        nc.vector.tensor_copy(state[:, c, :], own).then_inc(vector_done, 1)
                    else:
                        chain(("state", c - 1))
                        nc.vector.tensor_tensor(state[:, c, :].rearrange("p (h d) -> p h d", d=SSD_DIM),
                                                state[:, c - 1, :].rearrange("p (h d) -> p h d", d=SSD_DIM),
                                                bc(decay[0:GN, 2, c - 1, :], 2, [GN, HW, SSD_DIM]), ALU.mult).then_inc(vector_done, 1)
                        chain(("state_decay", c))
                        nc.vector.tensor_tensor(state[:, c, :], state[:, c, :], own, ALU.add).then_inc(vector_done, 1)
                def below_diagonal(c):
                    if c >= 2:
                        dve.wait_ge(tensor_done, E.after(("seg", c - 2), g))
                    for h in range(HW):
                        nc.vector.tensor_scalar(seg[:, c % 2, h, :], core.const("beyond"), a[:, c, h:h + 1], None, ALU.mult).then_inc(vector_done, 1)

                below_diagonal(0)
                for c in range(TB):
                    if c + 1 < TB:
                        below_diagonal(c + 1)
                    dve.wait_ge(scalar_done, A.after(("seg", c), g))
                    nc.vector.tensor_tensor(sc[:, c % 2, :, :], sc[:, c % 2, :, :], bc(cbm[:, c, :], 1, [P, HW, P]), ALU.mult).then_inc(vector_done, 1)
                    dve.wait_ge(tensor_done, E.after(("y", c), g))
                    yb = bank[6 + c % 2]
                    if c:
                        nc.vector.tensor_tensor(y[:, c, :, :], yb[:, SSD_GW:2 * SSD_GW].rearrange("p (h d) -> p h d", d=SSD_DIM),
                                                bc(decay[:, 0, c, :], 2, [P, HW, SSD_DIM]), ALU.mult).then_inc(vector_done, 1)
                        chain(("y_off", c))
                        nc.vector.tensor_tensor(y[:, c, :, :], y[:, c, :, :], yb[:, 0:SSD_GW].rearrange("p (h d) -> p h d", d=SSD_DIM), ALU.add).then_inc(vector_done, 1)
                    else:
                        nc.vector.tensor_copy(y[:, c, :, :], yb[:, 0:SSD_GW].rearrange("p (h d) -> p h d", d=SSD_DIM)).then_inc(vector_done, 1)
                nc.vector.tensor_tensor(xdd[:, :, :, :], xs[:, :, :].rearrange("p b (h d) -> p b h d", d=SSD_DIM),
                                        rows[:, 2, :].unsqueeze(1).unsqueeze(3).broadcast_to([P, TB, HW, SSD_DIM]), ALU.mult).then_inc(vector_done, 1)
                chain("skip")
                nc.vector.tensor_tensor(y[:, :, :, :], y[:, :, :, :], xdd[:, :, :, :], ALU.add).then_inc(vector_done, 1)
                yf = y[:, :, :, :].rearrange("p b h d -> p b (h d)")
                chain("y_skip")
                nc.vector.tensor_tensor(yf, yf, z[:, :, :], ALU.mult).then_inc(vector_done, 1)
                chain("gated")
                nc.vector.tensor_tensor(xdd[:, :, :, :].rearrange("p b h d -> p b (h d)"), yf, yf, ALU.mult).then_inc(vector_done, 1)
                chain("square")
                nc.vector.tensor_reduce(ss[:, 0, :], xdd[:, :, :, :].rearrange("p b h d -> p b (h d)"), AXX, ALU.add).then_inc(vector_done, 1)
                dve.wait_ge(scalar_done, A.after("std", g))
                nc.vector.reciprocal(ss[:, 2, :], ss[:, 1, :]).then_inc(vector_done, 1)
                chain("rstd")
                nc.vector.tensor_tensor(yf, yf, bc(ss[:, 2, :], 2, [P, TB, SSD_GW]), ALU.mult).then_inc(vector_done, 1)


def merge(nc, core, w_in, branch_w, hT, yT, mergedT):
    NB, YC = 3, 4
    with ExitStack() as ctx:
        sb, ps, sem = stage_tools(nc, ctx, "mg")
        wg = sb("wg", [P, 2, NB, KC, P])
        wb = sb("wb", [P, 2, NB, YC, P])
        RING = 4
        sig = sb("sig", [P, RING, HALF])
        part = sb("part", [P, 2, HALF])
        pg = [ps(f"pg{i}", [P, HALF]) for i in range(RING)]
        pb = [ps(f"pb{i}", [P, HALF]) for i in range(RING)]
        w_sem = [sem(f"w{j}_in") for j in range(2)]
        tensor_done, scalar_done, vector_done = sem("tensor_done"), sem("scalar_done"), sem("vector_done")
        units = [(j, half, n) for j in range(2) for half in range(2) for n in range(NB)]
        E = Steps(*[(s, u) for u in units for s in ("gate", "branch")])
        A = Steps(*units)
        V = Steps(*[(s, u) for u in units for s in ("plus", "recip", "product") + ("sum",) * (u[2] > 0)])
        LOADS = 16 * 2 * NB
        block = ctx.enter_context(nc.Block())
        wv_ = kc_view(w_in)
        wbv = branch_w.rearrange("n (k p) c -> n p k c", p=P)

        @block.sync
        def _(sp):
            with sp.Fori(0, KC // 2) as i:
                for j in range(2):
                    sp.wait_ge(tensor_done, E.passes(i))
                    for n in range(NB):
                        sp.dma_start(wg[:, j, n, :, :], wv_[:, :, bass.ds(i * 2 * P + (COL_G + n * D + j * P), P)]).then_inc(w_sem[j], 16)
                        sp.dma_start(wb[:, j, n, :, :], wbv[n, :, :, bass.ds(i * 2 * P + j * P, P)]).then_inc(w_sem[j], 16)

        @block.tensor
        def _(pe):
            with pe.Fori(0, KC // 2) as i:
                for x, (j, half, n) in enumerate(units):
                    ts = slice(half * HALF, (half + 1) * HALF)
                    r = x % RING
                    if half == 0 and n == 0:
                        pe.wait_ge(w_sem[j], i * LOADS + LOADS)
                    pe.wait_ge(vector_done, V.after(("product", units[x - RING]), i) if x >= RING else V.passes(i))
                    for k in range(KC):
                        last = nc.tensor.matmul(pg[r][:, :], wg[:, j, n, k, :], hT[:, k, ts], start=k == 0, stop=k == KC - 1)
                    last.then_inc(tensor_done, 1)
                    for k in range(YC):
                        last = nc.tensor.matmul(pb[r][:, :], wb[:, j, n, k, :], yT[n][:, k, ts], start=k == 0, stop=k == YC - 1)
                    last.then_inc(tensor_done, 1)

        @block.scalar
        def _(act):
            with act.Fori(0, KC // 2) as i:
                for x, u in enumerate(units):
                    act.wait_ge(tensor_done, E.after(("gate", u), i))
                    act.wait_ge(vector_done, V.after(("product", units[x - RING]), i) if x >= RING else V.passes(i))
                    nc.scalar.activation(sig[:, x % RING, :], pg[x % RING][:, :], ACT.Exp, scale=-1.0).then_inc(scalar_done, 1)

        @block.vector
        def _(dve):
            with dve.Fori(0, KC // 2) as i:
                for x, u in enumerate(units):
                    j, half, n = u
                    r = x % RING
                    dve.wait_ge(scalar_done, A.after(u, i))
                    nc.vector.tensor_scalar(sig[:, r, :], sig[:, r, :], 1.0, None, ALU.add).then_inc(vector_done, 1)
                    dve.wait_ge(vector_done, V.after(("plus", u), i))
                    nc.vector.reciprocal(sig[:, r, :], sig[:, r, :]).then_inc(vector_done, 1)
                    dve.wait_ge(vector_done, V.after(("recip", u), i))
                    dve.wait_ge(tensor_done, E.after(("branch", u), i))
                    out = mergedT[:, bass.ds(i * 2 + j, 1), half * HALF:(half + 1) * HALF].rearrange("p c t -> p (c t)")
                    nc.vector.tensor_tensor(part[:, n % 2, :] if n else out, sig[:, r, :], pb[r][:, :], ALU.mult).then_inc(vector_done, 1)
                    if n:
                        dve.wait_ge(vector_done, V.after(("product", u), i))
                        nc.vector.tensor_tensor(out, out, part[:, n % 2, :], ALU.add).then_inc(vector_done, 1)


def output_and_norm(nc, core, x, w_out, norm_w, mergedT, acc, h2T):
    with ExitStack() as ctx:
        sb, ps, sem = stage_tools(nc, ctx, "ou")
        wo = sb("w", [P, KC, D])
        xt = sb("x", [P, 2, D])
        squares = sb("squares", [P, D])
        xn = sb("xn", [P, 2, D])
        stat = sb("stat", [P, 2, 3])
        wcol = sb("wcol", [P, KC])
        po = [ps(f"po{i}", [P, 2, HALF]) for i in range(2)]
        turned = [ps(f"turned{i}", [P, KC, P]) for i in range(2)]
        w_sem = [sem(f"w{i}_in") for i in range(2)]
        x_in = [sem(f"x{i}_in") for i in range(2)]
        norm_in = sem("norm_in")
        tensor_done, scalar_done, vector_done = sem("tensor_done"), sem("scalar_done"), sem("vector_done")
        E = Steps(*[s for b in range(TB + 1) for s in [("out", b)] * (b < TB) + [("turned", b - 1)] * (b > 0)])
        A = Steps(*[(s, b) for b in range(TB) for s in ("squares", "std")])
        V = Steps(*[(s, b) for b in range(TB) for s in ("sum", "rstd", "xn", "h0", "h1")])
        block = ctx.enter_context(nc.Block())
        xv = x.rearrange("(b p) d -> p b d", p=P)
        wov = kc_view(w_out)

        @block.sync
        def _(sp):
            sp.dma_start(wcol[:, :], norm_w).then_inc(norm_in, 16)
            for half in range(2):
                sp.dma_start(wo[:, :, half * HALF:(half + 1) * HALF], wov[:, :, half * HALF:(half + 1) * HALF]).then_inc(w_sem[half], 16)
            for b in range(TB):
                if b >= 2:
                    sp.wait_ge(vector_done, V.after(("sum", b - 2)))
                sp.dma_start(xt[:, b % 2, :], xv[:, b, :]).then_inc(x_in[b % 2], 16)

        @block.tensor
        def _(pe):
            for b in range(TB + 1):
                if b < TB:
                    if b >= 2:
                        pe.wait_ge(vector_done, V.after(("sum", b - 2)))
                    for half in range(2):
                        if b == 0:
                            pe.wait_ge(w_sem[half], 16)
                        for k in range(KC):
                            last = nc.tensor.matmul(po[b % 2][:, half, :], mergedT[:, k, b * P:(b + 1) * P], wo[:, k, half * HALF:(half + 1) * HALF],
                                                    start=k == 0, stop=k == KC - 1)
                    last.then_inc(tensor_done, 1)
                if b > 0:
                    r = b - 1
                    pe.wait_ge(vector_done, V.after(("xn", r)))
                    if r >= 2:
                        pe.wait_ge(vector_done, V.after(("h1", r - 2)))
                    for k in range(KC):
                        last = nc.tensor.transpose(turned[r % 2][:, k, :], xn[:, r % 2, k * P:(k + 1) * P], core.const("ident"))
                    last.then_inc(tensor_done, 1)

        @block.scalar
        def _(act):
            for b in range(TB):
                act.wait_ge(vector_done, V.after(("sum", b)))
                nc.scalar.activation(squares[:, :], acc[:, b, :], ACT.Square, accum_out=stat[:, b % 2, 0:1]).then_inc(scalar_done, 1)
                act.wait_ge(scalar_done, A.after(("squares", b)))
                nc.scalar.activation(stat[:, b % 2, 1:2], stat[:, b % 2, 0:1], ACT.Sqrt, scale=1.0 / D, bias=core.eps[:, :]).then_inc(scalar_done, 1)

        @block.vector
        def _(dve):
            dve.wait_ge(norm_in, 16)
            for b in range(TB):
                dve.wait_ge(x_in[b % 2], 16 * (b // 2 + 1))
                dve.wait_ge(tensor_done, E.after(("out", b)))
                nc.vector.tensor_tensor(acc[:, b, :], xt[:, b % 2, :], po[b % 2][:, :, :].rearrange("p a d -> p (a d)"), ALU.add).then_inc(vector_done, 1)
                dve.wait_ge(scalar_done, A.after(("std", b)))
                nc.vector.reciprocal(stat[:, b % 2, 2:3], stat[:, b % 2, 1:2]).then_inc(vector_done, 1)
                if b >= 2:
                    dve.wait_ge(tensor_done, E.after(("turned", b - 2)))
                dve.wait_ge(vector_done, V.after(("rstd", b)))
                nc.vector.tensor_scalar(xn[:, b % 2, :], acc[:, b, :], stat[:, b % 2, 2:3], None, ALU.mult).then_inc(vector_done, 1)
                dve.wait_ge(tensor_done, E.after(("turned", b)))
                for n in range(2):
                    ks = slice(4 * n, 4 * n + 4)
                    nc.vector.tensor_tensor(h2T[:, ks, b * P:(b + 1) * P], turned[b % 2][:, ks, :], bc(wcol[:, ks], 2, [P, 4, P]), ALU.mult).then_inc(vector_done, 1)


def norm_output(nc, norm_row, acc, out):
    with ExitStack() as ctx:
        sb, ps, sem = stage_tools(nc, ctx, "no")
        wrow = sb("w", [P, D])
        squares = sb("squares", [P, D])
        stat = sb("stat", [P, 3, TB])
        scaled = sb("scaled", [P, 2, D])
        eps = sb("eps", [P, 1])
        eps_set = sem("eps_set")
        w_in_sem = sem("w_in")
        out_sem = [sem(f"out{i}") for i in range(2)]
        scalar_done, vector_done = sem("scalar_done"), sem("vector_done")
        A = Steps(*[(s, b) for b in range(TB) for s in ("squares", "std")])
        V = Steps(*[(s, b) for b in range(TB) for s in ("rstd", "out")])
        block = ctx.enter_context(nc.Block())

        @block.sync
        def _(sp):
            sp.dma_start(wrow[:, :], norm_row.broadcast_to([P, D])).then_inc(w_in_sem, 16)
            for b in range(TB):
                sp.wait_ge(vector_done, V.after(("out", b)))
                sp.dma_start(out[b * P:(b + 1) * P, :], scaled[:, b % 2, :]).then_inc(out_sem[b % 2], 16)
            for i in range(2):
                sp.wait_ge(out_sem[i], 16 * TB // 2)

        @block.scalar
        def _(act):
            act.wait_ge(eps_set, 1)
            for b in range(TB):
                nc.scalar.activation(squares[:, :], acc[:, b, :], ACT.Square, accum_out=stat[:, 0, b:b + 1]).then_inc(scalar_done, 1)
                act.wait_ge(scalar_done, A.after(("squares", b)))
                nc.scalar.activation(stat[:, 1, b:b + 1], stat[:, 0, b:b + 1], ACT.Sqrt, scale=1.0 / D, bias=eps[:, :]).then_inc(scalar_done, 1)

        @block.vector
        def _(dve):
            nc.vector.memset(eps[:, :], EPS).then_inc(eps_set, 1)
            dve.wait_ge(w_in_sem, 16)
            for b in range(TB):
                dve.wait_ge(scalar_done, A.after(("std", b)))
                nc.vector.reciprocal(stat[:, 2, b:b + 1], stat[:, 1, b:b + 1]).then_inc(vector_done, 1)
                dve.wait_ge(vector_done, V.after(("rstd", b)))
                if b >= 2:
                    dve.wait_ge(out_sem[b % 2], 16 * (b // 2))
                nc.vector.scalar_tensor_tensor(scaled[:, b % 2, :], acc[:, b, :], stat[:, 2, b:b + 1], wrow[:, :], ALU.mult, ALU.mult).then_inc(vector_done, 1)


def peer_select(nc, core, w_q, keysT, h2T, slot_row, slot_col, slot_gate):
    K = TOPK
    LAST = 7
    LOWEST = -3.0e38
    with ExitStack() as ctx:
        sb, ps, sem = stage_tools(nc, ctx, "se")
        w = sb("w", [P, KC, 2 * P])
        keys = sb("keys", [P, 2, KEYS])
        qT = sb("qT", [P, 2, T])
        s = sb("s", [P, TB, 2, KEYS])
        rest = sb("rest", [P, 3, 2, KEYS])
        pace = sb("pace", [P, 1])
        val = sb("val", [P, TB, 2, K])
        idx = sb("idx", [P, TB, 2, K], U32)
        pair = sb("pair", [P, 3, K * K])
        pair_rest = sb("pair_rest", [P, 3, K * K])
        top = sb("top", [P, TB, K])
        pos = sb("pos", [P, TB, K], U32)
        part = sb("part", [P, 2, TB * K], U32)
        partf = sb("partf", [P, 2, TB, K])
        idxf = sb("idxf", [P, TB, 2, K])
        hit = sb("hit", [P, 2, TB, K, K])
        ex = sb("ex", [P, TB, K])
        total = sb("total", [P, 2, TB])
        pq = [ps(f"pq{i}", [P, HALF]) for i in range(4)]
        psc = [ps(f"psc{i}", [P, 2, 2, KEYS]) for i in range(4)]
        w_sem, keys_sem = sem("w_in"), sem("keys_in")
        tensor_done, scalar_done, vector_done, pool_done = (sem("tensor_done"), sem("scalar_done"), sem("vector_done"), sem("pool_done"))
        E = Steps(*[("q", i) for i in range(4)], *[("score", i) for i in range(4)])
        A = Steps(*[("q", i) for i in range(4)], *[("score", i) for i in range(4)], "exp")
        V = Steps(*[("rank", step) for step in range(TB + LAST)],
                  "shifted", "part0", "part1", "partf", "idxf", "equal0", "equal1", "sum", "recip", "gate", ("found", 0), ("found", 1))
        G = Steps(("hit", 0), ("hit", 1))
        block = ctx.enter_context(nc.Block())
        wv_ = kc_view(w_q)

        @block.sync
        def _(sp):
            with sp.Fori(0, PEER_HEADS) as h:
                sp.wait_ge(tensor_done, E.passes(h))
                sp.dma_start(w[:, :, :], wv_[:, :, bass.ds(h * 2 * P, 2 * P)]).then_inc(w_sem, 16)
                sp.dma_start(keys[:, :, :], keysT[bass.ds(h * 2, 2), :, :].rearrange("s d k -> d s k")).then_inc(keys_sem, 16)

        @block.tensor
        def _(pe):
            with pe.Fori(0, PEER_HEADS) as h:
                pe.wait_ge(w_sem, h * 16 + 16)
                pe.wait_ge(scalar_done, A.passes(h))
                for i in range(4):
                    p, half = i // 2, i % 2
                    for k in range(KC):
                        last = nc.tensor.matmul(pq[i][:, :], w[:, k, p * P:(p + 1) * P], h2T[:, k, half * HALF:(half + 1) * HALF],
                                                start=k == 0, stop=k == KC - 1)
                    last.then_inc(tensor_done, 1)
                pe.wait_ge(keys_sem, h * 16 + 16)
                pe.wait_ge(scalar_done, A.after(("q", 3), h))
                for i in range(4):
                    for tb in (2 * i, 2 * i + 1):
                        for p in range(2):
                            last = nc.tensor.matmul(psc[i][:, tb % 2, p, :], qT[:, p, tb * P:(tb + 1) * P], keys[:, p, :], start=True, stop=True)
                    last.then_inc(tensor_done, 1)

        @block.scalar
        def _(act):
            nc.scalar.preload_act_table_set(LOG_EXP)
            with act.Fori(0, PEER_HEADS) as h:
                for i in range(4):
                    act.wait_ge(tensor_done, E.after(("q", i), h))
                    nc.scalar.copy(qT[:, i // 2, (i % 2) * HALF:(i % 2 + 1) * HALF], pq[i][:, :]).then_inc(scalar_done, 1)
                act.wait_ge(vector_done, V.passes(h))
                for i in range(4):
                    act.wait_ge(tensor_done, E.after(("score", i), h))
                    nc.scalar.copy(s[:, 2 * i:2 * i + 2, :, :].rearrange("p b s k -> p (b s k)"),
                                   psc[i][:, :, :, :].rearrange("p b s k -> p (b s k)")).then_inc(scalar_done, 1)
                act.wait_ge(vector_done, V.after("shifted", h))
                nc.scalar.activation(ex[:, :, :], ex[:, :, :], ACT.Exp).then_inc(scalar_done, 1)

        @block.vector
        def _(dve):
            with dve.Fori(0, PEER_HEADS) as h:
                def chain(name):
                    dve.wait_ge(vector_done, V.after(name, h))

                for step in range(TB + LAST):
                    if step < TB and step % 2 == 0:
                        dve.wait_ge(scalar_done, A.after(("score", step // 2), h))
                    dve.wait_ge(vector_done, V.after(("rank", step - 1), h) if step else V.passes(h))
                    last = nc.vector.memset(pace[:, :], 0.0)
                    for p in range(2):
                        if step < TB:
                            last = nc.vector.max(val[:, step, p, 0:8], s[:, step, p, :])
                        if 0 <= (tb := step - 1) < TB:
                            nc.vector.max_index(idx[:, tb, p, 0:8], val[:, tb, p, 0:8], s[:, tb, p, :])
                            last = nc.vector.match_replace(rest[:, tb % 3, p, :], val[:, tb, p, 0:8], s[:, tb, p, :], LOWEST)
                        if 0 <= (tb := step - 2) < TB:
                            last = nc.vector.max(val[:, tb, p, 8:16], rest[:, tb % 3, p, :])
                        if 0 <= (tb := step - 3) < TB:
                            last = nc.vector.max_index(idx[:, tb, p, 8:16], val[:, tb, p, 8:16], rest[:, tb % 3, p, :])
                    if 0 <= (tb := step - 3) < TB:
                        last = nc.vector.tensor_tensor(pair[:, tb % 3, :].rearrange("p (a b) -> p a b", b=K), bc(val[:, tb, 0, :], 2, [P, K, K]),
                                                       bc(val[:, tb, 1, :], 1, [P, K, K]), ALU.add)
                    if 0 <= (tb := step - 4) < TB:
                        last = nc.vector.max(top[:, tb, 0:8], pair[:, tb % 3, :])
                    if 0 <= (tb := step - 5) < TB:
                        nc.vector.max_index(pos[:, tb, 0:8], top[:, tb, 0:8], pair[:, tb % 3, :])
                        last = nc.vector.match_replace(pair_rest[:, tb % 3, :], top[:, tb, 0:8], pair[:, tb % 3, :], LOWEST)
                    if 0 <= (tb := step - 6) < TB:
                        last = nc.vector.max(top[:, tb, 8:16], pair_rest[:, tb % 3, :])
                    if 0 <= (tb := step - 7) < TB:
                        last = nc.vector.max_index(pos[:, tb, 8:16], top[:, tb, 8:16], pair_rest[:, tb % 3, :])
                    last.then_inc(vector_done, 1)
                chain(("rank", TB + LAST - 1))
                nc.vector.tensor_tensor(ex[:, :, :], top[:, :, :], top[:, :, 0:1].broadcast_to([P, TB, K]), ALU.subtract).then_inc(vector_done, 1)
                posf = pos[:, :, :].rearrange("p b k -> p (b k)")
                nc.vector.tensor_scalar(part[:, 0, :], posf, 4, None, ALU.logical_shift_right).then_inc(vector_done, 1)
                nc.vector.tensor_scalar(part[:, 1, :], posf, K - 1, None, ALU.bitwise_and).then_inc(vector_done, 1)
                chain("part1")
                nc.vector.tensor_copy(partf[:, :, :, :].rearrange("p s b k -> p s (b k)"), part[:, :, :]).then_inc(vector_done, 1)
                nc.vector.tensor_copy(idxf[:, :, :, :], idx[:, :, :, :]).then_inc(vector_done, 1)
                chain("idxf")
                for p in range(2):
                    nc.vector.tensor_tensor(hit[:, p, :, :, :].rearrange("p b k r -> p (b k) r"),
                                            bc(core.const("iota")[:, 0:K], 1, [P, TB * K, K]),
                                            bc(partf[:, p, :, :].rearrange("p b k -> p (b k)"), 2, [P, TB * K, K]), ALU.is_equal).then_inc(vector_done, 1)
                dve.wait_ge(scalar_done, A.after("exp", h))
                nc.vector.tensor_reduce(total[:, 0, :], ex[:, :, :], AXX, ALU.add).then_inc(vector_done, 1)
                chain("sum")
                nc.vector.reciprocal(total[:, 1, :], total[:, 0, :]).then_inc(vector_done, 1)
                chain("recip")
                nc.vector.tensor_tensor(slot_gate[:, :, bass.ds(h * K, K)], ex[:, :, :], bc(total[:, 1, :], 2, [P, TB, K]), ALU.mult).then_inc(vector_done, 1)
                for p, out in enumerate((slot_row, slot_col)):
                    dve.wait_ge(pool_done, G.after(("hit", p), h))
                    nc.vector.tensor_reduce(out[:, :, bass.ds(h * K, K)], hit[:, p, :, :, :], AXX, ALU.add).then_inc(vector_done, 1)

        @block.gpsimd
        def _(pool):
            with pool.Fori(0, PEER_HEADS) as h:
                for p in range(2):
                    pool.wait_ge(vector_done, V.after(f"equal{p}", h))
                    nc.gpsimd.tensor_tensor(hit[:, p, :, :, :], hit[:, p, :, :, :], bc(idxf[:, :, p, :], 2, [P, TB, K, K]), ALU.mult).then_inc(pool_done, 1)


def gate_matrix(nc, core, slot_row, slot_col, slot_gate, gates):
    PER, RING, BLOCK = 4, 4, 64
    TURNS = BLOCK // (PER * RING)
    NB = T // BLOCK
    with ExitStack() as ctx:
        sb, ps, sem = stage_tools(nc, ctx, "gm")
        rowT = sb("rowT", [P, T])
        colT = sb("colT", [P, T])
        gateT = sb("gateT", [P, T])
        hot_row = sb("hot_row", [P, RING, PER, KEYS])
        hot_col = sb("hot_col", [P, RING, PER, KEYS])
        staged = sb("staged", [P, 2, KEYS, BLOCK])
        pt = [ps(f"pt{i}", [P, 2, HALF]) for i in range(2)]
        pg = [ps(f"pg{i}", [P, PER, KEYS]) for i in range(RING)]
        turned, copied = sem("turned"), sem("copied")
        hot = [sem(f"hot{r}") for r in range(RING)]
        multiplied = [sem(f"multiplied{r}") for r in range(RING)]
        collected = [sem(f"collected{r}") for r in range(RING)]
        stored = [sem(f"stored{i}") for i in range(2)]
        block = ctx.enter_context(nc.Block())
        tables = ((slot_row, rowT), (slot_col, colT), (slot_gate, gateT))

        def turn_of(i, half, j):
            return i * (2 * TURNS) + (j + half * TURNS)

        @block.tensor
        def _(pe):
            for n, (table, _) in enumerate(tables):
                if n == 2:
                    pe.wait_ge(copied, 1)
                for tb in range(TB):
                    last = nc.tensor.transpose(pt[n % 2][:, tb // 4, (tb % 4) * P:(tb % 4 + 1) * P], table[:, tb, :], core.const("ident"))
                last.then_inc(turned, 1)
            with pe.Fori(0, NB // 2) as i:
                for half in range(2):
                    with pe.Fori(0, TURNS) as j:
                        for r in range(RING):
                            n = turn_of(i, half, j)
                            pe.wait_ge(hot[r], n + 1)
                            pe.wait_ge(collected[r], n)
                            for x in range(PER):
                                last = nc.tensor.matmul(pg[r][:, x, :], hot_col[:, r, x, :], hot_row[:, r, x, :], start=True, stop=True)
                            last.then_inc(multiplied[r], 1)

        @block.vector
        def _(dve):
            dve.wait_ge(copied, 3)
            iota = core.const("iota")
            with dve.Fori(0, NB // 2) as i:
                for half in range(2):
                    with dve.Fori(0, TURNS) as j:
                        for r in range(RING):
                            n = turn_of(i, half, j)
                            dve.wait_ge(multiplied[r], n)
                            for x in range(PER):
                                t = bass.ds(n * (RING * PER) + (r * PER + x), 1)
                                nc.vector.tensor_scalar(hot_row[:, r, x, :], iota, rowT[:, t], None, ALU.is_equal)
                                last = nc.vector.tensor_scalar(hot_col[:, r, x, :], iota, colT[:, t], gateT[:, t], ALU.is_equal, ALU.mult)
                            last.then_inc(hot[r], 1)

        @block.scalar
        def _(act):
            for n, (_, table) in enumerate(tables):
                act.wait_ge(turned, n + 1)
                nc.scalar.copy(table[:, :], pt[n % 2][:, :, :].rearrange("p a t -> p (a t)")).then_inc(copied, 1)
            with act.Fori(0, NB // 2) as i:
                for half in range(2):
                    act.wait_ge(stored[half], i * 16)
                    with act.Fori(0, TURNS) as j:
                        for r in range(RING):
                            act.wait_ge(multiplied[r], turn_of(i, half, j) + 1)
                            nc.scalar.copy(staged[:, half, :, bass.ds(j * (RING * PER) + r * PER, PER)].rearrange("p k t -> p t k"),
                                           pg[r][:, :, :]).then_inc(collected[r], 1)

        @block.sync
        def _(sp):
            with sp.Fori(0, NB // 2) as i:
                for half in range(2):
                    for r in range(RING):
                        sp.wait_ge(collected[r], i * (2 * TURNS) + (half + 1) * TURNS)
                    sp.dma_start(gates[bass.ds(i * 2 + half, 1), :, :].rearrange("b p n -> (b p) n"),
                                 staged[:, half, :, :].rearrange("p k t -> p (k t)")).then_inc(stored[half], 16)
            for half in range(2):
                sp.wait_ge(stored[half], 16 * NB // 2)


def peer_experts(nc, uT, v, gates, h2T, acc):
    EG, BLOCK = 4, 64
    NG = KEYS // EG
    NB = T // BLOCK
    UNITS, RING = TB * 2, 4
    with ExitStack() as ctx:
        sb, ps, sem = stage_tools(nc, ctx, "pe")
        ut = sb("u", [P, 2, EG, D])
        vt = sb("v", [P, 2, EG, D])
        gt = sb("g", [P, 2, NB, EG, BLOCK])
        wt = sb("weights", [P, 2, EG, T])
        act_t = sb("act", [P, 2, T])
        pu = [ps(f"pu{i}", [P, 2, HALF]) for i in range(2)]
        pv = [ps(f"pv{i}", [P, HALF]) for i in range(RING)]
        u_in = [sem(f"u{i}_in") for i in range(2)]
        v_in = [sem(f"v{i}_in") for i in range(2)]
        g_in = [sem(f"g{i}_in") for i in range(2)]
        up_done, gelu_done, weighted, down_done = sem("up_done"), sem("gelu_done"), sem("weighted"), sem("down_done")
        added = [sem(f"added{i}") for i in range(RING)]
        block = ctx.enter_context(nc.Block())
        gv = gates.rearrange("b p (k t) -> p b k t", t=BLOCK)

        @block.sync
        def _(sp):
            def load(i, s, first):
                n = i * 2 + s
                if not first:
                    sp.wait_ge(up_done, (n - 1) * EG)
                sp.dma_start(ut[:, s, :, :], uT[bass.ds(n * EG, EG), :, :].rearrange("e p n -> p e n")).then_inc(u_in[s], 16)
                if not first:
                    sp.wait_ge(weighted, (n - 1) * EG)
                for e in range(EG):
                    sp.dma_start(gt[:, s, :, e, :], gv[:, :, bass.ds(n * EG + e, 1), :].rearrange("p b k t -> p b (k t)")).then_inc(g_in[s], 16)
                if not first:
                    sp.wait_ge(down_done, (n - 1) * UNITS)
                sp.dma_start(vt[:, s, :, :], v[bass.ds(n * EG * P, EG * P), :].rearrange("(e p) d -> p e d", p=P)).then_inc(v_in[s], 16)

            load(0, 0, True)
            load(0, 1, True)
            with sp.Fori(1, NG // 2) as i:
                load(i, 0, False)
                load(i, 1, False)

        def schedule(eng, up, down):
            up(0, 0, True)
            with eng.Fori(0, NG // 2 - 1) as i:
                up(i, 1, False)
                down(i, 0)
                up(i + 1, 0, False)
                down(i, 1)
            up(NG // 2 - 1, 1, False)
            down(NG // 2 - 1, 0)
            down(NG // 2 - 1, 1)

        @block.tensor
        def _(pe):
            def up(i, s, first):
                n = i * 2 + s
                pe.wait_ge(u_in[s], i * 16 + 16)
                for e in range(EG):
                    if not (first and e < 2):
                        pe.wait_ge(gelu_done, n * EG + (e - 1))
                    for half in range(2):
                        for k in range(KC):
                            last = nc.tensor.matmul(pu[e % 2][:, half, :], ut[:, s, e, k * P:(k + 1) * P], h2T[:, k, half * HALF:(half + 1) * HALF],
                                                    start=k == 0, stop=k == KC - 1)
                    last.then_inc(up_done, 1)

            def down(i, s):
                n = i * 2 + s
                pe.wait_ge(v_in[s], i * 16 + 16)
                pe.wait_ge(weighted, n * EG + EG)
                for x in range(UNITS):
                    tb, half = x // 2, x % 2
                    pe.wait_ge(added[x % RING], n * (UNITS // RING) + x // RING)
                    for e in range(EG):
                        last = nc.tensor.matmul(pv[x % RING][:, :], wt[:, s, e, tb * P:(tb + 1) * P], vt[:, s, e, half * HALF:(half + 1) * HALF],
                                                start=e == 0, stop=e == EG - 1)
                    last.then_inc(down_done, 1)

            schedule(pe, up, down)

        @block.scalar
        def _(act):
            def up(i, s, first):
                n = i * 2 + s
                for e in range(EG):
                    act.wait_ge(up_done, n * EG + (e + 1))
                    if not (first and e < 2):
                        act.wait_ge(weighted, n * EG + (e - 1))
                    nc.scalar.activation(act_t[:, e % 2, :], pu[e % 2][:, :, :].rearrange("p a t -> p (a t)"), ACT.Gelu).then_inc(gelu_done, 1)

            schedule(act, up, lambda i, s: None)

        @block.vector
        def _(dve):
            def up(i, s, first):
                n = i * 2 + s
                dve.wait_ge(g_in[s], i * (16 * EG) + 16 * EG)
                if not first:
                    dve.wait_ge(down_done, (n - 1) * UNITS)
                for e in range(EG):
                    dve.wait_ge(gelu_done, n * EG + (e + 1))
                    nc.vector.tensor_tensor(wt[:, s, e, :].rearrange("p (b t) -> p b t", t=BLOCK), act_t[:, e % 2, :].rearrange("p (b t) -> p b t", t=BLOCK),
                                            gt[:, s, :, e, :], ALU.mult).then_inc(weighted, 1)

            def down(i, s):
                n = i * 2 + s
                for x in range(UNITS):
                    a = acc[:, x // 2, (x % 2) * HALF:(x % 2 + 1) * HALF]
                    dve.wait_ge(down_done, n * UNITS + (x + 1))
                    nc.vector.tensor_tensor(a, a, pv[x % RING][:, :], ALU.add).then_inc(added[x % RING], 1)

            schedule(dve, up, down)


def packed_consts():
    import numpy as np

    r, c = np.arange(P)[:, None], np.arange(P)[None, :]
    mats = {
        "ident": r == c,
        "neg_from": -1.0 * (r >= c),
        "neg_before": -1.0 * (r < c),
        "causal_bias": NEG * (r >= c),
        "upto": r <= c,
        "beyond": r > c,
        "ones": np.ones((P, P)),
        "iota": c + 0 * r,
    }
    parts = [mats[name] for name in CONSTS]
    for m in LEVELS:
        parts.append((r // (2 * m) == c // (2 * m)) & (r % (2 * m) < m) & (c % (2 * m) >= m))
    parts.append(r == c)
    t = np.arange(T)[None, :]
    parts.append((t % P != 0) + 0 * r)
    return np.ascontiguousarray(np.concatenate([np.asarray(m, np.float32) for m in parts], axis=1))


def hybrid_layer(nc, a, gates, out):
    with ExitStack() as ctx:
        def sb(stack, name, shape):
            return stack.enter_context(nc.sbuf_tensor(name, shape, F32))

        hT = acc = sb(ctx, "hT_acc", [P, KC, T])
        y_sb_hg = h2T = sb(ctx, "y_h2T", [P, KC, T])
        ysbT, yhgT = y_sb_hg[:, 0:KC // 2, :], y_sb_hg[:, KC // 2:KC, :]
        with ExitStack() as upto_gates:
            core = Core(nc, upto_gates)
            with ExitStack() as mixer:
                norm_input(nc, core, a["x"], a["norm1_w"], a["consts"], hT)
                yssdT = sb(mixer, "yssdT", [P, KC // 2, T])
                stick_breaking(nc, core, a["w_in"], hT, ysbT)
                hgrn2(nc, core, a["w_in"], a["lb_logits"], a["hg_norm_w"], hT, yhgT)
                ssd(nc, core, a["w_in"], a["conv_wb"], a["ssd_rows"], a["ssd_norm_w"], hT, yssdT)
                mergedT = sb(mixer, "mergedT", [P, KC, T])
                merge(nc, core, a["w_in"], a["branch_w"], hT, [ysbT, yhgT, yssdT], mergedT)
                output_and_norm(nc, core, a["x"], a["w_out"], a["norm2_w"], mergedT, acc, h2T)
            slots = [sb(upto_gates, name, [P, TB, P]) for name in ("slot_row", "slot_col", "slot_gate")]
            peer_select(nc, core, a["peer_w_q"], a["keysT"], h2T, *slots)
            gate_matrix(nc, core, *slots, gates)
        peer_experts(nc, a["uT"], a["v"], gates, h2T, acc)
        norm_output(nc, a["final_norm_w"], acc, out)


def columns(w):
    return w.reshape(-1, P).T


def kernel(x, norm1_w, w_in, hg_lb_logits, hg_norm_w, ssd_conv_w, ssd_conv_b, ssd_dt_bias, ssd_a_log, ssd_d, ssd_norm_w,
           w_branch_sb, w_branch_hg, w_branch_ssd, w_out, norm2_w, peer_w_q, peer_sub_keys, peer_u, peer_v, final_norm_w):
    import concourse.bacc as bacc
    import numpy as np
    from concourse.bass_utils import run_bass_kernel_spmd

    laid_out = {
        "x": x[0],
        "norm1_w": columns(norm1_w[0]),
        "w_in": w_in[0],
        "lb_logits": columns(hg_lb_logits[0]),
        "hg_norm_w": columns(hg_norm_w[0]),
        "conv_wb": np.concatenate([ssd_conv_w[0].T, ssd_conv_b[0][:, None]], axis=1),
        "ssd_rows": np.stack([ssd_dt_bias[0], ssd_a_log[0], ssd_d[0]])[None],
        "ssd_norm_w": columns(ssd_norm_w[0]),
        "branch_w": np.concatenate([w_branch_sb, w_branch_hg, w_branch_ssd]),
        "w_out": w_out[0],
        "norm2_w": columns(norm2_w[0]),
        "peer_w_q": peer_w_q[0],
        "keysT": peer_sub_keys[0].reshape(2 * PEER_HEADS, KEYS, P).transpose(0, 2, 1),
        "uT": peer_u[0].reshape(KEYS, KEYS, KC, P).transpose(0, 3, 2, 1).reshape(KEYS, P, D),
        "v": peer_v[0],
        "final_norm_w": final_norm_w[None],
        "consts": packed_consts(),
    }
    laid_out = {name: np.ascontiguousarray(value) for name, value in laid_out.items()}
    nc = bacc.Bacc("TRN2", target_bir_lowering=False, num_devices=1)
    aps = {name: nc.dram_tensor(f"{name}_dram", value.shape, mybir.dt.from_np(value.dtype), kind="ExternalInput").ap()
           for name, value in laid_out.items()}
    gates = nc.dram_tensor("gates_dram", (T // 64, P, KEYS * 64), F32, kind="Internal").ap()
    out = nc.dram_tensor("out_dram", (T, D), F32, kind="ExternalOutput").ap()
    hybrid_layer(nc, aps, gates, out)
    result = run_bass_kernel_spmd(nc, [{f"{name}_dram": value for name, value in laid_out.items()}], core_ids=[0])
    return result.results[0]["out_dram"].reshape(1, T, D)
```

```python
from contextlib import ExitStack

import concourse.bass as bass
from concourse import mybir

F32 = mybir.dt.float32
U32 = mybir.dt.uint32
ALU = mybir.AluOpType
ACT = mybir.ActivationFunctionType
AXX = mybir.AxisListType.X

P = 128
T = 1024
D = 1024
KC = D // P
TB = T // P
HALF = 512
EPS = 1e-6

SB_HEADS, SB_DIM = 8, 64
HG_HEADS, HG_DIM = 4, 128
SSD_HEADS, SSD_DIM, SSD_GROUPS, SSD_STATE, SSD_CONV = 8, 64, 2, 64, 4
SSD_HPG = SSD_HEADS // SSD_GROUPS
SSD_GW = SSD_HPG * SSD_DIM
SB_W = SB_HEADS * SB_DIM
HG_W = HG_HEADS * HG_DIM
SSD_W = SSD_HEADS * SSD_DIM
COL_Q = 0
COL_K = COL_Q + SB_W
COL_V = COL_K + SB_W
COL_HF = COL_V + SB_W
COL_HQ = COL_HF + HG_W
COL_HI = COL_HQ + HG_W
COL_HG = COL_HI + HG_W
COL_Z = COL_HG + HG_W
COL_X = COL_Z + SSD_W
COL_B = COL_X + SSD_W
COL_C = COL_B + SSD_GROUPS * SSD_STATE
COL_DT = COL_C + SSD_GROUPS * SSD_STATE
COL_G = COL_DT + SSD_HEADS

PEER_HEADS, KEYS, TOPK = 8, 128, 16
NEG = -1e30
LOG_EXP = "natural_log_exp_and_others"

CONSTS = ("ident", "neg_from", "neg_before", "causal_bias", "upto", "beyond", "ones", "iota")
LEVELS = [64, 32, 16, 8, 4, 2, 1]
C_AT = {name: P * i for i, name in enumerate(CONSTS)}
C_LEVEL = P * len(CONSTS)
C_RESET = C_LEVEL + P * (len(LEVELS) + 1)
C_COLS = C_RESET + T


F32R = mybir.dt.float32r


def product_of_parts(nc, out, a_high, a_rest, b_high, b_rest, start, stop):
    nc.tensor.matmul(out, a_high, b_high, start=start, stop=False)
    nc.tensor.matmul(out, a_high, b_rest, start=False, stop=False)
    return nc.tensor.matmul(out, a_rest, b_high, start=False, stop=stop)


class Steps:

    def __init__(self, *names):
        self.at = {name: i + 1 for i, name in enumerate(names)}
        self.per = len(names)
        assert len(self.at) == self.per

    def after(self, name, n=0):
        return n * self.per + (self.at[name] + 1)

    def passes(self, n):
        return n * self.per + 1


def kc_view(w):
    return w.rearrange("(k p) c -> p k c", p=P)


def bc(ap, axis, shape):
    return ap.unsqueeze(axis).broadcast_to(shape)


class Core:

    def __init__(self, nc, ctx):
        self.nc = nc
        self.ctx = ctx
        self.consts = ctx.enter_context(nc.sbuf_tensor("consts", [P, C_COLS], F32))
        self.eps = ctx.enter_context(nc.sbuf_tensor("eps", [P, 1], F32))

    def const(self, name):
        at = C_AT[name]
        return self.consts[:, at:at + P]

    def level_mask(self, n):
        return self.consts[:, C_LEVEL + P * n:C_LEVEL + P * (n + 1)]


def stage_tools(nc, ctx, prefix):

    def sb(name, shape, dt=F32):
        return ctx.enter_context(nc.sbuf_tensor(f"{prefix}_{name}", shape, dt))

    def ps(name, shape):
        return ctx.enter_context(nc.psum_tensor(f"{prefix}_{name}", shape, F32))

    def sem(name):
        return ctx.enter_context(nc.semaphore(f"{prefix}_{name}"))

    return sb, ps, sem


def norm_input(nc, core, x, norm_w, packed_consts, hT):
    with ExitStack() as ctx:
        sb, ps, sem = stage_tools(nc, ctx, "ni")
        xt = sb("x", [P, 2, D])
        squares = sb("squares", [P, D])
        xn = sb("xn", [P, 2, D])
        stat = sb("stat", [P, 3])
        wcol = sb("wcol", [P, KC])
        turned = ps("turned", [P, KC, P])
        consts_in, w_in = sem("consts_in"), sem("w_in")
        x_in = [sem(f"x_in{j}") for j in range(2)]
        scalar_done, vector_done, tensor_done = sem("scalar_done"), sem("vector_done"), sem("tensor_done")
        eps_set = sem("eps_set")
        A = Steps(*[(s, j) for j in range(2) for s in ("squares", "std")])
        V = Steps(*[(s, j) for j in range(2) for s in ("rstd", "xn", "turned0", "turned1")])
        E = Steps(("turned", 0), ("turned", 1))
        block = ctx.enter_context(nc.Block())
        xv = x.rearrange("(b p) d -> p b d", p=P)

        @block.sync
        def _(sp):
            sp.dma_start(core.consts[:, :], packed_consts).then_inc(consts_in, 16)
            sp.dma_start(wcol[:, :], norm_w).then_inc(w_in, 16)
            with sp.Fori(0, TB // 2) as i:
                for j in range(2):
                    sp.wait_ge(vector_done, V.passes(i))
                    sp.dma_start(xt[:, j, :], xv[:, bass.ds(i * 2 + j, 1), :].rearrange("p b d -> p (b d)")).then_inc(x_in[j], 16)

        @block.scalar
        def _(act):
            act.sem_inc(scalar_done, 1)
            act.wait_ge(eps_set, 1)
            with act.Fori(0, TB // 2) as i:
                for j in range(2):
                    act.wait_ge(x_in[j], i * 16 + 16)
                    act.wait_ge(vector_done, V.passes(i) if j == 0 else V.after(("xn", 0), i))
                    nc.scalar.activation(squares[:, :], xt[:, j, :], ACT.Square, accum_out=stat[:, 0:1]).then_inc(scalar_done, 1)
                    act.wait_ge(scalar_done, A.after(("squares", j), i))
                    nc.scalar.activation(stat[:, 1:2], stat[:, 0:1], ACT.Sqrt, scale=1.0 / D, bias=core.eps[:, :]).then_inc(scalar_done, 1)

        @block.vector
        def _(dve):
            dve.sem_inc(vector_done, 1)
            nc.vector.memset(core.eps[:, :], EPS).then_inc(eps_set, 1)
            dve.wait_ge(w_in, 16)
            with dve.Fori(0, TB // 2) as i:
                for j in range(2):
                    dve.wait_ge(scalar_done, A.after(("std", j), i))
                    nc.vector.reciprocal(stat[:, 2:3], stat[:, 1:2]).then_inc(vector_done, 1)
                    dve.wait_ge(vector_done, V.after(("rstd", j), i))
                    dve.wait_ge(tensor_done, E.passes(i))
                    nc.vector.tensor_scalar(xn[:, j, :], xt[:, j, :], stat[:, 2:3], None, ALU.mult).then_inc(vector_done, 1)
                    dve.wait_ge(tensor_done, E.after(("turned", j), i))
                    for b in range(2):
                        ks = slice(4 * b, 4 * b + 4)
                        nc.vector.tensor_tensor(hT[:, ks, bass.ts(i * 2 + j, P)], turned[:, ks, :],
                                                bc(wcol[:, ks], 2, [P, 4, P]), ALU.mult).then_inc(vector_done, 1)

        @block.tensor
        def _(pe):
            pe.sem_inc(tensor_done, 1)
            pe.wait_ge(consts_in, 16)
            with pe.Fori(0, TB // 2) as i:
                for j in range(2):
                    pe.wait_ge(vector_done, V.after(("xn", j), i))
                    for k in range(KC):
                        last = nc.tensor.transpose(turned[:, k, :], xn[:, j, k * P:(k + 1) * P], core.const("ident"))
                    last.then_inc(tensor_done, 1)


def stick_breaking(nc, core, w_in, hT, ysbT):
    with ExitStack() as ctx:
        sb, ps, sem = stage_tools(nc, ctx, "sb")
        wq = sb("wq", [P, KC, P])
        wk = sb("wk", [P, KC, P])
        wv = sb("wv", [P, KC, P])
        qT = sb("qT", [P, T])
        kT = sb("kT", [P, T])
        v = sb("v", [P, TB, P])
        NZ = 5
        SOFT, TAIL, REST, EXP, Y = 1, 2, 3, 3, 4
        zs = sb("zs", [P, NZ, HALF])
        mag = sb("mag", [P, NZ, HALF])
        soft = sb("soft", [P, NZ, HALF])
        aT = sb("aT", [P, NZ, HALF])
        pz = [ps(f"pz{i}", [P, HALF]) for i in range(3)]
        pacc = [ps(f"pacc{i}", [P, HALF]) for i in range(2)]
        py = ps("py", [P, HALF])
        pp = [ps(f"pp{i}", [P, HALF]) for i in range(2)]
        w_in_sem = [sem(f"w{n}_in") for n in "qkv"]
        tensor_done, scalar_done, vector_done = sem("tensor_done"), sem("scalar_done"), sem("vector_done")

        tiles = []
        for half in range(2):
            for kb in reversed(range(4 * half + 4)):
                for head in range(2):
                    tiles.append((head, half, kb, max(0, kb - 4 * half) * P))
        N = len(tiles)
        diagonal = [kb >= 4 * half for _, half, kb, _ in tiles]
        ends = {max(i for i, t in enumerate(tiles) if t[1] == half): half for half in range(2)}
        units = [("q", 0), ("q", 1), ("k", 0), ("k", 1)] + [("v", n) for n in range(2)]

        e_names = [("proj", u) for u in units]
        for s in range(N + Y):
            e_names += [("z", s)] * (s < N) + [("rest", s - REST)] * (REST <= s < N + REST)
            e_names += [("tail", s - TAIL)] * (TAIL <= s < N + TAIL) + [("y", s - Y)] * (s >= Y)
        E = Steps(*e_names)
        v_names = []
        for s in range(N + TAIL):
            if s < N:
                v_names += [("zs", s)] + [("zd", s)] * (diagonal[s] and tiles[s][3] + P < HALF)
            v_names += [("soft", s - SOFT)] * (SOFT <= s < N + SOFT) + [("arg", s - TAIL)] * (s >= TAIL)
        V = Steps(*v_names)
        a_names = [("proj", u) for u in units]
        for s in range(N + EXP):
            a_names += [("mag", s), ("exp", s), ("ln", s)] * (s < N) + [("weights", s - EXP)] * (s >= EXP)
            a_names += [("out", ends[s - Y])] if s - Y in ends else []
        a_names += [("out", 1)]
        A = Steps(*a_names)
        block = ctx.enter_context(nc.Block())
        wv_ = kc_view(w_in)

        @block.sync
        def _(sp):
            def load(c):
                for dst, col, s in ((wq, COL_Q, 0), (wk, COL_K, 1), (wv, COL_V, 2)):
                    sp.dma_start(dst[:, :, :], wv_[:, :, bass.ds(c * P + col, P)]).then_inc(w_in_sem[s], 16)

            load(0)
            with sp.Fori(1, SB_HEADS // 2) as c:
                sp.wait_ge(tensor_done, E.after(("proj", units[-1]), c - 1))
                load(c)

        @block.tensor
        def _(pe):
            pe.sem_inc(tensor_done, 1)
            with pe.Fori(0, SB_HEADS // 2) as c:
                for n, (kind, part) in enumerate(units):
                    pe.wait_ge(w_in_sem["qkv".index(kind)], c * 16 + 16)
                    pe.wait_ge(scalar_done, A.passes(c) if n < 2 else A.after(("proj", units[n - 2]), c))
                    if kind in "qk":
                        w = wq if kind == "q" else wk
                        for k in range(KC):
                            last = nc.tensor.matmul(pp[n % 2][:, :], w[:, k, :], hT[:, k, part * HALF:(part + 1) * HALF],
                                                    start=k == 0, stop=k == KC - 1)
                    else:
                        for tb in range(4):
                            for k in range(KC):
                                last = nc.tensor.matmul(pp[n % 2][:, tb * P:(tb + 1) * P],
                                                        hT[:, k, (4 * part + tb) * P:(4 * part + tb + 1) * P],
                                                        wv[:, k, :], start=k == 0, stop=k == KC - 1)
                    last.then_inc(tensor_done, 1)
                pe.wait_ge(scalar_done, A.after(("proj", units[-1]), c))
                for s in range(N + Y):
                    if s < N:
                        head, half, kb, q0 = tiles[s]
                        hp = slice(64 * head, 64 * head + 64)
                        if s >= 3:
                            pe.wait_ge(vector_done, V.after(("zd" if ("zd", s - 3) in V.at else "zs", s - 3), c))
                        nc.tensor.matmul(pz[s % 3][:, q0:HALF], kT[hp, kb * P:(kb + 1) * P],
                                         qT[hp, half * HALF + q0:(half + 1) * HALF],
                                         start=True, stop=True).then_inc(tensor_done, 1)
                    if REST <= s < N + REST:
                        r = s - REST
                        head, half, kb, q0 = tiles[r]
                        pe.wait_ge(vector_done, V.after(("arg", r), c))
                        nc.tensor.matmul(pacc[head][:, q0:HALF], core.const("neg_before"), soft[:, r % NZ, q0:HALF],
                                         start=False, stop=True, skip_group_check=True).then_inc(tensor_done, 1)
                    if TAIL <= s < N + TAIL:
                        r = s - TAIL
                        head, half, kb, q0 = tiles[r]
                        pe.wait_ge(vector_done, V.after(("soft", r), c))
                        nc.tensor.matmul(pacc[head][:, q0:HALF], core.const("neg_from"), soft[:, r % NZ, q0:HALF],
                                         start=kb == 4 * half + 3, stop=False, skip_group_check=True).then_inc(tensor_done, 1)
                    if s >= Y:
                        r = s - Y
                        head, half, kb, q0 = tiles[r]
                        pe.wait_ge(scalar_done, A.after(("weights", r), c))
                        if half == 1 and kb == 7:
                            pe.wait_ge(scalar_done, A.after(("out", 0), c))
                        nc.tensor.matmul(py[64 * head:64 * head + 64, q0:HALF], v[:, kb, 64 * head:64 * head + 64],
                                         aT[:, r % NZ, q0:HALF], start=kb == 4 * half + 3, stop=kb == 0,
                                         skip_group_check=True).then_inc(tensor_done, 1)

        @block.scalar
        def _(act):
            act.sem_inc(scalar_done, 1)
            nc.scalar.preload_act_table_set(LOG_EXP)
            with act.Fori(0, SB_HEADS // 2) as c:
                for n, (kind, part) in enumerate(units):
                    act.wait_ge(tensor_done, E.after(("proj", units[n]), c))
                    if kind == "q":
                        nc.scalar.mul(qT[:, part * HALF:(part + 1) * HALF], pp[n % 2][:, :], SB_DIM ** -0.5).then_inc(scalar_done, 1)
                    elif kind == "k":
                        nc.scalar.copy(kT[:, part * HALF:(part + 1) * HALF], pp[n % 2][:, :]).then_inc(scalar_done, 1)
                    else:
                        nc.scalar.copy(v[:, 4 * part:4 * part + 4, :].rearrange("p b d -> p (b d)"), pp[n % 2][:, :]).then_inc(scalar_done, 1)

                def out(half):
                    last = max(i for i, t in enumerate(tiles) if t[1] == half)
                    act.wait_ge(tensor_done, E.after(("y", last), c))
                    nc.scalar.copy(ysbT[:, bass.ds(c, 1), half * HALF:(half + 1) * HALF].rearrange("p c t -> p (c t)"),
                                   py[:, :]).then_inc(scalar_done, 1)

                for s in range(N + EXP):
                    if s < N:
                        q0 = tiles[s][3]
                        act.wait_ge(vector_done, V.after(("zd" if ("zd", s) in V.at else "zs", s), c))
                        nc.scalar.activation(mag[:, s % NZ, q0:HALF], zs[:, s % NZ, q0:HALF], ACT.Abs).then_inc(scalar_done, 1)
                        act.wait_ge(scalar_done, A.after(("mag", s), c))
                        nc.scalar.activation(mag[:, s % NZ, q0:HALF], mag[:, s % NZ, q0:HALF], ACT.Exp, scale=-1.0).then_inc(scalar_done, 1)
                        act.wait_ge(scalar_done, A.after(("exp", s), c))
                        nc.scalar.activation(mag[:, s % NZ, q0:HALF], mag[:, s % NZ, q0:HALF], ACT.Ln, bias=1.0).then_inc(scalar_done, 1)
                    if s >= EXP:
                        r = s - EXP
                        q0 = tiles[r][3]
                        act.wait_ge(vector_done, V.after(("arg", r), c))
                        if r >= NZ:
                            act.wait_ge(tensor_done, E.after(("y", r - NZ), c))
                        nc.scalar.activation(aT[:, r % NZ, q0:HALF], zs[:, r % NZ, q0:HALF], ACT.Exp).then_inc(scalar_done, 1)
                    if s - Y in ends:
                        out(ends[s - Y])
                out(1)

        @block.vector
        def _(dve):
            dve.sem_inc(vector_done, 1)
            with dve.Fori(0, SB_HEADS // 2) as c:
                for s in range(N + TAIL):
                    if s < N:
                        q0 = tiles[s][3]
                        dve.wait_ge(tensor_done, E.after(("z", s), c))
                        dve.wait_ge(scalar_done, A.after(("weights", s - NZ), c) if s >= NZ else A.passes(c))
                        if diagonal[s]:
                            nc.vector.tensor_tensor(zs[:, s % NZ, q0:q0 + P], pz[s % 3][:, q0:q0 + P],
                                                    core.const("causal_bias"), ALU.add).then_inc(vector_done, 1)
                            if q0 + P < HALF:
                                nc.vector.tensor_copy(zs[:, s % NZ, q0 + P:HALF], pz[s % 3][:, q0 + P:HALF]).then_inc(vector_done, 1)
                        else:
                            nc.vector.tensor_copy(zs[:, s % NZ, :], pz[s % 3][:, :]).then_inc(vector_done, 1)
                    if SOFT <= s < N + SOFT:
                        r = s - SOFT
                        q0 = tiles[r][3]
                        dve.wait_ge(scalar_done, A.after(("ln", r), c))
                        if r >= NZ:
                            dve.wait_ge(tensor_done, E.after(("rest", r - NZ), c))
                        nc.vector.scalar_tensor_tensor(soft[:, r % NZ, q0:HALF], zs[:, r % NZ, q0:HALF], 0.0,
                                                       mag[:, r % NZ, q0:HALF], ALU.max, ALU.add).then_inc(vector_done, 1)
                    if s >= TAIL:
                        r = s - TAIL
                        q0 = tiles[r][3]
                        dve.wait_ge(tensor_done, E.after(("tail", r), c))
                        nc.vector.tensor_tensor(zs[:, r % NZ, q0:HALF], zs[:, r % NZ, q0:HALF],
                                                pacc[tiles[r][0]][:, q0:HALF], ALU.add).then_inc(vector_done, 1)


def hgrn2(nc, core, w_in, lb_logits, norm_w, hT, yhgT):
    NL = len(LEVELS)
    with ExitStack() as ctx:
        sb, ps, sem = stage_tools(nc, ctx, "hg")
        w = sb("w", [P, 4, KC, P])
        logits = sb("lb_logits", [P, HG_HEADS])
        shifted = sb("shifted", [P, HG_HEADS])
        gamma_of = sb("gamma", [P, 2, HG_HEADS])
        lower = sb("lower", [P, HG_HEADS])
        upper = sb("upper", [P, HG_HEADS])
        lb = sb("lb", [P, 2])
        nw = sb("norm_w", [P, 1])
        ln_c = sb("ln_c", [P, 2])
        e1 = sb("e1", [P, T])
        e2 = sb("e2", [P, T])
        q = sb("q", [P, T])
        key = sb("key", [P, T])
        logf = sb("logf", [P, T])
        b = sb("b", [P, TB, P])
        ebl = sb("chunk_decay", [P, TB])
        XR = 3
        x = sb("x", [P, XR, T])
        masked = sb("masked", [P, 2, T])
        eq = sb("eq", [P, T])
        q_raw = sb("q_raw", [P, T])
        scores = sb("scores", [P, TB, P])
        v = sb("v", [P, TB, P])
        gate = sb("gate", [P, TB, P])
        kd = sb("kd", [P, TB, P])
        kdn = sb("kdn", [P, TB, P])
        qd = sb("qd", [P, TB, P])
        state = sb("state", [P, TB, P])
        y = sb("y", [P, TB, P])
        ss = sb("ss", [P, 3 * TB])
        big = [ps(f"big{i}", [P, 2, HALF]) for i in range(4)]
        w_sem = [sem(f"w{n}_in") for n in range(4)]
        small_in = sem("small_in")
        nw_in = sem("norm_w_in")
        tensor_done, scalar_done, vector_done, pool_done = (sem("tensor_done"), sem("scalar_done"), sem("vector_done"), sem("pool_done"))
        projected, taken = sem("projected"), sem("taken")

        E = Steps("i", "g", "same", *[("level", n) for n in range(NL)], "kdn", "dstate", "o", "yT")
        EF = Steps("f", "q")
        L = Steps("shifted", "recip", "gamma", "lower", "upper")
        V = Steps("lb", "one_minus_lb", "e1p", "f", "e2p", "key", "f_lb", "key_lb", "f_hi", "f_lo", "logf", "b",
                  "qp", "qr", "q", "kd_arg", "kd", "qd", ("diff", 0), ("diff", 1), "gp", "gr", "gate",
                  "same_masked", ("left", 0), ("right", 0),
                  *[step for n in range(NL) for step in [("left", n + 1), ("right", n + 1)] * (n + 1 < NL)
                    + [("diff", n + 2)] * (n + 2 < NL) + [("masked", n)]],
                  *[("state", n) for n in range(1, TB)], "ss", "rstd", "y_rstd", "y")
        A = Steps("ln_hi", "ln_lo", "v", "exp_b", "kd_exp", "chunk_decay",
                  *[(s, n) for n in range(2) for s in ("decay_left", "decay_right")], "eg",
                  *[(s, n) for n in range(2, NL) for s in ("decay_left", "decay_right")], "kdn", "square", "std", "yT")
        AF = Steps("e1", "e2", "eq", "q_raw")
        G = Steps(*[("sum", n) for n in range(NL)])
        lnc_done, const_set = sem("ln_c_done"), sem("const_set")
        bound_done, bound_exp_done = sem("bound_done"), sem("bound_exp_done")
        block = ctx.enter_context(nc.Block())
        wv_ = kc_view(w_in)
        CUT, UP = 2.0 ** -40, 2.0 ** 60

        def flat(ap):
            return ap.rearrange("p b d -> p (b d)")

        @block.sync
        def _(sp):
            sp.dma_start(nw[:, :], norm_w).then_inc(nw_in, 16)
            sp.dma_start(logits[:, :], lb_logits).then_inc(small_in, 16)
            def load(h, names):
                for n in names:
                    col = (COL_HF, COL_HQ, COL_HI, COL_HG)[n]
                    sp.dma_start(w[:, n, :, :], wv_[:, :, bass.ds(h * P + col, P)]).then_inc(w_sem[n], 16)

            load(0, range(4))
            with sp.Fori(1, HG_HEADS) as h:
                sp.wait_ge(projected, EF.after("q", h - 1))
                load(h, (0, 1))
                sp.wait_ge(tensor_done, E.after("g", h - 1))
                load(h, (2, 3))

        @block.tensor
        def _(pe):
            pe.sem_inc(tensor_done, 1)
            pe.sem_inc(projected, 1)

            def project_ahead(h, pieces):
                for n, half, k in pieces:
                    if half == 0 and k == 0:
                        pe.wait_ge(w_sem[n], h * 16 + 16)
                    last = nc.tensor.matmul(big[2 + n][:, half, :], w[:, n, k, :], hT[:, k, half * HALF:(half + 1) * HALF],
                                            start=k == 0, stop=k == KC - 1)
                    if half == 1 and k == KC - 1:
                        last.then_inc(projected, 1)

            pieces = [(n, half, k) for n in range(2) for half in range(2) for k in range(KC)]

            def one_head(h, last_head):
                pe.wait_ge(scalar_done, A.passes(h))
                pe.wait_ge(vector_done, V.passes(h))
                for n, name in enumerate(("i", "g")):
                    pe.wait_ge(taken, AF.after(("e2", "q_raw")[n], h))
                    pe.wait_ge(w_sem[2 + n], h * 16 + 16)
                    for tb in range(TB):
                        for k in range(KC):
                            last = nc.tensor.matmul(big[2 + n][:, tb // 4, (tb % 4) * P:(tb % 4 + 1) * P], hT[:, k, tb * P:(tb + 1) * P],
                                                    w[:, 2 + n, k, :], start=k == 0, stop=k == KC - 1)
                    last.then_inc(tensor_done, 1)
                pe.wait_ge(vector_done, V.after("q", h))
                for c in range(TB):
                    cs = slice(c * P, (c + 1) * P)
                    last = nc.tensor.matmul(big[0][:, c // 4, (c % 4) * P:(c % 4 + 1) * P], key[:, cs], q[:, cs], start=True, stop=True)
                last.then_inc(tensor_done, 1)
                for n in range(NL):
                    pe.wait_ge(vector_done, V.after(("right", n), h))
                    if n >= 1:
                        pe.wait_ge(vector_done, V.after("same_masked" if n == 1 else ("masked", n - 2), h))
                    for c in range(TB):
                        cs = slice(c * P, (c + 1) * P)
                        last = nc.tensor.matmul(big[(n + 1) % 2][:, c // 4, (c % 4) * P:(c % 4 + 1) * P], x[:, n % XR, cs], x[:, n % XR, cs],
                                                start=True, stop=True)
                    last.then_inc(tensor_done, 1)
                    if not last_head:
                        if n == 0:
                            pe.wait_ge(scalar_done, A.after("v", h))
                            pe.wait_ge(vector_done, V.after("gate", h))
                        per = -(-len(pieces) // NL)
                        project_ahead(h + 1, pieces[n * per:(n + 1) * per])
                if last_head:
                    pe.wait_ge(scalar_done, A.after("v", h))
                else:
                    pe.wait_ge(taken, AF.after("e2", h + 1))
                pe.wait_ge(vector_done, V.after("kd", h))
                for c in range(TB):
                    last = nc.tensor.transpose(big[2][:, c // 4, (c % 4) * P:(c % 4 + 1) * P], kd[:, c, :], core.const("ident"))
                last.then_inc(tensor_done, 1)
                pe.wait_ge(scalar_done, A.after("kdn", h))
                pe.wait_ge(vector_done, V.after("gate", h))
                if not last_head:
                    pe.wait_ge(taken, AF.after("q_raw", h + 1))
                for c in range(TB):
                    last = nc.tensor.matmul(big[3][:, c // 4, (c % 4) * P:(c % 4 + 1) * P], kdn[:, c, :], v[:, c, :], start=True, stop=True)
                last.then_inc(tensor_done, 1)
                pe.wait_ge(vector_done, V.after(("state", TB - 1), h))
                pe.wait_ge(pool_done, G.after(("sum", NL - 1), h))
                for c in range(TB):
                    o = big[0][:, c // 4, (c % 4) * P:(c % 4 + 1) * P]
                    last = nc.tensor.matmul(o, scores[:, c, :], v[:, c, :], start=True, stop=c == 0)
                    if c:
                        last = nc.tensor.matmul(o, qd[:, c, :], state[:, c, :], start=False, stop=True)
                last.then_inc(tensor_done, 1)
                pe.wait_ge(vector_done, V.after("y", h))
                for c in range(TB):
                    last = nc.tensor.transpose(big[1][:, c // 4, (c % 4) * P:(c % 4 + 1) * P], y[:, c, :], core.const("ident"))
                last.then_inc(tensor_done, 1)

            project_ahead(0, pieces)
            with pe.Fori(0, HG_HEADS - 1) as h:
                one_head(h, False)
            one_head(HG_HEADS - 1, True)

        @block.scalar
        def _(act):
            act.sem_inc(scalar_done, 1)
            nc.scalar.preload_act_table_set(LOG_EXP)
            act.wait_ge(const_set, 1)
            nc.scalar.activation(ln_c[:, 1:2], ln_c[:, 0:1], ACT.Ln).then_inc(lnc_done, 1)
            act.wait_ge(bound_done, L.after("shifted"))
            nc.scalar.activation(gamma_of[:, 0, :], shifted[:, :], ACT.Exp).then_inc(bound_exp_done, 1)
            act.wait_ge(nw_in, 16)
            def take_f(h):
                act.wait_ge(projected, EF.after("f", h))
                nc.scalar.activation(e1[:, :], flat(big[2][:, :, :]), ACT.Exp, scale=-1.0).then_inc(taken, 1)
                nc.scalar.activation(e2[:, :], flat(big[2][:, :, :]), ACT.Exp).then_inc(taken, 1)

            def take_q(h):
                act.wait_ge(projected, EF.after("q", h))
                nc.scalar.activation(eq[:, :], flat(big[3][:, :, :]), ACT.Exp, scale=-1.0).then_inc(taken, 1)
                nc.scalar.copy(q_raw[:, :], flat(big[3][:, :, :])).then_inc(taken, 1)

            def decays(h, n):
                act.wait_ge(vector_done, V.after(("diff", n), h))
                xv = x[:, n % XR, :].rearrange("p (b s m) -> p b s m", s=2, m=LEVELS[n])
                nc.scalar.activation(xv[:, :, 0, :], xv[:, :, 0, :], ACT.Exp, scale=-1.0).then_inc(scalar_done, 1)
                nc.scalar.activation(xv[:, :, 1, :], xv[:, :, 1, :], ACT.Exp).then_inc(scalar_done, 1)

            def one_head(h, last_head):
                act.wait_ge(vector_done, V.after("f_lo", h))
                nc.scalar.activation(e1[:, :], e1[:, :], ACT.Ln).then_inc(scalar_done, 1)
                nc.scalar.activation(e2[:, :], e2[:, :], ACT.Ln, scale=UP).then_inc(scalar_done, 1)
                act.wait_ge(tensor_done, E.after("i", h))
                nc.scalar.copy(flat(v[:, :, :]), flat(big[2][:, :, :])).then_inc(scalar_done, 1)
                act.wait_ge(vector_done, V.after("b", h))
                nc.scalar.activation(flat(qd[:, :, :]), flat(b[:, :, :]), ACT.Exp).then_inc(scalar_done, 1)
                act.wait_ge(vector_done, V.after("kd_arg", h))
                nc.scalar.activation(flat(kd[:, :, :]), flat(kd[:, :, :]), ACT.Exp).then_inc(scalar_done, 1)
                nc.scalar.activation(ebl[:, :], b[:, :, P - 1], ACT.Exp).then_inc(scalar_done, 1)
                decays(h, 0)
                decays(h, 1)
                act.wait_ge(tensor_done, E.after("g", h))
                nc.scalar.activation(flat(gate[:, :, :]), flat(big[3][:, :, :]), ACT.Exp, scale=-1.0).then_inc(scalar_done, 1)
                for n in range(2, NL):
                    decays(h, n)
                    if n == NL - 2 and not last_head:
                        act.wait_ge(vector_done, V.after("gate", h))
                        take_f(h + 1)
                if not last_head:
                    take_q(h + 1)
                act.wait_ge(tensor_done, E.after("kdn", h))
                nc.scalar.copy(flat(kdn[:, :, :]), flat(big[2][:, :, :])).then_inc(scalar_done, 1)
                act.wait_ge(tensor_done, E.after("o", h))
                nc.scalar.activation(logf[:, :], flat(big[0][:, :, :]), ACT.Square).then_inc(scalar_done, 1)
                act.wait_ge(vector_done, V.after("ss", h))
                nc.scalar.activation(ss[:, TB:2 * TB], ss[:, 0:TB], ACT.Sqrt, scale=1.0 / HG_DIM, bias=core.eps[:, :]).then_inc(scalar_done, 1)
                act.wait_ge(tensor_done, E.after("yT", h))
                nc.scalar.activation(yhgT[:, bass.ds(h, 1), :].rearrange("p c t -> p (c t)"), flat(big[1][:, :, :]),
                                     ACT.Copy, scale=nw[:, :]).then_inc(scalar_done, 1)

            act.sem_inc(taken, 1)
            take_f(0)
            take_q(0)
            with act.Fori(0, HG_HEADS - 1) as h:
                one_head(h, False)
            one_head(HG_HEADS - 1, True)

        @block.vector
        def _(dve):
            dve.sem_inc(vector_done, 1)
            def chain(name, h):
                dve.wait_ge(vector_done, V.after(name, h))

            dve.sem_inc(bound_done, 1)
            nc.vector.memset(ln_c[:, 0:1], CUT * UP).then_inc(const_set, 1)
            dve.wait_ge(small_in, 16)
            nc.vector.tensor_tensor(shifted[:, :], logits[:, :], logits[:, :], ALU.subtract).then_inc(bound_done, 1)
            dve.wait_ge(bound_exp_done, 1)
            nc.vector.reciprocal(gamma_of[:, 1, :], gamma_of[:, 0, :]).then_inc(bound_done, 1)
            dve.wait_ge(bound_done, L.after("recip"))
            nc.vector.tensor_tensor(shifted[:, :], gamma_of[:, 0, :], gamma_of[:, 1, :], ALU.mult).then_inc(bound_done, 1)
            dve.wait_ge(bound_done, L.after("gamma"))
            nc.vector.tensor_tensor(lower[:, :], shifted[:, :], shifted[:, :], ALU.subtract).then_inc(bound_done, 1)
            dve.wait_ge(bound_done, L.after("lower"))
            nc.vector.tensor_scalar(upper[:, :], lower[:, :], -1.0, 1.0, ALU.mult, ALU.add).then_inc(bound_done, 1)
            dve.wait_ge(bound_done, L.after("upper"))
            dve.wait_ge(lnc_done, 1)
            with dve.Fori(0, HG_HEADS) as h:
                nc.vector.tensor_copy(lb[:, 0:1], lower[:, bass.ds(h, 1)]).then_inc(vector_done, 1)
                nc.vector.tensor_copy(lb[:, 1:2], upper[:, bass.ds(h, 1)]).then_inc(vector_done, 1)
                dve.wait_ge(taken, AF.after("e1", h))
                nc.vector.tensor_scalar(e1[:, :], e1[:, :], 1.0, None, ALU.add).then_inc(vector_done, 1)
                chain("e1p", h)
                nc.vector.reciprocal(logf[:, :], e1[:, :]).then_inc(vector_done, 1)
                dve.wait_ge(taken, AF.after("e2", h))
                nc.vector.tensor_scalar(e2[:, :], e2[:, :], 1.0, None, ALU.add).then_inc(vector_done, 1)
                chain("e2p", h)
                nc.vector.reciprocal(key[:, :], e2[:, :]).then_inc(vector_done, 1)
                chain("one_minus_lb", h)
                nc.vector.tensor_scalar(logf[:, :], logf[:, :], lb[:, 1:2], lb[:, 0:1], ALU.mult, ALU.add).then_inc(vector_done, 1)
                chain("key", h)
                nc.vector.tensor_scalar(key[:, :], key[:, :], lb[:, 1:2], None, ALU.mult).then_inc(vector_done, 1)
                chain("f_lb", h)
                nc.vector.tensor_scalar(e1[:, :], logf[:, :], CUT, None, ALU.max).then_inc(vector_done, 1)
                nc.vector.tensor_scalar(e2[:, :], logf[:, :], 1e-30, CUT, ALU.max, ALU.min).then_inc(vector_done, 1)
                dve.wait_ge(scalar_done, A.after("ln_lo", h))
                nc.vector.scalar_tensor_tensor(logf[:, :], e2[:, :], ln_c[:, 1:2], e1[:, :], ALU.subtract, ALU.add).then_inc(vector_done, 1)
                chain("logf", h)
                nc.vector.tensor_tensor_scan(flat(b[:, :, :]), core.consts[:, C_RESET:C_RESET + T], logf[:, :], 0.0,
                                             ALU.mult, ALU.add).then_inc(vector_done, 1)
                dve.wait_ge(taken, AF.after("q_raw", h))
                nc.vector.tensor_scalar(eq[:, :], eq[:, :], 1.0, None, ALU.add).then_inc(vector_done, 1)
                chain("qp", h)
                nc.vector.reciprocal(q[:, :], eq[:, :]).then_inc(vector_done, 1)
                chain("qr", h)
                nc.vector.scalar_tensor_tensor(q[:, :], q_raw[:, :], HG_DIM ** -0.5, q[:, :], ALU.mult, ALU.mult).then_inc(vector_done, 1)
                chain("b", h)
                nc.vector.tensor_tensor(kd[:, :, :], b[:, :, P - 1:P].broadcast_to([P, TB, P]), b[:, :, :], ALU.subtract).then_inc(vector_done, 1)
                dve.wait_ge(scalar_done, A.after("kd_exp", h))
                nc.vector.tensor_tensor(flat(kd[:, :, :]), flat(kd[:, :, :]), key[:, :], ALU.mult).then_inc(vector_done, 1)
                chain("q", h)
                nc.vector.tensor_tensor(flat(qd[:, :, :]), flat(qd[:, :, :]), q[:, :], ALU.mult).then_inc(vector_done, 1)
                def diff(n):
                    m = LEVELS[n]
                    xv = x[:, n % XR, :].rearrange("p (b s) -> p b s", s=2 * m)
                    bv = flat(b[:, :, :]).rearrange("p (b s) -> p b s", s=2 * m)
                    nc.vector.tensor_tensor(xv, bv, bv[:, :, m - 1:m].broadcast_to([P, T // (2 * m), 2 * m]), ALU.subtract).then_inc(vector_done, 1)

                def decayed(n):
                    m = LEVELS[n]
                    xs = x[:, n % XR, :].rearrange("p (b s m) -> p b s m", s=2, m=m)
                    ks = key[:, :].rearrange("p (b s m) -> p b s m", s=2, m=m)
                    qs = q[:, :].rearrange("p (b s m) -> p b s m", s=2, m=m)
                    dve.wait_ge(scalar_done, A.after(("decay_left", n), h))
                    nc.vector.tensor_tensor(xs[:, :, 0, :], xs[:, :, 0, :], ks[:, :, 0, :], ALU.mult).then_inc(vector_done, 1)
                    dve.wait_ge(scalar_done, A.after(("decay_right", n), h))
                    nc.vector.tensor_tensor(xs[:, :, 1, :], xs[:, :, 1, :], qs[:, :, 1, :], ALU.mult).then_inc(vector_done, 1)

                diff(0)
                diff(1)
                dve.wait_ge(scalar_done, A.after("eg", h))
                nc.vector.tensor_scalar(logf[:, :], flat(gate[:, :, :]), 1.0, None, ALU.add).then_inc(vector_done, 1)
                chain("gp", h)
                nc.vector.reciprocal(e2[:, :], logf[:, :]).then_inc(vector_done, 1)
                chain("gr", h)
                nc.vector.tensor_tensor(flat(gate[:, :, :]), flat(big[3][:, :, :]), e2[:, :], ALU.mult).then_inc(vector_done, 1)
                dve.wait_ge(tensor_done, E.after("same", h))
                nc.vector.tensor_tensor(scores[:, :, :], big[0][:, :, :].rearrange("p a (b t) -> p (a b) t", t=P),
                                        bc(core.level_mask(NL), 1, [P, TB, P]), ALU.mult).then_inc(vector_done, 1)
                decayed(0)
                for n in range(NL):
                    if n + 1 < NL:
                        decayed(n + 1)
                    if n + 2 < NL:
                        diff(n + 2)
                    dve.wait_ge(tensor_done, E.after(("level", n), h))
                    if n >= 2:
                        dve.wait_ge(pool_done, G.after(("sum", n - 2), h))
                    nc.vector.tensor_tensor(masked[:, n % 2, :].rearrange("p (b t) -> p b t", t=P),
                                            big[(n + 1) % 2][:, :, :].rearrange("p a (b t) -> p (a b) t", t=P),
                                            bc(core.level_mask(n), 1, [P, TB, P]), ALU.mult).then_inc(vector_done, 1)
                dve.wait_ge(tensor_done, E.after("dstate", h))
                dve.wait_ge(scalar_done, A.after("chunk_decay", h))
                for c in range(1, TB):
                    own = big[3][:, (c - 1) // 4, ((c - 1) % 4) * P:((c - 1) % 4 + 1) * P]
                    if c == 1:
                        nc.vector.tensor_copy(state[:, c, :], own).then_inc(vector_done, 1)
                    else:
                        chain(("state", c - 1), h)
                        nc.vector.scalar_tensor_tensor(state[:, c, :], state[:, c - 1, :], ebl[:, c - 1:c], own, ALU.mult, ALU.add).then_inc(vector_done, 1)
                dve.wait_ge(scalar_done, A.after("square", h))
                nc.vector.tensor_reduce(ss[:, 0:TB], logf[:, :].rearrange("p (b d) -> p b d", d=P), AXX, ALU.add).then_inc(vector_done, 1)
                dve.wait_ge(scalar_done, A.after("std", h))
                nc.vector.reciprocal(ss[:, 2 * TB:3 * TB], ss[:, TB:2 * TB]).then_inc(vector_done, 1)
                chain("rstd", h)
                nc.vector.tensor_tensor(y[:, :, :], big[0][:, :, :].rearrange("p a (b t) -> p (a b) t", t=P),
                                        bc(ss[:, 2 * TB:3 * TB], 2, [P, TB, P]), ALU.mult).then_inc(vector_done, 1)
                chain("y_rstd", h)
                nc.vector.tensor_tensor(y[:, :, :], y[:, :, :], gate[:, :, :], ALU.mult).then_inc(vector_done, 1)

        @block.gpsimd
        def _(pool):
            pool.sem_inc(pool_done, 1)
            with pool.Fori(0, HG_HEADS) as h:
                for n in range(NL):
                    if n:
                        pool.wait_ge(pool_done, G.after(("sum", n - 1), h))
                    pool.wait_ge(vector_done, V.after(("masked", n), h))
                    nc.gpsimd.tensor_tensor(flat(scores[:, :, :]), flat(scores[:, :, :]), masked[:, n % 2, :], ALU.add).then_inc(pool_done, 1)


def ssd(nc, core, w_in, conv_wb, head_rows, norm_w, hT, yssdT):
    HW, XC = SSD_HPG, SSD_GW // P
    GN = SSD_STATE
    NCV = XC + 2
    PAD = SSD_CONV - 1
    with ExitStack() as ctx:
        sb, ps, sem = stage_tools(nc, ctx, "ssd")
        wx = sb("wx", [P, KC, SSD_GW])
        wz = sb("wz", [P, KC, SSD_GW])
        wbc = sb("wbc", [P, 2, KC, GN])
        wdt = sb("wdt", [P, KC, HW])
        cw = sb("conv_w", [P, NCV, SSD_CONV + 1])
        cw_all = sb("conv_w_all", [P, SSD_GROUPS, NCV, SSD_CONV + 1])
        rows = sb("rows", [P, 3, HW])
        rows_all = sb("rows_all", [P, 3, SSD_HEADS])
        nw = sb("norm_w", [P, SSD_GROUPS * XC])
        raw = sb("raw", [P, NCV, T + PAD])
        conv = sb("conv", [P, NCV, T])
        sig = sb("sig", [P, NCV, T])
        xs = sb("xs", [P, TB, SSD_GW])
        xdt = sig[:, 0:XC, :].rearrange("p u (b h d) -> p (u b) h d", h=HW, d=SSD_DIM)
        xdd = sig[:, XC:NCV, :].rearrange("p u (b h d) -> p (u b) h d", h=HW, d=SSD_DIM)
        bn = sb("bn", [P, TB, GN])
        z = sb("z", [P, TB, SSD_GW])
        y = sb("y", [P, TB, HW, SSD_DIM])
        dt = sb("dt", [P, 3, TB, HW])
        a = sb("a", [P, TB, HW])
        decay = sb("decay", [P, 3, TB, HW])
        rate = sb("rate", [P, HW])
        seg = sb("seg", [P, 2, HW, P])
        cbm = sb("cbm", [P, TB, P])
        sc = sb("sc", [P, 2, HW, P])
        state = sb("state", [GN, TB, SSD_GW])
        ss = sb("ss", [P, 3, TB])
        bank = [ps(f"bank{i}", [P, HALF]) for i in range(8)]
        w_sem = {n: sem(f"w{n}_in") for n in ("x", "bc", "z", "dt")}
        rows_in = sem("rows_in")
        tensor_done, scalar_done, vector_done = sem("tensor_done"), sem("scalar_done"), sem("vector_done")
        pads_set = sem("pads_set")

        SMALL = 16 * (3 * SSD_GROUPS + 2)
        halves = [(u, half) for u in range(NCV) for half in range(2)]
        E = Steps(*[("in", u) for u in halves], "dt", *[("z", i) for i in range(4)], "sums",
                  *[("xs", i) for i in range(4)], "cb0", "cb1", "bn",
                  *[("own", i) for i in range(4)],
                  ("seg", 0), *[s for c in range(1, TB) for s in (("seg", c), ("y", c - 1))], ("y", TB - 1), *[("yT", i) for i in range(XC)])
        V = Steps("taps_x", "taps_bc", "rows", *[s for u in range(NCV) for s in [("tap", u, j) for j in range(SSD_CONV)]],
                  "dt_raw", "dt", "a",
                  *[s for u in range(NCV) for s in (("sp", u), ("sr", u), ("silu", u))],
                  "zp0", "zp1", "zp2", "zp3", "zr", "z0", "z1", "z2", "z3",
                  "cbm0", "cbm1", "xdt", "xdd",
                  *[s for c in range(1, TB) for s in (("state_decay", c), ("state", c))][1:],
                  *[("tri", 0, h) for h in range(HW)],
                  *[s for c in range(TB) for s in [("tri", c + 1, h) for h in range(HW) if c + 1 < TB] + [("sc", c)]
                    + [("y_off", c)] * (c > 0) + [("y", c)]],
                  "skip", "y_skip", "gated", "square", "ss", "rstd", "y_norm")
        A = Steps(*[("in", u) for u in halves], "rate", "dt_abs", "dt_exp", "dt_ln", *[("z", i) for i in range(4)],
                  "decay", *[("conv_exp", u) for u in range(NCV)],
                  *[("xs", i) for i in range(4)], "bn",
                  *[("seg", c) for c in range(TB)], "std", *[("yT", i) for i in range(XC)])
        block = ctx.enter_context(nc.Block())
        wv_ = kc_view(w_in)

        @block.sync
        def _(sp):
            for g in range(SSD_GROUPS):
                sp.dma_start(cw_all[:, g, 0:XC, :], conv_wb[g * SSD_GW:(g + 1) * SSD_GW, :].rearrange("(u p) j -> p u j", p=P)).then_inc(rows_in, 16)
                for n in range(2):
                    row = SSD_W + (n * SSD_GROUPS + g) * GN
                    sp.dma_start(cw_all[0:GN, g, XC + n, :], conv_wb[row:row + GN, :]).then_inc(rows_in, 16)
            sp.dma_start(rows_all[:, :, :], head_rows.broadcast_to([P, 3, SSD_HEADS])).then_inc(rows_in, 16)
            sp.dma_start(nw[:, :], norm_w).then_inc(rows_in, 16)
            def load(g):
                sp.dma_start(wx[:, :, :], wv_[:, :, bass.ds(g * SSD_GW + COL_X, SSD_GW)]).then_inc(w_sem["x"], 16)
                for n, col in enumerate((COL_B, COL_C)):
                    sp.dma_start(wbc[:, n, :, :], wv_[:, :, bass.ds(g * GN + col, GN)]).then_inc(w_sem["bc"], 16)
                sp.dma_start(wz[:, :, :], wv_[:, :, bass.ds(g * SSD_GW + COL_Z, SSD_GW)]).then_inc(w_sem["z"], 16)
                sp.dma_start(wdt[:, :, :], wv_[:, :, bass.ds(g * HW + COL_DT, HW)]).then_inc(w_sem["dt"], 16)

            load(0)
            with sp.Fori(1, SSD_GROUPS) as g:
                sp.wait_ge(tensor_done, E.after(("z", 3), g - 1))
                load(g)

        @block.tensor
        def _(pe):
            pe.sem_inc(tensor_done, 1)
            with pe.Fori(0, SSD_GROUPS) as g:
                pe.wait_ge(scalar_done, A.passes(g))
                pe.wait_ge(vector_done, V.passes(g))
                for n, (u, half) in enumerate(halves):
                    m = P if u < XC else GN
                    if half == 0:
                        pe.wait_ge(w_sem["x" if u < XC else "bc"], g * 16 + 16 if u < XC else g * 32 + 32)
                    for k in range(KC):
                        w = wx[:, k, u * P:(u + 1) * P] if u < XC else wbc[:, u - XC, k, :]
                        last = nc.tensor.matmul(bank[n][0:m, :], w, hT[:, k, half * HALF:(half + 1) * HALF], start=k == 0, stop=k == KC - 1)
                    last.then_inc(tensor_done, 1)
                pe.wait_ge(w_sem["dt"], g * 16 + 16)
                pe.wait_ge(scalar_done, A.after(("in", halves[0]), g))
                for tb in range(TB):
                    for k in range(KC):
                        last = nc.tensor.matmul(bank[0][:, tb * HW:(tb + 1) * HW], hT[:, k, tb * P:(tb + 1) * P], wdt[:, k, :],
                                                start=k == 0, stop=k == KC - 1)
                last.then_inc(tensor_done, 1)
                pe.wait_ge(w_sem["z"], g * 16 + 16)
                for i in range(4):
                    pe.wait_ge(scalar_done, A.after(("in", halves[1 + i]), g))
                    for tb in (2 * i, 2 * i + 1):
                        for k in range(KC):
                            last = nc.tensor.matmul(bank[1 + i][:, (tb % 2) * SSD_GW:(tb % 2 + 1) * SSD_GW], hT[:, k, tb * P:(tb + 1) * P],
                                                    wz[:, k, :], start=k == 0, stop=k == KC - 1)
                    last.then_inc(tensor_done, 1)
                pe.wait_ge(vector_done, V.after("a", g))
                pe.wait_ge(scalar_done, A.after(("in", halves[7]), g))
                for n, tri in enumerate(("upto", "beyond", "ones")):
                    last = nc.tensor.matmul(bank[5][:, n * TB * HW:(n + 1) * TB * HW], core.const(tri),
                                            a[:, :, :].rearrange("p b h -> p (b h)"), start=True, stop=True)
                last.then_inc(tensor_done, 1)
                for i in range(4):
                    if i == 0:
                        pe.wait_ge(vector_done, V.after(("silu", XC - 1), g))
                    if i >= 2:
                        pe.wait_ge(scalar_done, A.after(("xs", i - 2), g))
                    for tb in (2 * i, 2 * i + 1):
                        for u in range(XC):
                            at = (tb % 2) * SSD_GW + u * P
                            last = nc.tensor.transpose(bank[6 + i % 2][:, at:at + P], conv[:, u, tb * P:(tb + 1) * P], core.const("ident"))
                    last.then_inc(tensor_done, 1)
                pe.wait_ge(vector_done, V.after(("silu", XC + 1), g))
                pe.wait_ge(vector_done, V.after("dt", g))
                for i in range(2):
                    pe.wait_ge(scalar_done, A.after(("xs", 2 + i), g))
                    for c in range(4 * i, 4 * i + 4):
                        last = nc.tensor.matmul(bank[6 + i][:, (c % 4) * P:(c % 4 + 1) * P], conv[0:GN, XC, c * P:(c + 1) * P],
                                                conv[0:GN, XC + 1, c * P:(c + 1) * P], start=True, stop=True)
                    last.then_inc(tensor_done, 1)
                for tb in range(TB):
                    last = nc.tensor.transpose(bank[0][:, tb * GN:(tb + 1) * GN], conv[0:GN, XC, tb * P:(tb + 1) * P], core.const("ident")[0:GN, 0:GN])
                last.then_inc(tensor_done, 1)
                pe.wait_ge(vector_done, V.after("xdd", g))
                pe.wait_ge(scalar_done, A.after("bn", g))
                for i in range(4):
                    for c in (2 * i, 2 * i + 1):
                        last = nc.tensor.matmul(bank[1 + i][0:GN, (c % 2) * SSD_GW:(c % 2 + 1) * SSD_GW], bn[:, c, :],
                                                xdd[:, c, :, :].rearrange("p h d -> p (h d)"), start=True, stop=True)
                    last.then_inc(tensor_done, 1)
                for c in range(TB + 1):
                    if c < TB:
                        if c >= 2:
                            pe.wait_ge(scalar_done, A.after(("seg", c - 2), g))
                        if c == 0:
                            pe.wait_ge(scalar_done, A.after("decay", g))
                        pe.wait_ge(vector_done, V.after(("tri", c, HW - 1), g))
                        for h in range(HW):
                            last = nc.tensor.matmul(bank[(0, 5)[c % 2]][:, h * P:(h + 1) * P], seg[:, c % 2, h, :], core.const("upto"), start=True, stop=True)
                        last.then_inc(tensor_done, 1)
                    if c >= 1:
                        r = c - 1
                        pe.wait_ge(vector_done, V.after(("sc", r), g))
                        if r >= 2:
                            pe.wait_ge(vector_done, V.after(("y", r - 2), g))
                        yb = bank[6 + r % 2]
                        for h in range(HW):
                            last = nc.tensor.matmul(yb[:, h * SSD_DIM:(h + 1) * SSD_DIM], sc[:, r % 2, h, :], xdt[:, r, h, :], start=True, stop=True)
                        if r >= 1:
                            last = nc.tensor.matmul(yb[:, SSD_GW:2 * SSD_GW], conv[0:GN, XC + 1, r * P:(r + 1) * P], state[:, r, :], start=True, stop=True)
                        last.then_inc(tensor_done, 1)
                pe.wait_ge(vector_done, V.after("y_norm", g))
                for u in range(XC):
                    for tb in range(TB):
                        last = nc.tensor.transpose(bank[1 + 2 * u + tb // 4][:, (tb % 4) * P:(tb % 4 + 1) * P],
                                                   y[:, tb, 2 * u:2 * u + 2, :].rearrange("p h d -> p (h d)"), core.const("ident"))
                    last.then_inc(tensor_done, 1)

        @block.scalar
        def _(act):
            act.sem_inc(scalar_done, 1)
            nc.scalar.preload_act_table_set(LOG_EXP)
            act.wait_ge(pads_set, 1)
            act.wait_ge(rows_in, SMALL)
            with act.Fori(0, SSD_GROUPS) as g:
                for n, (u, half) in enumerate(halves):
                    m = P if u < XC else GN
                    act.wait_ge(tensor_done, E.after(("in", (u, half)), g))
                    nc.scalar.copy(raw[0:m, u, PAD + half * HALF:PAD + (half + 1) * HALF], bank[n][0:m, :]).then_inc(scalar_done, 1)
                act.wait_ge(vector_done, V.after("rows", g))
                nc.scalar.activation(rate[:, :], rows[:, 1, :], ACT.Exp).then_inc(scalar_done, 1)
                act.wait_ge(vector_done, V.after("dt_raw", g))
                nc.scalar.activation(dt[:, 1, :, :], dt[:, 0, :, :], ACT.Abs).then_inc(scalar_done, 1)
                act.wait_ge(scalar_done, A.after("dt_abs", g))
                nc.scalar.activation(dt[:, 1, :, :], dt[:, 1, :, :], ACT.Exp, scale=-1.0).then_inc(scalar_done, 1)
                act.wait_ge(scalar_done, A.after("dt_exp", g))
                nc.scalar.activation(dt[:, 1, :, :], dt[:, 1, :, :], ACT.Ln, bias=1.0).then_inc(scalar_done, 1)
                for i in range(4):
                    act.wait_ge(tensor_done, E.after(("z", i), g))
                    nc.scalar.activation(z[:, 2 * i:2 * i + 2, :].rearrange("p b d -> p (b d)"), bank[1 + i][:, :], ACT.Exp, scale=-1.0).then_inc(scalar_done, 1)
                act.wait_ge(tensor_done, E.after("sums", g))
                nc.scalar.activation(decay[:, :, :, :].rearrange("p s b h -> p (s b h)"), bank[5][:, 0:3 * TB * HW], ACT.Exp).then_inc(scalar_done, 1)
                for u in range(NCV):
                    m = P if u < XC else GN
                    act.wait_ge(vector_done, V.after(("tap", u, SSD_CONV - 1), g))
                    nc.scalar.activation(sig[0:m, u, :], conv[0:m, u, :], ACT.Exp, scale=-1.0).then_inc(scalar_done, 1)
                for i in range(4):
                    act.wait_ge(tensor_done, E.after(("xs", i), g))
                    nc.scalar.copy(xs[:, 2 * i:2 * i + 2, :].rearrange("p b d -> p (b d)"), bank[6 + i % 2][:, :]).then_inc(scalar_done, 1)
                act.wait_ge(tensor_done, E.after("bn", g))
                nc.scalar.copy(bn[:, :, :].rearrange("p b n -> p (b n)"), bank[0][:, :]).then_inc(scalar_done, 1)
                for c in range(TB):
                    act.wait_ge(tensor_done, E.after(("seg", c), g))
                    if c >= 2:
                        act.wait_ge(tensor_done, E.after(("y", c - 2), g))
                    nc.scalar.activation(sc[:, c % 2, :, :].rearrange("p h t -> p (h t)"), bank[(0, 5)[c % 2]][:, :], ACT.Exp).then_inc(scalar_done, 1)
                act.wait_ge(vector_done, V.after("ss", g))
                nc.scalar.activation(ss[:, 1, :], ss[:, 0, :], ACT.Sqrt, scale=1.0 / SSD_GW, bias=core.eps[:, :]).then_inc(scalar_done, 1)
                for u in range(XC):
                    act.wait_ge(tensor_done, E.after(("yT", u), g))
                    for half in range(2):
                        last = nc.scalar.activation(yssdT[:, bass.ds(g * XC + u, 1), half * HALF:(half + 1) * HALF].rearrange("p c t -> p (c t)"),
                                                    bank[1 + 2 * u + half][:, :], ACT.Copy, scale=nw[:, bass.ds(g * XC + u, 1)])
                    last.then_inc(scalar_done, 1)

        @block.vector
        def _(dve):
            dve.sem_inc(vector_done, 1)
            nc.vector.memset(raw[:, :, 0:PAD], 0.0).then_inc(pads_set, 1)
            dve.wait_ge(rows_in, SMALL)
            with dve.Fori(0, SSD_GROUPS) as g:
                def chain(name):
                    dve.wait_ge(vector_done, V.after(name, g))

                nc.vector.tensor_copy(cw[:, 0:XC, :], cw_all[:, bass.ds(g, 1), 0:XC, :].rearrange("p g u j -> p (g u) j")).then_inc(vector_done, 1)
                nc.vector.tensor_copy(cw[0:GN, XC:NCV, :], cw_all[0:GN, bass.ds(g, 1), XC:NCV, :].rearrange("p g u j -> p (g u) j")).then_inc(vector_done, 1)
                nc.vector.tensor_copy(rows[:, :, :], rows_all[:, :, bass.ds(g * HW, HW)]).then_inc(vector_done, 1)
                chain("rows")
                for u in range(NCV):
                    m = P if u < XC else GN
                    dve.wait_ge(scalar_done, A.after(("in", (u, 1)), g))
                    for j in range(SSD_CONV):
                        if j == 0:
                            nc.vector.tensor_scalar(conv[0:m, u, :], raw[0:m, u, 0:T], cw[0:m, u, 0:1], cw[0:m, u, SSD_CONV:SSD_CONV + 1],
                                                    ALU.mult, ALU.add).then_inc(vector_done, 1)
                        else:
                            chain(("tap", u, j - 1))
                            nc.vector.scalar_tensor_tensor(conv[0:m, u, :], raw[0:m, u, j:j + T], cw[0:m, u, j:j + 1], conv[0:m, u, :],
                                                           ALU.mult, ALU.add).then_inc(vector_done, 1)
                dve.wait_ge(tensor_done, E.after("dt", g))
                nc.vector.tensor_tensor(dt[:, 0, :, :], bank[0][:, 0:TB * HW].rearrange("p (b h) -> p b h", h=HW),
                                        bc(rows[:, 0, :], 1, [P, TB, HW]), ALU.add).then_inc(vector_done, 1)
                dve.wait_ge(scalar_done, A.after("dt_ln", g))
                nc.vector.scalar_tensor_tensor(dt[:, 2, :, :], dt[:, 0, :, :], 0.0, dt[:, 1, :, :], ALU.max, ALU.add).then_inc(vector_done, 1)
                chain("dt")
                nc.vector.scalar_tensor_tensor(a[:, :, :], dt[:, 2, :, :], -1.0, bc(rate[:, :], 1, [P, TB, HW]), ALU.mult, ALU.mult).then_inc(vector_done, 1)
                for u in range(NCV):
                    m = P if u < XC else GN
                    dve.wait_ge(scalar_done, A.after(("conv_exp", u), g))
                    nc.vector.tensor_scalar(sig[0:m, u, :], sig[0:m, u, :], 1.0, None, ALU.add).then_inc(vector_done, 1)
                    chain(("sp", u))
                    nc.vector.reciprocal(sig[0:m, u, :], sig[0:m, u, :]).then_inc(vector_done, 1)
                    chain(("sr", u))
                    nc.vector.tensor_tensor(conv[0:m, u, :], conv[0:m, u, :], sig[0:m, u, :], ALU.mult).then_inc(vector_done, 1)
                zf = z[:, :, :].rearrange("p (i b) d -> p i (b d)", b=2)
                for i in range(4):
                    dve.wait_ge(scalar_done, A.after(("z", i), g))
                    nc.vector.tensor_scalar(zf[:, i, :], zf[:, i, :], 1.0, None, ALU.add).then_inc(vector_done, 1)
                chain("zp3")
                nc.vector.reciprocal(z[:, :, :], z[:, :, :]).then_inc(vector_done, 1)
                chain("zr")
                for i in range(4):
                    nc.vector.tensor_tensor(zf[:, i, :], zf[:, i, :], bank[1 + i][:, :], ALU.mult).then_inc(vector_done, 1)
                for i in range(2):
                    dve.wait_ge(tensor_done, E.after(f"cb{i}", g))
                    nc.vector.tensor_tensor(cbm[:, 4 * i:4 * i + 4, :], bank[6 + i][:, :].rearrange("p (c t) -> p c t", t=P),
                                            bc(core.const("upto"), 1, [P, 4, P]), ALU.mult).then_inc(vector_done, 1)
                dve.wait_ge(scalar_done, A.after(("xs", 3), g))
                nc.vector.tensor_tensor(xdt[:, :, :, :].rearrange("p b h d -> p (b h) d"), xs[:, :, :].rearrange("p b (h d) -> p (b h) d", d=SSD_DIM),
                                        bc(dt[:, 2, :, :].rearrange("p b h -> p (b h)"), 2, [P, TB * HW, SSD_DIM]), ALU.mult).then_inc(vector_done, 1)
                chain("xdt")
                nc.vector.tensor_tensor(xdd[:, :, :, :].rearrange("p b h d -> p (b h) d"), xdt[:, :, :, :].rearrange("p b h d -> p (b h) d"),
                                        bc(decay[:, 1, :, :].rearrange("p b h -> p (b h)"), 2, [P, TB * HW, SSD_DIM]), ALU.mult).then_inc(vector_done, 1)
                for c in range(1, TB):
                    own = bank[1 + (c - 1) // 2][0:GN, ((c - 1) % 2) * SSD_GW:((c - 1) % 2 + 1) * SSD_GW]
                    dve.wait_ge(tensor_done, E.after(("own", (c - 1) // 2), g))
                    if c == 1:
                        nc.vector.tensor_copy(state[:, c, :], own).then_inc(vector_done, 1)
                    else:
                        chain(("state", c - 1))
                        nc.vector.tensor_tensor(state[:, c, :].rearrange("p (h d) -> p h d", d=SSD_DIM),
                                                state[:, c - 1, :].rearrange("p (h d) -> p h d", d=SSD_DIM),
                                                bc(decay[0:GN, 2, c - 1, :], 2, [GN, HW, SSD_DIM]), ALU.mult).then_inc(vector_done, 1)
                        chain(("state_decay", c))
                        nc.vector.tensor_tensor(state[:, c, :], state[:, c, :], own, ALU.add).then_inc(vector_done, 1)
                def below_diagonal(c):
                    if c >= 2:
                        dve.wait_ge(tensor_done, E.after(("seg", c - 2), g))
                    for h in range(HW):
                        nc.vector.tensor_scalar(seg[:, c % 2, h, :], core.const("beyond"), a[:, c, h:h + 1], None, ALU.mult).then_inc(vector_done, 1)

                below_diagonal(0)
                for c in range(TB):
                    if c + 1 < TB:
                        below_diagonal(c + 1)
                    dve.wait_ge(scalar_done, A.after(("seg", c), g))
                    nc.vector.tensor_tensor(sc[:, c % 2, :, :], sc[:, c % 2, :, :], bc(cbm[:, c, :], 1, [P, HW, P]), ALU.mult).then_inc(vector_done, 1)
                    dve.wait_ge(tensor_done, E.after(("y", c), g))
                    yb = bank[6 + c % 2]
                    if c:
                        nc.vector.tensor_tensor(y[:, c, :, :], yb[:, SSD_GW:2 * SSD_GW].rearrange("p (h d) -> p h d", d=SSD_DIM),
                                                bc(decay[:, 0, c, :], 2, [P, HW, SSD_DIM]), ALU.mult).then_inc(vector_done, 1)
                        chain(("y_off", c))
                        nc.vector.tensor_tensor(y[:, c, :, :], y[:, c, :, :], yb[:, 0:SSD_GW].rearrange("p (h d) -> p h d", d=SSD_DIM), ALU.add).then_inc(vector_done, 1)
                    else:
                        nc.vector.tensor_copy(y[:, c, :, :], yb[:, 0:SSD_GW].rearrange("p (h d) -> p h d", d=SSD_DIM)).then_inc(vector_done, 1)
                nc.vector.tensor_tensor(xdd[:, :, :, :], xs[:, :, :].rearrange("p b (h d) -> p b h d", d=SSD_DIM),
                                        rows[:, 2, :].unsqueeze(1).unsqueeze(3).broadcast_to([P, TB, HW, SSD_DIM]), ALU.mult).then_inc(vector_done, 1)
                chain("skip")
                nc.vector.tensor_tensor(y[:, :, :, :], y[:, :, :, :], xdd[:, :, :, :], ALU.add).then_inc(vector_done, 1)
                yf = y[:, :, :, :].rearrange("p b h d -> p b (h d)")
                chain("y_skip")
                nc.vector.tensor_tensor(yf, yf, z[:, :, :], ALU.mult).then_inc(vector_done, 1)
                chain("gated")
                nc.vector.tensor_tensor(xdd[:, :, :, :].rearrange("p b h d -> p b (h d)"), yf, yf, ALU.mult).then_inc(vector_done, 1)
                chain("square")
                nc.vector.tensor_reduce(ss[:, 0, :], xdd[:, :, :, :].rearrange("p b h d -> p b (h d)"), AXX, ALU.add).then_inc(vector_done, 1)
                dve.wait_ge(scalar_done, A.after("std", g))
                nc.vector.reciprocal(ss[:, 2, :], ss[:, 1, :]).then_inc(vector_done, 1)
                chain("rstd")
                nc.vector.tensor_tensor(yf, yf, bc(ss[:, 2, :], 2, [P, TB, SSD_GW]), ALU.mult).then_inc(vector_done, 1)


def merge(nc, core, w_in, branch_w, hT, yT, mergedT):
    NB, YC = 3, 4
    with ExitStack() as ctx:
        sb, ps, sem = stage_tools(nc, ctx, "mg")
        wg = sb("wg", [P, 2, NB, KC, P])
        wb = sb("wb", [P, 2, NB, YC, P])
        RING = 4
        sig = sb("sig", [P, RING, HALF])
        part = sb("part", [P, 2, HALF])
        pg = [ps(f"pg{i}", [P, HALF]) for i in range(RING)]
        pb = [ps(f"pb{i}", [P, HALF]) for i in range(RING)]
        w_sem = [sem(f"w{j}_in") for j in range(2)]
        tensor_done, scalar_done, vector_done = sem("tensor_done"), sem("scalar_done"), sem("vector_done")
        units = [(j, half, n) for j in range(2) for half in range(2) for n in range(NB)]
        E = Steps(*[(s, u) for u in units for s in ("gate", "branch")])
        A = Steps(*units)
        V = Steps(*[(s, u) for u in units for s in ("plus", "recip", "product") + ("sum",) * (u[2] > 0)])
        LOADS = 16 * 2 * NB
        block = ctx.enter_context(nc.Block())
        wv_ = kc_view(w_in)
        wbv = branch_w.rearrange("n (k p) c -> n p k c", p=P)

        @block.sync
        def _(sp):
            with sp.Fori(0, KC // 2) as i:
                for j in range(2):
                    sp.wait_ge(tensor_done, E.passes(i))
                    for n in range(NB):
                        sp.dma_start(wg[:, j, n, :, :], wv_[:, :, bass.ds(i * 2 * P + (COL_G + n * D + j * P), P)]).then_inc(w_sem[j], 16)
                        sp.dma_start(wb[:, j, n, :, :], wbv[n, :, :, bass.ds(i * 2 * P + j * P, P)]).then_inc(w_sem[j], 16)

        @block.tensor
        def _(pe):
            pe.sem_inc(tensor_done, 1)
            with pe.Fori(0, KC // 2) as i:
                for x, (j, half, n) in enumerate(units):
                    ts = slice(half * HALF, (half + 1) * HALF)
                    r = x % RING
                    if half == 0 and n == 0:
                        pe.wait_ge(w_sem[j], i * LOADS + LOADS)
                    pe.wait_ge(vector_done, V.after(("product", units[x - RING]), i) if x >= RING else V.passes(i))
                    for k in range(KC):
                        last = nc.tensor.matmul(pg[r][:, :], wg[:, j, n, k, :], hT[:, k, ts], start=k == 0, stop=k == KC - 1)
                    last.then_inc(tensor_done, 1)
                    for k in range(YC):
                        last = nc.tensor.matmul(pb[r][:, :], wb[:, j, n, k, :], yT[n][:, k, ts], start=k == 0, stop=k == YC - 1)
                    last.then_inc(tensor_done, 1)

        @block.scalar
        def _(act):
            act.sem_inc(scalar_done, 1)
            with act.Fori(0, KC // 2) as i:
                for x, u in enumerate(units):
                    act.wait_ge(tensor_done, E.after(("gate", u), i))
                    act.wait_ge(vector_done, V.after(("product", units[x - RING]), i) if x >= RING else V.passes(i))
                    nc.scalar.activation(sig[:, x % RING, :], pg[x % RING][:, :], ACT.Exp, scale=-1.0).then_inc(scalar_done, 1)

        @block.vector
        def _(dve):
            dve.sem_inc(vector_done, 1)
            with dve.Fori(0, KC // 2) as i:
                for x, u in enumerate(units):
                    j, half, n = u
                    r = x % RING
                    dve.wait_ge(scalar_done, A.after(u, i))
                    nc.vector.tensor_scalar(sig[:, r, :], sig[:, r, :], 1.0, None, ALU.add).then_inc(vector_done, 1)
                    dve.wait_ge(vector_done, V.after(("plus", u), i))
                    nc.vector.reciprocal(sig[:, r, :], sig[:, r, :]).then_inc(vector_done, 1)
                    dve.wait_ge(vector_done, V.after(("recip", u), i))
                    dve.wait_ge(tensor_done, E.after(("branch", u), i))
                    out = mergedT[:, bass.ds(i * 2 + j, 1), half * HALF:(half + 1) * HALF].rearrange("p c t -> p (c t)")
                    nc.vector.tensor_tensor(part[:, n % 2, :] if n else out, sig[:, r, :], pb[r][:, :], ALU.mult).then_inc(vector_done, 1)
                    if n:
                        dve.wait_ge(vector_done, V.after(("product", u), i))
                        nc.vector.tensor_tensor(out, out, part[:, n % 2, :], ALU.add).then_inc(vector_done, 1)


def output_and_norm(nc, core, x, w_out, norm_w, mergedT, acc, h2T):
    with ExitStack() as ctx:
        sb, ps, sem = stage_tools(nc, ctx, "ou")
        wo = sb("w", [P, KC, D])
        xt = sb("x", [P, 2, D])
        squares = sb("squares", [P, D])
        xn = sb("xn", [P, 2, D])
        stat = sb("stat", [P, 2, 3])
        wcol = sb("wcol", [P, KC])
        po = [ps(f"po{i}", [P, 2, HALF]) for i in range(2)]
        turned = [ps(f"turned{i}", [P, KC, P]) for i in range(2)]
        w_sem = [sem(f"w{i}_in") for i in range(2)]
        x_in = [sem(f"x{i}_in") for i in range(2)]
        norm_in = sem("norm_in")
        tensor_done, scalar_done, vector_done = sem("tensor_done"), sem("scalar_done"), sem("vector_done")
        E = Steps(*[s for b in range(TB + 1) for s in [("out", b)] * (b < TB) + [("turned", b - 1)] * (b > 0)])
        A = Steps(*[(s, b) for b in range(TB) for s in ("squares", "std")])
        V = Steps(*[(s, b) for b in range(TB) for s in ("sum", "rstd", "xn", "h0", "h1")])
        block = ctx.enter_context(nc.Block())
        xv = x.rearrange("(b p) d -> p b d", p=P)
        wov = kc_view(w_out)

        @block.sync
        def _(sp):
            sp.dma_start(wcol[:, :], norm_w).then_inc(norm_in, 16)
            for half in range(2):
                sp.dma_start(wo[:, :, half * HALF:(half + 1) * HALF], wov[:, :, half * HALF:(half + 1) * HALF]).then_inc(w_sem[half], 16)
            for b in range(TB):
                if b >= 2:
                    sp.wait_ge(vector_done, V.after(("sum", b - 2)))
                sp.dma_start(xt[:, b % 2, :], xv[:, b, :]).then_inc(x_in[b % 2], 16)

        @block.tensor
        def _(pe):
            pe.sem_inc(tensor_done, 1)
            for b in range(TB + 1):
                if b < TB:
                    if b >= 2:
                        pe.wait_ge(vector_done, V.after(("sum", b - 2)))
                    for half in range(2):
                        if b == 0:
                            pe.wait_ge(w_sem[half], 16)
                        for k in range(KC):
                            last = nc.tensor.matmul(po[b % 2][:, half, :], mergedT[:, k, b * P:(b + 1) * P], wo[:, k, half * HALF:(half + 1) * HALF],
                                                    start=k == 0, stop=k == KC - 1)
                    last.then_inc(tensor_done, 1)
                if b > 0:
                    r = b - 1
                    pe.wait_ge(vector_done, V.after(("xn", r)))
                    if r >= 2:
                        pe.wait_ge(vector_done, V.after(("h1", r - 2)))
                    for k in range(KC):
                        last = nc.tensor.transpose(turned[r % 2][:, k, :], xn[:, r % 2, k * P:(k + 1) * P], core.const("ident"))
                    last.then_inc(tensor_done, 1)

        @block.scalar
        def _(act):
            act.sem_inc(scalar_done, 1)
            for b in range(TB):
                act.wait_ge(vector_done, V.after(("sum", b)))
                nc.scalar.activation(squares[:, :], acc[:, b, :], ACT.Square, accum_out=stat[:, b % 2, 0:1]).then_inc(scalar_done, 1)
                act.wait_ge(scalar_done, A.after(("squares", b)))
                nc.scalar.activation(stat[:, b % 2, 1:2], stat[:, b % 2, 0:1], ACT.Sqrt, scale=1.0 / D, bias=core.eps[:, :]).then_inc(scalar_done, 1)

        @block.vector
        def _(dve):
            dve.sem_inc(vector_done, 1)
            dve.wait_ge(norm_in, 16)
            for b in range(TB):
                dve.wait_ge(x_in[b % 2], 16 * (b // 2 + 1))
                dve.wait_ge(tensor_done, E.after(("out", b)))
                nc.vector.tensor_tensor(acc[:, b, :], xt[:, b % 2, :], po[b % 2][:, :, :].rearrange("p a d -> p (a d)"), ALU.add).then_inc(vector_done, 1)
                dve.wait_ge(scalar_done, A.after(("std", b)))
                nc.vector.reciprocal(stat[:, b % 2, 2:3], stat[:, b % 2, 1:2]).then_inc(vector_done, 1)
                if b >= 2:
                    dve.wait_ge(tensor_done, E.after(("turned", b - 2)))
                dve.wait_ge(vector_done, V.after(("rstd", b)))
                nc.vector.tensor_scalar(xn[:, b % 2, :], acc[:, b, :], stat[:, b % 2, 2:3], None, ALU.mult).then_inc(vector_done, 1)
                dve.wait_ge(tensor_done, E.after(("turned", b)))
                for n in range(2):
                    ks = slice(4 * n, 4 * n + 4)
                    nc.vector.tensor_tensor(h2T[:, ks, b * P:(b + 1) * P], turned[b % 2][:, ks, :], bc(wcol[:, ks], 2, [P, 4, P]), ALU.mult).then_inc(vector_done, 1)


def norm_output(nc, norm_row, acc, out):
    with ExitStack() as ctx:
        sb, ps, sem = stage_tools(nc, ctx, "no")
        wrow = sb("w", [P, D])
        squares = sb("squares", [P, D])
        stat = sb("stat", [P, 3, TB])
        scaled = sb("scaled", [P, 2, D])
        eps = sb("eps", [P, 1])
        eps_set = sem("eps_set")
        w_in_sem = sem("w_in")
        out_sem = [sem(f"out{i}") for i in range(2)]
        scalar_done, vector_done = sem("scalar_done"), sem("vector_done")
        A = Steps(*[(s, b) for b in range(TB) for s in ("squares", "std")])
        V = Steps(*[(s, b) for b in range(TB) for s in ("rstd", "out")])
        block = ctx.enter_context(nc.Block())

        @block.sync
        def _(sp):
            sp.dma_start(wrow[:, :], norm_row.broadcast_to([P, D])).then_inc(w_in_sem, 16)
            for b in range(TB):
                sp.wait_ge(vector_done, V.after(("out", b)))
                sp.dma_start(out[b * P:(b + 1) * P, :], scaled[:, b % 2, :]).then_inc(out_sem[b % 2], 16)
            for i in range(2):
                sp.wait_ge(out_sem[i], 16 * TB // 2)

        @block.scalar
        def _(act):
            act.sem_inc(scalar_done, 1)
            act.wait_ge(eps_set, 1)
            for b in range(TB):
                nc.scalar.activation(squares[:, :], acc[:, b, :], ACT.Square, accum_out=stat[:, 0, b:b + 1]).then_inc(scalar_done, 1)
                act.wait_ge(scalar_done, A.after(("squares", b)))
                nc.scalar.activation(stat[:, 1, b:b + 1], stat[:, 0, b:b + 1], ACT.Sqrt, scale=1.0 / D, bias=eps[:, :]).then_inc(scalar_done, 1)

        @block.vector
        def _(dve):
            dve.sem_inc(vector_done, 1)
            nc.vector.memset(eps[:, :], EPS).then_inc(eps_set, 1)
            dve.wait_ge(w_in_sem, 16)
            for b in range(TB):
                dve.wait_ge(scalar_done, A.after(("std", b)))
                nc.vector.reciprocal(stat[:, 2, b:b + 1], stat[:, 1, b:b + 1]).then_inc(vector_done, 1)
                dve.wait_ge(vector_done, V.after(("rstd", b)))
                if b >= 2:
                    dve.wait_ge(out_sem[b % 2], 16 * (b // 2))
                nc.vector.scalar_tensor_tensor(scaled[:, b % 2, :], acc[:, b, :], stat[:, 2, b:b + 1], wrow[:, :], ALU.mult, ALU.mult).then_inc(vector_done, 1)


def peer_select(nc, core, w_q, keysT, h2T, slot_row, slot_col, slot_gate):
    K = TOPK
    LAST = 7
    LOWEST = -3.0e38
    with ExitStack() as ctx:
        sb, ps, sem = stage_tools(nc, ctx, "se")
        w = sb("w", [P, KC, 2 * P])
        keys = sb("keys", [P, 2, KEYS])
        qT = sb("qT", [P, 2, T])
        s = sb("s", [P, 2, TB, 2, KEYS])
        rest = sb("rest", [P, 3, 2, KEYS])
        pace = sb("pace", [P, 1])
        pool_pace = sb("pool_pace", [P, 1])
        val = sb("val", [P, TB, 2, K])
        idx = sb("idx", [P, TB, 2, K], U32)
        pair = sb("pair", [P, 3, K * K])
        pair_rest = sb("pair_rest", [P, 3, K * K])
        top = sb("top", [P, TB, K])
        pos = sb("pos", [P, TB, K], U32)
        part = sb("part", [P, 2, TB * K], U32)
        partf = sb("partf", [P, 2, TB, K])
        idxf = sb("idxf", [P, TB, 2, K])
        hit = sb("hit", [P, 2, TB, K, K])
        ex = sb("ex", [P, TB, K])
        total = sb("total", [P, 2, TB])
        pq = [ps(f"pq{i}", [P, HALF]) for i in range(4)]
        psc = [ps(f"psc{i}", [P, 2, 2, KEYS]) for i in range(4)]
        w_sem, keys_sem, exp_done = sem("w_in"), sem("keys_in"), sem("exp_done")
        tensor_done, scalar_done, vector_done, pool_done = (sem("tensor_done"), sem("scalar_done"), sem("vector_done"), sem("pool_done"))
        E = Steps(*[("q", i) for i in range(4)], *[("score", i) for i in range(4)])
        A = Steps(*[("q", i) for i in range(4)], *[("score", i) for i in range(4)])
        V = Steps(*[("rank", step) for step in range(TB + LAST)],
                  "shifted", "part0", "part1", "partf", "idxf", "equal0", "equal1", "sum", "recip", "gate")
        G = Steps(*[(step, p) for step in ("hit", K // 2, K // 4, K // 8, 1) for p in range(2)])
        block = ctx.enter_context(nc.Block())
        wv_ = kc_view(w_q)

        @block.sync
        def _(sp):
            with sp.Fori(0, PEER_HEADS) as h:
                sp.wait_ge(tensor_done, E.passes(h))
                sp.dma_start(w[:, :, :], wv_[:, :, bass.ds(h * 2 * P, 2 * P)]).then_inc(w_sem, 16)
                sp.dma_start(keys[:, :, :], keysT[bass.ds(h * 2, 2), :, :].rearrange("s d k -> d s k")).then_inc(keys_sem, 16)

        @block.tensor
        def _(pe):
            pe.sem_inc(tensor_done, 1)
            with pe.Fori(0, PEER_HEADS) as h:
                pe.wait_ge(w_sem, h * 16 + 16)
                pe.wait_ge(scalar_done, A.passes(h))
                for i in range(4):
                    p, half = i // 2, i % 2
                    for k in range(KC):
                        last = nc.tensor.matmul(pq[i][:, :], w[:, k, p * P:(p + 1) * P], h2T[:, k, half * HALF:(half + 1) * HALF],
                                                start=k == 0, stop=k == KC - 1)
                    last.then_inc(tensor_done, 1)
                pe.wait_ge(keys_sem, h * 16 + 16)
                pe.wait_ge(scalar_done, A.after(("q", 3), h))
                for i in range(4):
                    for tb in (2 * i, 2 * i + 1):
                        for p in range(2):
                            last = nc.tensor.matmul(psc[i][:, tb % 2, p, :], qT[:, p, tb * P:(tb + 1) * P], keys[:, p, :], start=True, stop=True)
                    last.then_inc(tensor_done, 1)

        @block.scalar
        def _(act):
            act.sem_inc(scalar_done, 1)
            nc.scalar.preload_act_table_set(LOG_EXP)
            def scores(h, parity, first):
                for i in range(4):
                    act.wait_ge(tensor_done, E.after(("q", i), h))
                    nc.scalar.copy(qT[:, i // 2, (i % 2) * HALF:(i % 2 + 1) * HALF], pq[i][:, :]).then_inc(scalar_done, 1)
                if not first:
                    act.wait_ge(vector_done, V.after(("rank", TB + LAST - 1), h - 2))
                for i in range(4):
                    act.wait_ge(tensor_done, E.after(("score", i), h))
                    nc.scalar.copy(s[:, parity, 2 * i:2 * i + 2, :, :].rearrange("p b s k -> p (b s k)"),
                                   psc[i][:, :, :, :].rearrange("p b s k -> p (b s k)")).then_inc(scalar_done, 1)

            def exponentials(h):
                act.wait_ge(vector_done, V.after("shifted", h))
                nc.scalar.activation(ex[:, :, :], ex[:, :, :], ACT.Exp).then_inc(exp_done, 1)

            scores(0, 0, True)
            scores(1, 1, True)
            exponentials(0)
            with act.Fori(1, PEER_HEADS // 2) as i:
                scores(i * 2, 0, False)
                exponentials(i * 2 - 1)
                scores(i * 2 + 1, 1, False)
                exponentials(i * 2)
            exponentials(PEER_HEADS - 1)
        @block.vector
        def _(dve):
            dve.sem_inc(vector_done, 1)
            def rank(h, parity):
                def chain(name):
                    dve.wait_ge(vector_done, V.after(name, h))

                for step in range(TB + LAST):
                    if step < TB and step % 2 == 0:
                        dve.wait_ge(scalar_done, A.after(("score", step // 2), h))
                    dve.wait_ge(vector_done, V.after(("rank", step - 1), h) if step else V.passes(h))
                    last = nc.vector.memset(pace[:, :], 0.0)
                    for p in range(2):
                        if step < TB:
                            last = nc.vector.max(val[:, step, p, 0:8], s[:, parity, step, p, :])
                        if 0 <= (tb := step - 1) < TB:
                            nc.vector.max_index(idx[:, tb, p, 0:8], val[:, tb, p, 0:8], s[:, parity, tb, p, :])
                            last = nc.vector.match_replace(rest[:, tb % 3, p, :], val[:, tb, p, 0:8], s[:, parity, tb, p, :], LOWEST)
                        if 0 <= (tb := step - 2) < TB:
                            last = nc.vector.max(val[:, tb, p, 8:16], rest[:, tb % 3, p, :])
                        if 0 <= (tb := step - 3) < TB:
                            last = nc.vector.max_index(idx[:, tb, p, 8:16], val[:, tb, p, 8:16], rest[:, tb % 3, p, :])
                    if 0 <= (tb := step - 3) < TB:
                        last = nc.vector.tensor_tensor(pair[:, tb % 3, :].rearrange("p (a b) -> p a b", b=K), bc(val[:, tb, 0, :], 2, [P, K, K]),
                                                       bc(val[:, tb, 1, :], 1, [P, K, K]), ALU.add)
                    if 0 <= (tb := step - 4) < TB:
                        last = nc.vector.max(top[:, tb, 0:8], pair[:, tb % 3, :])
                    if 0 <= (tb := step - 5) < TB:
                        nc.vector.max_index(pos[:, tb, 0:8], top[:, tb, 0:8], pair[:, tb % 3, :])
                        last = nc.vector.match_replace(pair_rest[:, tb % 3, :], top[:, tb, 0:8], pair[:, tb % 3, :], LOWEST)
                    if 0 <= (tb := step - 6) < TB:
                        last = nc.vector.max(top[:, tb, 8:16], pair_rest[:, tb % 3, :])
                    if 0 <= (tb := step - 7) < TB:
                        last = nc.vector.max_index(pos[:, tb, 8:16], top[:, tb, 8:16], pair_rest[:, tb % 3, :])
                    last.then_inc(vector_done, 1)
                chain(("rank", TB + LAST - 1))
                nc.vector.tensor_tensor(ex[:, :, :], top[:, :, :], top[:, :, 0:1].broadcast_to([P, TB, K]), ALU.subtract).then_inc(vector_done, 1)
                posf = pos[:, :, :].rearrange("p b k -> p (b k)")
                nc.vector.tensor_scalar(part[:, 0, :], posf, 4, None, ALU.logical_shift_right).then_inc(vector_done, 1)
                nc.vector.tensor_scalar(part[:, 1, :], posf, K - 1, None, ALU.bitwise_and).then_inc(vector_done, 1)
                chain("part1")
                nc.vector.tensor_copy(partf[:, :, :, :].rearrange("p s b k -> p s (b k)"), part[:, :, :]).then_inc(vector_done, 1)
                dve.wait_ge(pool_done, G.passes(h))
                nc.vector.tensor_copy(idxf[:, :, :, :], idx[:, :, :, :]).then_inc(vector_done, 1)
                chain("idxf")
                for p in range(2):
                    nc.vector.tensor_tensor(hit[:, p, :, :, :].rearrange("p b k r -> p (b k) r"),
                                            bc(core.const("iota")[:, 0:K], 1, [P, TB * K, K]),
                                            bc(partf[:, p, :, :].rearrange("p b k -> p (b k)"), 2, [P, TB * K, K]), ALU.is_equal).then_inc(vector_done, 1)
                dve.wait_ge(exp_done, h + 1)
                nc.vector.tensor_reduce(total[:, 0, :], ex[:, :, :], AXX, ALU.add).then_inc(vector_done, 1)
                chain("sum")
                nc.vector.reciprocal(total[:, 1, :], total[:, 0, :]).then_inc(vector_done, 1)
                chain("recip")
                nc.vector.tensor_tensor(slot_gate[:, :, bass.ds(h * K, K)], ex[:, :, :], bc(total[:, 1, :], 2, [P, TB, K]), ALU.mult).then_inc(vector_done, 1)

            with dve.Fori(0, PEER_HEADS // 2) as i:
                rank(i * 2, 0)
                rank(i * 2 + 1, 1)

        @block.gpsimd
        def _(pool):
            pool.sem_inc(pool_done, 1)
            nc.gpsimd.memset(pool_pace[:, :], 0.0)
            with pool.Fori(0, PEER_HEADS) as h:
                for p in range(2):
                    pool.wait_ge(vector_done, V.after(f"equal{p}", h))
                    nc.gpsimd.tensor_tensor(hit[:, p, :, :, :], hit[:, p, :, :, :], bc(idxf[:, :, p, :], 2, [P, TB, K, K]), ALU.mult).then_inc(pool_done, 1)
                wide = "hit"
                for m in (K // 2, K // 4, K // 8):
                    for p in range(2):
                        pool.wait_ge(pool_done, G.after((wide, p), h))
                        nc.gpsimd.tensor_tensor(hit[:, p, :, :, 0:m], hit[:, p, :, :, 0:m], hit[:, p, :, :, m:2 * m], ALU.add).then_inc(pool_done, 1)
                    wide = m
                pool.wait_ge(pool_done, G.after((wide, 1), h))
                nc.gpsimd.tensor_tensor(pool_pace[:, :], pool_pace[:, :], pool_pace[:, :], ALU.add)
                for p, out in enumerate((slot_row, slot_col)):
                    nc.gpsimd.tensor_tensor(out[:, :, bass.ds(h * K, K)], hit[:, p, :, :, 0], hit[:, p, :, :, 1], ALU.add).then_inc(pool_done, 1)


def gate_matrix(nc, core, slot_row, slot_col, slot_gate, gates):
    PER, RING, BLOCK = 4, 4, 64
    TURNS = BLOCK // (PER * RING)
    NB = T // BLOCK
    with ExitStack() as ctx:
        sb, ps, sem = stage_tools(nc, ctx, "gm")
        rowT = sb("rowT", [P, T])
        colT = sb("colT", [P, T])
        gateT = sb("gateT", [P, T])
        hot_row = sb("hot_row", [P, RING, PER, KEYS])
        hot_col = sb("hot_col", [P, RING, PER, KEYS])
        staged = sb("staged", [P, 2, KEYS, BLOCK])
        pt = [ps(f"pt{i}", [P, 2, HALF]) for i in range(2)]
        pg = [ps(f"pg{i}", [P, PER, KEYS]) for i in range(RING)]
        turned, copied = sem("turned"), sem("copied")
        hot = [sem(f"hot{r}") for r in range(RING)]
        weighted = [sem(f"weighted{r}") for r in range(RING)]
        multiplied = [sem(f"multiplied{r}") for r in range(RING)]
        collected = [sem(f"collected{r}") for r in range(RING)]
        stored = [sem(f"stored{i}") for i in range(2)]
        block = ctx.enter_context(nc.Block())
        tables = ((slot_row, rowT), (slot_col, colT), (slot_gate, gateT))

        def turn_of(i, half, j):
            return i * (2 * TURNS) + (j + half * TURNS)

        @block.tensor
        def _(pe):
            for n, (table, _) in enumerate(tables):
                if n == 2:
                    pe.wait_ge(copied, 1)
                for tb in range(TB):
                    last = nc.tensor.transpose(pt[n % 2][:, tb // 4, (tb % 4) * P:(tb % 4 + 1) * P], table[:, tb, :], core.const("ident"))
                last.then_inc(turned, 1)
            for r in range(RING):
                pe.sem_inc(multiplied[r], 1)
            with pe.Fori(0, NB // 2) as i:
                for half in range(2):
                    with pe.Fori(0, TURNS) as j:
                        for r in range(RING):
                            n = turn_of(i, half, j)
                            pe.wait_ge(weighted[r], n + 1)
                            pe.wait_ge(collected[r], n + 1)
                            for x in range(PER):
                                last = nc.tensor.matmul(pg[r][:, x, :], hot_col[:, r, x, :], hot_row[:, r, x, :], start=True, stop=True)
                            last.then_inc(multiplied[r], 1)

        @block.vector
        def _(dve):
            dve.wait_ge(copied, 3)
            iota = bc(core.const("iota"), 1, [P, PER, KEYS])
            with dve.Fori(0, NB // 2) as i:
                for half in range(2):
                    with dve.Fori(0, TURNS) as j:
                        for r in range(RING):
                            n = turn_of(i, half, j)
                            dve.wait_ge(multiplied[r], n + 1)
                            for hot_one, index in ((hot_row, rowT), (hot_col, colT)):
                                t = bass.ds(n * (RING * PER) + r * PER, PER)
                                last = nc.vector.tensor_tensor(hot_one[:, r, :, :], iota, bc(index[:, t], 2, [P, PER, KEYS]), ALU.is_equal)
                            last.then_inc(hot[r], 1)

        @block.gpsimd
        def _(pool):
            pool.wait_ge(copied, 3)
            with pool.Fori(0, NB // 2) as i:
                for half in range(2):
                    with pool.Fori(0, TURNS) as j:
                        for r in range(RING):
                            n = turn_of(i, half, j)
                            pool.wait_ge(hot[r], n + 1)
                            gate = gateT[:, bass.ds(n * (RING * PER) + r * PER, PER)]
                            nc.gpsimd.tensor_tensor(hot_col[:, r, :, :], hot_col[:, r, :, :], bc(gate, 2, [P, PER, KEYS]), ALU.mult).then_inc(weighted[r], 1)

        @block.scalar
        def _(act):
            for n, (_, table) in enumerate(tables):
                act.wait_ge(turned, n + 1)
                nc.scalar.copy(table[:, :], pt[n % 2][:, :, :].rearrange("p a t -> p (a t)")).then_inc(copied, 1)
            for r in range(RING):
                act.sem_inc(collected[r], 1)
            with act.Fori(0, NB // 2) as i:
                for half in range(2):
                    act.wait_ge(stored[half], i * 16 + 16)
                    with act.Fori(0, TURNS) as j:
                        for r in range(RING):
                            act.wait_ge(multiplied[r], turn_of(i, half, j) + 2)
                            nc.scalar.copy(staged[:, half, :, bass.ds(j * (RING * PER) + r * PER, PER)].rearrange("p k t -> p t k"),
                                           pg[r][:, :, :]).then_inc(collected[r], 1)

        @block.sync
        def _(sp):
            for half in range(2):
                sp.sem_inc(stored[half], 16)
            with sp.Fori(0, NB // 2) as i:
                for half in range(2):
                    for r in range(RING):
                        sp.wait_ge(collected[r], i * (2 * TURNS) + ((half + 1) * TURNS + 1))
                    sp.dma_start(gates[bass.ds(i * 2 + half, 1), :, :].rearrange("b p n -> (b p) n"),
                                 staged[:, half, :, :].rearrange("p k t -> p (k t)")).then_inc(stored[half], 16)
            for half in range(2):
                sp.wait_ge(stored[half], 16 * (NB // 2 + 1))


def peer_experts(nc, uT, v, gates, h2T, acc):
    EG, BLOCK = 2, 64
    NG = KEYS // EG
    NB = T // BLOCK
    UNITS, RING = TB * 2, 4
    with ExitStack() as ctx:
        sb, ps, sem = stage_tools(nc, ctx, "pe")
        h2 = sb("h2_parts", [P, 2, KC, T], F32R)
        ut = sb("u_parts", [P, 2, EG, D], F32R)
        vt = sb("v_parts", [P, 2, EG, D], F32R)
        wt = sb("weight_parts", [P, 2, 2, EG, T], F32R)
        u_whole, v_whole, g_whole, w_whole = (h2T[:, EG * j:EG * (j + 1), :] for j in range(4))
        gt = g_whole.rearrange("p e (b t) -> p (e b) t", t=EG * BLOCK)
        pu = [ps(f"pu{i}", [P, 2, HALF]) for i in range(2)]
        pv = [ps(f"pv{i}", [P, HALF]) for i in range(RING)]
        u_in, v_in, g_in = sem("u_in"), sem("v_in"), sem("g_in")
        h_high, h_cut = sem("h_high"), sem("h_cut")
        u_high, u_cut, v_high, v_cut = sem("u_high"), sem("u_cut"), sem("v_high"), sem("v_cut")
        up_done, gelu_done, down_done = sem("up_done"), sem("gelu_done"), sem("down_done")
        gated, w_high, w_cut = sem("gated"), sem("w_high"), sem("w_cut")
        added = [sem(f"added{i}") for i in range(RING)]
        block = ctx.enter_context(nc.Block())
        gv = gates.rearrange("b p n -> p b n")

        @block.sync
        def _(sp):
            def load(n, first):
                sp.wait_ge(*((h_cut, EG) if first else (u_cut, n)))
                sp.dma_start(u_whole, uT[bass.ds(n * EG, EG), :, :].rearrange("e p n -> p e n")).then_inc(u_in, 16)
                sp.wait_ge(*((h_cut, 3 * EG) if first else (gated, n * EG)))
                sp.dma_start(gt, gv[:, :, bass.ds(n * (EG * BLOCK), EG * BLOCK)]).then_inc(g_in, 16)
                if not first:
                    sp.wait_ge(v_cut, n)
                sp.dma_start(v_whole, v[bass.ds(n * EG * P, EG * P), :].rearrange("(e p) d -> p e d", p=P)).then_inc(v_in, 16)

            load(0, True)
            with sp.Fori(1, NG) as n:
                load(n, False)

        def schedule(eng, up, down):
            up(0, 0, True)
            with eng.Fori(0, NG // 2 - 1) as i:
                for s in range(2):
                    up(i * 2 + (s + 1), 1 - s, False)
                    down(i * 2 + s, s, 2)
            up(NG - 1, 1, False)
            down(NG - 2, 0, 1)
            down(NG - 1, 1, 0)

        @block.tensor
        def _(pe):
            def up(n, s, first):
                pe.wait_ge(u_cut, n + 1)
                for e in range(EG):
                    if not first:
                        pe.wait_ge(gelu_done, (n - 1) * EG + (e + 1))
                    for k in range(KC):
                        if first and e == 0:
                            pe.wait_ge(h_cut, k + 1)
                        for half in range(2):
                            span = slice(half * HALF, (half + 1) * HALF)
                            last = product_of_parts(nc, pu[e][:, half, :], ut[:, 0, e, k * P:(k + 1) * P], ut[:, 1, e, k * P:(k + 1) * P],
                                                    h2[:, 0, k, span], h2[:, 1, k, span], k == 0, k == KC - 1)
                    last.then_inc(up_done, 1)

            def down(n, s, after):
                pe.wait_ge(v_cut, n + 1)
                pe.wait_ge(w_cut, n * EG + EG)
                for x in range(UNITS):
                    tb, half = x // 2, x % 2
                    tok, span = slice(tb * P, (tb + 1) * P), slice(half * HALF, (half + 1) * HALF)
                    pe.wait_ge(added[x % RING], n * (UNITS // RING) + (x // RING + 1))
                    for e in range(EG):
                        last = product_of_parts(nc, pv[x % RING][:, :], wt[:, 0, s, e, tok], wt[:, 1, s, e, tok],
                                                vt[:, 0, e, span], vt[:, 1, e, span], e == 0, e == EG - 1)
                    last.then_inc(down_done, 1)

            schedule(pe, up, down)

        @block.scalar
        def _(act):
            def high_u(n, first):
                act.wait_ge(u_in, n * 16 + 16)
                if not first:
                    act.wait_ge(up_done, n * EG)
                nc.scalar.copy(ut[:, 0, :, :], u_whole).then_inc(u_high, 1)

            def high_v(n, first):
                act.wait_ge(v_in, n * 16 + 16)
                if not first:
                    act.wait_ge(down_done, n * UNITS)
                nc.scalar.copy(vt[:, 0, :, :], v_whole).then_inc(v_high, 1)

            def up(n, s, first):
                for e in range(EG):
                    act.wait_ge(up_done, n * EG + (e + 1))
                    if not first:
                        act.wait_ge(w_cut, (n - 1) * EG + (e + 1))
                    nc.scalar.activation(w_whole[:, e, :], pu[e][:, :, :].rearrange("p a t -> p (a t)"), ACT.Gelu).then_inc(gelu_done, 1)
                if first:
                    high_u(1, False)

            def down(n, s, after):
                if after > 1:
                    high_u(n + 2, False)
                if after > 0:
                    high_v(n + 1, False)

            for k in range(KC):
                nc.scalar.copy(h2[:, 0, k, :], h2T[:, k, :]).then_inc(h_high, 1)
            high_u(0, True)
            high_v(0, True)
            schedule(act, up, down)

        @block.vector
        def _(dve):
            def up(n, s, first):
                dve.wait_ge(g_in, n * 16 + 16)
                for e in range(EG):
                    dve.wait_ge(gelu_done, n * EG + (e + 1))
                    whole = w_whole[:, e, :].rearrange("p (b t) -> p b t", t=BLOCK)
                    nc.vector.tensor_tensor(whole, whole, gt[:, :, e * BLOCK:(e + 1) * BLOCK], ALU.mult).then_inc(gated, 1)
                    dve.wait_ge(gated, n * EG + (e + 1))
                    nc.vector.tensor_copy(wt[:, 0, s, e, :], w_whole[:, e, :]).then_inc(w_high, 1)
                    dve.wait_ge(w_high, n * EG + (e + 1))
                    nc.vector.tensor_tensor(wt[:, 1, s, e, :], w_whole[:, e, :], wt[:, 0, s, e, :].bitcast(F32), ALU.subtract).then_inc(w_cut, 1)

            def down(n, s, after):
                for x in range(UNITS):
                    a = acc[:, x // 2, (x % 2) * HALF:(x % 2 + 1) * HALF]
                    dve.wait_ge(down_done, n * UNITS + (x + 1))
                    nc.vector.tensor_tensor(a, a, pv[x % RING][:, :], ALU.add).then_inc(added[x % RING], 1)

            for r in range(RING):
                dve.sem_inc(added[r], 1)
            for k in range(KC):
                dve.wait_ge(h_high, k + 1)
                nc.vector.tensor_tensor(h2[:, 1, k, :], h2T[:, k, :], h2[:, 0, k, :].bitcast(F32), ALU.subtract).then_inc(h_cut, 1)
            schedule(dve, up, down)

        @block.gpsimd
        def _(pool):
            def rest(cut, high, parts, whole, n):
                pool.wait_ge(high, n + 1)
                nc.gpsimd.tensor_tensor(parts[:, 1, :, :], whole, parts[:, 0, :, :].bitcast(F32), ALU.subtract).then_inc(cut, 1)

            def rest_u(n):
                rest(u_cut, u_high, ut, u_whole, n)

            def rest_v(n):
                rest(v_cut, v_high, vt, v_whole, n)

            rest_u(0)
            rest_v(0)
            rest_u(1)
            with pool.Fori(0, NG - 2) as n:
                rest_u(n + 2)
                rest_v(n + 1)
            rest_v(NG - 1)


def packed_consts():
    import numpy as np

    r, c = np.arange(P)[:, None], np.arange(P)[None, :]
    mats = {
        "ident": r == c,
        "neg_from": -1.0 * (r >= c),
        "neg_before": -1.0 * (r < c),
        "causal_bias": NEG * (r >= c),
        "upto": r <= c,
        "beyond": r > c,
        "ones": np.ones((P, P)),
        "iota": c + 0 * r,
    }
    parts = [mats[name] for name in CONSTS]
    for m in LEVELS:
        parts.append((r // (2 * m) == c // (2 * m)) & (r % (2 * m) < m) & (c % (2 * m) >= m))
    parts.append(r == c)
    t = np.arange(T)[None, :]
    parts.append((t % P != 0) + 0 * r)
    return np.ascontiguousarray(np.concatenate([np.asarray(m, np.float32) for m in parts], axis=1))


def hybrid_layer(nc, a, gates, out):
    with ExitStack() as ctx:
        def sb(stack, name, shape):
            return stack.enter_context(nc.sbuf_tensor(name, shape, F32))

        hT = acc = sb(ctx, "hT_acc", [P, KC, T])
        y_sb_hg = h2T = sb(ctx, "y_h2T", [P, KC, T])
        ysbT, yhgT = y_sb_hg[:, 0:KC // 2, :], y_sb_hg[:, KC // 2:KC, :]
        with ExitStack() as upto_gates:
            core = Core(nc, upto_gates)
            with ExitStack() as mixer:
                norm_input(nc, core, a["x"], a["norm1_w"], a["consts"], hT)
                yssdT = sb(mixer, "yssdT", [P, KC // 2, T])
                stick_breaking(nc, core, a["w_in"], hT, ysbT)
                hgrn2(nc, core, a["w_in"], a["lb_logits"], a["hg_norm_w"], hT, yhgT)
                ssd(nc, core, a["w_in"], a["conv_wb"], a["ssd_rows"], a["ssd_norm_w"], hT, yssdT)
                mergedT = sb(mixer, "mergedT", [P, KC, T])
                merge(nc, core, a["w_in"], a["branch_w"], hT, [ysbT, yhgT, yssdT], mergedT)
                output_and_norm(nc, core, a["x"], a["w_out"], a["norm2_w"], mergedT, acc, h2T)
            slots = [sb(upto_gates, name, [P, TB, P]) for name in ("slot_row", "slot_col", "slot_gate")]
            peer_select(nc, core, a["peer_w_q"], a["keysT"], h2T, *slots)
            gate_matrix(nc, core, *slots, gates)
        peer_experts(nc, a["uT"], a["v"], gates, h2T, acc)
        norm_output(nc, a["final_norm_w"], acc, out)


def columns(w):
    return w.reshape(-1, P).T


def kernel(x, norm1_w, w_in, hg_lb_logits, hg_norm_w, ssd_conv_w, ssd_conv_b, ssd_dt_bias, ssd_a_log, ssd_d, ssd_norm_w,
           w_branch_sb, w_branch_hg, w_branch_ssd, w_out, norm2_w, peer_w_q, peer_sub_keys, peer_u, peer_v, final_norm_w):
    import concourse.bacc as bacc
    import numpy as np
    from concourse.bass_utils import run_bass_kernel_spmd

    laid_out = {
        "x": x[0],
        "norm1_w": columns(norm1_w[0]),
        "w_in": w_in[0],
        "lb_logits": columns(hg_lb_logits[0]),
        "hg_norm_w": columns(hg_norm_w[0]),
        "conv_wb": np.concatenate([ssd_conv_w[0].T, ssd_conv_b[0][:, None]], axis=1),
        "ssd_rows": np.stack([ssd_dt_bias[0], ssd_a_log[0], ssd_d[0]])[None],
        "ssd_norm_w": columns(ssd_norm_w[0]),
        "branch_w": np.concatenate([w_branch_sb, w_branch_hg, w_branch_ssd]),
        "w_out": w_out[0],
        "norm2_w": columns(norm2_w[0]),
        "peer_w_q": peer_w_q[0],
        "keysT": peer_sub_keys[0].reshape(2 * PEER_HEADS, KEYS, P).transpose(0, 2, 1),
        "uT": peer_u[0].reshape(KEYS, KEYS, KC, P).transpose(0, 3, 2, 1).reshape(KEYS, P, D),
        "v": peer_v[0],
        "final_norm_w": final_norm_w[None],
        "consts": packed_consts(),
    }
    laid_out = {name: np.ascontiguousarray(value) for name, value in laid_out.items()}
    nc = bacc.Bacc("TRN2", target_bir_lowering=False, num_devices=1)
    aps = {name: nc.dram_tensor(f"{name}_dram", value.shape, mybir.dt.from_np(value.dtype), kind="ExternalInput").ap()
           for name, value in laid_out.items()}
    gates = nc.dram_tensor("gates_dram", (T // 64, P, KEYS * 64), F32, kind="Internal").ap()
    out = nc.dram_tensor("out_dram", (T, D), F32, kind="ExternalOutput").ap()
    hybrid_layer(nc, aps, gates, out)
    result = run_bass_kernel_spmd(nc, [{f"{name}_dram": value for name, value in laid_out.items()}], core_ids=[0])
    return result.results[0]["out_dram"].reshape(1, T, D)
```

```python
from contextlib import ExitStack

import concourse.bass as bass
from concourse import mybir

F32 = mybir.dt.float32
U32 = mybir.dt.uint32
BF16 = mybir.dt.bfloat16
ALU = mybir.AluOpType
ACT = mybir.ActivationFunctionType
AXX = mybir.AxisListType.X

P = 128
T = 1024
D = 1024
KC = D // P
TB = T // P
HALF = 512
EPS = 1e-6

SB_HEADS, SB_DIM = 8, 64
HG_HEADS, HG_DIM = 4, 128
SSD_HEADS, SSD_DIM, SSD_GROUPS, SSD_STATE, SSD_CONV = 8, 64, 2, 64, 4
SSD_HPG = SSD_HEADS // SSD_GROUPS
SSD_GW = SSD_HPG * SSD_DIM
SB_W = SB_HEADS * SB_DIM
HG_W = HG_HEADS * HG_DIM
SSD_W = SSD_HEADS * SSD_DIM
COL_Q = 0
COL_K = COL_Q + SB_W
COL_V = COL_K + SB_W
COL_HF = COL_V + SB_W
COL_HQ = COL_HF + HG_W
COL_HI = COL_HQ + HG_W
COL_HG = COL_HI + HG_W
COL_Z = COL_HG + HG_W
COL_X = COL_Z + SSD_W
COL_B = COL_X + SSD_W
COL_C = COL_B + SSD_GROUPS * SSD_STATE
COL_DT = COL_C + SSD_GROUPS * SSD_STATE
COL_G = COL_DT + SSD_HEADS

PEER_HEADS, KEYS, TOPK = 8, 128, 16
NEG = -1e30
LOG_EXP = "natural_log_exp_and_others"

CONSTS = ("ident", "neg_from", "neg_before", "causal_bias", "upto", "beyond", "ones", "iota")
LEVELS = [64, 32, 16, 8, 4, 2, 1]
C_AT = {name: P * i for i, name in enumerate(CONSTS)}
C_LEVEL = P * len(CONSTS)
C_RESET = C_LEVEL + P * (len(LEVELS) + 1)
C_COLS = C_RESET + T


F32R = mybir.dt.float32r


def product_of_parts(nc, out, a_high, a_rest, b_high, b_rest, start, stop):
    nc.tensor.matmul(out, a_high, b_high, start=start, stop=False)
    nc.tensor.matmul(out, a_high, b_rest, start=False, stop=False)
    return nc.tensor.matmul(out, a_rest, b_high, start=False, stop=stop)


class Steps:

    def __init__(self, *names, open_passes=0):
        self.at = {name: i + 1 for i, name in enumerate(names)}
        self.per = len(names)
        self.opening = open_passes * self.per + 1
        assert len(self.at) == self.per

    def after(self, name, n=0):
        return n * self.per + (self.opening + self.at[name])

    def passes(self, n):
        return n * self.per + self.opening


def kc_view(w):
    return w.rearrange("(k p) c -> p k c", p=P)


def bc(ap, axis, shape):
    return ap.unsqueeze(axis).broadcast_to(shape)


class Core:

    def __init__(self, nc, ctx):
        self.nc = nc
        self.ctx = ctx
        self.consts = ctx.enter_context(nc.sbuf_tensor("consts", [P, C_COLS], F32))
        self.eps = ctx.enter_context(nc.sbuf_tensor("eps", [P, 1], F32))

    def const(self, name):
        at = C_AT[name]
        return self.consts[:, at:at + P]

    def level_mask(self, n):
        return self.consts[:, C_LEVEL + P * n:C_LEVEL + P * (n + 1)]


class Weights:

    def __init__(self, nc, ctx, name, w_in, room, cols):
        self.w_in = kc_view(w_in)
        self.cols = cols
        self.w = [room[:, n, :].rearrange("p (k c) -> p k c", c=P) for n in range(len(cols))]
        self.loaded = [ctx.enter_context(nc.semaphore(f"{name}{n}_loaded")) for n in range(len(cols))]

    def load(self, sp, n, i):
        sp.dma_start(self.w[n], self.w_in[:, :, bass.ds(i * P + self.cols[n], P)]).then_inc(self.loaded[n], 16)

    def load_first(self, sp):
        for n in range(len(self.cols)):
            self.load(sp, n, 0)


def stage_tools(nc, ctx, prefix):

    def sb(name, shape, dt=F32):
        return ctx.enter_context(nc.sbuf_tensor(f"{prefix}_{name}", shape, dt))

    def ps(name, shape):
        return ctx.enter_context(nc.psum_tensor(f"{prefix}_{name}", shape, F32))

    def sem(name):
        return ctx.enter_context(nc.semaphore(f"{prefix}_{name}"))

    return sb, ps, sem


def norm_input(nc, core, x, norm_w, packed_consts, hT, next_weights):
    RING = 4
    with ExitStack() as ctx:
        sb, ps, sem = stage_tools(nc, ctx, "ni")
        xt = sb("x", [P, RING, D])
        squares = sb("squares", [P, D])
        xn = sb("xn", [P, 2, D])
        stat = sb("stat", [P, 3, TB])
        wcol = sb("wcol", [P, KC])
        turned = [ps(f"turned{j}", [P, KC, P]) for j in range(2)]
        consts_in, w_in = sem("consts_in"), sem("w_in")
        x_in = [sem(f"x_in{j}") for j in range(RING)]
        scalar_done, vector_done, tensor_done = sem("scalar_done"), sem("vector_done"), sem("tensor_done")
        eps_set = sem("eps_set")
        A = Steps(*[(s, b) for b in range(TB) for s in ("squares", "std")])
        V = Steps(*[step for b in range(TB + 1) for step in [(s, b) for s in ("rstd", "xn")] * (b < TB)
                    + [(s, b - 1) for s in ("turned0", "turned1")] * (b > 0)])
        E = Steps(*range(TB))
        block = ctx.enter_context(nc.Block())
        xv = x.rearrange("(b p) d -> p b d", p=P)

        @block.sync
        def _(sp):
            for b in range(TB):
                if b >= RING:
                    sp.wait_ge(vector_done, V.after(("xn", b - RING)))
                sp.dma_start(xt[:, b % RING, :], xv[:, b, :]).then_inc(x_in[b % RING], 16)
                if b == 0:
                    sp.dma_start(core.consts[:, :], packed_consts).then_inc(consts_in, 16)
                    sp.dma_start(wcol[:, :], norm_w).then_inc(w_in, 16)
            next_weights.load_first(sp)

        @block.scalar
        def _(act):
            act.sem_inc(scalar_done, 1)
            act.wait_ge(eps_set, 1)
            for b in range(TB):
                act.wait_ge(x_in[b % RING], 16 * (b // RING + 1))
                nc.scalar.activation(squares[:, :], xt[:, b % RING, :], ACT.Square, accum_out=stat[:, 0, b:b + 1]).then_inc(scalar_done, 1)
                act.wait_ge(scalar_done, A.after(("squares", b)))
                nc.scalar.activation(stat[:, 1, b:b + 1], stat[:, 0, b:b + 1], ACT.Sqrt, scale=1.0 / D, bias=core.eps[:, :]).then_inc(scalar_done, 1)

        @block.vector
        def _(dve):
            dve.sem_inc(vector_done, 1)
            nc.vector.memset(core.eps[:, :], EPS).then_inc(eps_set, 1)
            dve.wait_ge(w_in, 16)
            for b in range(TB + 1):
                if b < TB:
                    dve.wait_ge(scalar_done, A.after(("std", b)))
                    nc.vector.reciprocal(stat[:, 2, b:b + 1], stat[:, 1, b:b + 1]).then_inc(vector_done, 1)
                    dve.wait_ge(vector_done, V.after(("rstd", b)))
                    if b >= 2:
                        dve.wait_ge(tensor_done, E.after(b - 2))
                    nc.vector.tensor_scalar(xn[:, b % 2, :], xt[:, b % RING, :], stat[:, 2, b:b + 1], None, ALU.mult).then_inc(vector_done, 1)
                if b > 0:
                    r = b - 1
                    dve.wait_ge(tensor_done, E.after(r))
                    for n in range(2):
                        ks = slice(4 * n, 4 * n + 4)
                        nc.vector.tensor_tensor(hT[:, ks, r * P:(r + 1) * P], turned[r % 2][:, ks, :],
                                                bc(wcol[:, ks], 2, [P, 4, P]), ALU.mult).then_inc(vector_done, 1)

        @block.tensor
        def _(pe):
            pe.sem_inc(tensor_done, 1)
            pe.wait_ge(consts_in, 16)
            for b in range(TB):
                pe.wait_ge(vector_done, V.after(("xn", b)))
                if b >= 2:
                    pe.wait_ge(vector_done, V.after(("turned1", b - 2)))
                for k in range(KC):
                    last = nc.tensor.transpose(turned[b % 2][:, k, :], xn[:, b % 2, k * P:(k + 1) * P], core.const("ident"))
                last.then_inc(tensor_done, 1)


def stick_breaking(nc, core, weights, hT, ysbT, next_weights):
    with ExitStack() as ctx:
        sb, ps, sem = stage_tools(nc, ctx, "sb")
        wq, wk, wv = weights.w
        qT = sb("qT", [P, T])
        kT = sb("kT", [P, T])
        v = sb("v", [P, TB, P])
        qT_next = sb("qT_next", [P, T])
        kT_next = sb("kT_next", [P, T])
        v_next = sb("v_next", [P, TB, P])
        NZ = 7
        SOFT, TAIL, REST, EXP, Y = 1, 3, 4, 4, 5
        zs = sb("zs", [P, NZ, HALF])
        mag = sb("mag", [P, NZ, HALF])
        soft = sb("soft_parts", [P, 2, NZ, HALF], F32R)
        triangles = sb("triangles", [P, 2, P], F32R)
        aT = sb("aT", [P, NZ, HALF])
        pz = [ps(f"pz{i}", [P, HALF]) for i in range(3)]
        pacc = [ps(f"pacc{i}", [P, HALF]) for i in range(2)]
        py = ps("py", [P, HALF])
        pp = [ps(f"pp{i}", [P, HALF]) for i in range(2)]
        triangles_set = sem("triangles_set")
        projected, taken, qk_moved, v_moved = sem("projected"), sem("taken"), sem("qk_moved"), sem("v_moved")
        tensor_done, scalar_done, vector_done, pool_done = (sem("tensor_done"), sem("scalar_done"), sem("vector_done"), sem("pool_done"))

        tiles = []
        for half in range(2):
            for kb in reversed(range(4 * half + 4)):
                for head in range(2):
                    tiles.append((head, half, kb, max(0, kb - 4 * half) * P))
        N = len(tiles)
        diagonal = [kb >= 4 * half for _, half, kb, _ in tiles]
        ends = {max(i for i, t in enumerate(tiles) if t[1] == half): half for half in range(2)}
        units = [("q", 0), ("q", 1), ("k", 0), ("k", 1)] + [("v", n) for n in range(2)]

        EP, AP = Steps(*units), Steps(*units)
        pieces = [(n, k) for n in range(4) for k in range(KC)] + [(n, tb) for n in (4, 5) for tb in range(4)]
        at_step, spent = {}, 0
        for n, x in pieces:
            price = 1 if n < 4 else 2
            at_step.setdefault(spent * N // (4 * KC + 16), []).append((n, x))
            spent += price
        whole_at = {n: max(step for step, some in at_step.items() if any(m == n for m, _ in some)) for n in range(6)}

        e_names = []
        for s in range(N + Y):
            e_names += [("z", s)] * (s < N) + [("rest", s - REST)] * (REST <= s < N + REST)
            e_names += [("tail", s - TAIL)] * (TAIL <= s < N + TAIL) + [("y", s - Y)] * (s >= Y)
        E = Steps(*e_names)
        v_names = []
        for s in range(N + TAIL):
            if s < N:
                v_names += [("zs", s)] + [("zd", s)] * (diagonal[s] and tiles[s][3] + P < HALF)
            v_names += [("soft", s - SOFT), ("high", s - SOFT)] * (SOFT <= s < N + SOFT) + [("arg", s - TAIL)] * (s >= TAIL)
        V = Steps(*v_names)
        a_names = []
        for s in range(N + EXP):
            a_names += [("mag", s), ("exp", s), ("ln", s)] * (s < N) + [("weights", s - EXP)] * (s >= EXP)
            a_names += [("out", ends[s - Y])] if s - Y in ends else []
        a_names += [("out", 1)]
        A = Steps(*a_names)
        G = Steps(*range(N))
        block = ctx.enter_context(nc.Block())

        @block.sync
        def _(sp):
            next_weights.load_first(sp)
            with sp.Fori(1, SB_HEADS // 2) as c:
                for n in range(3):
                    sp.wait_ge(projected, EP.after(units[2 * n + 1], c - 1))
                    weights.load(sp, n, c)

        @block.tensor
        def _(pe):
            pe.sem_inc(tensor_done, 1)
            pe.wait_ge(triangles_set, 2)
            pe.sem_inc(projected, 1)

            def project(c, some, first):
                for n, x in some:
                    kind, part = units[n]
                    if x == 0:
                        pe.wait_ge(weights.loaded["qkv".index(kind)], c * 16 + 16)
                        if n >= 2:
                            pe.wait_ge(taken, AP.after(units[n - 2], c))
                        elif not first:
                            pe.wait_ge(taken, AP.after(units[n + 4], c - 1))
                    if kind in "qk":
                        w = wq if kind == "q" else wk
                        last = nc.tensor.matmul(pp[n % 2][:, :], w[:, x, :], hT[:, x, part * HALF:(part + 1) * HALF],
                                                start=x == 0, stop=x == KC - 1)
                    else:
                        for k in range(KC):
                            last = nc.tensor.matmul(pp[n % 2][:, x * P:(x + 1) * P], hT[:, k, (4 * part + x) * P:(4 * part + x + 1) * P],
                                                    wv[:, k, :], start=k == 0, stop=k == KC - 1)
                    if x == (KC - 1 if kind in "qk" else 3):
                        last.then_inc(projected, 1)

            def attend(c, ahead):
                pe.wait_ge(qk_moved, c * 2 + 2)
                for s in range(N + Y):
                    if s < N:
                        head, half, kb, q0 = tiles[s]
                        hp = slice(64 * head, 64 * head + 64)
                        if s >= 3:
                            pe.wait_ge(vector_done, V.after(("zd" if ("zd", s - 3) in V.at else "zs", s - 3), c))
                        nc.tensor.matmul(pz[s % 3][:, q0:HALF], kT[hp, kb * P:(kb + 1) * P],
                                         qT[hp, half * HALF + q0:(half + 1) * HALF],
                                         start=True, stop=True).then_inc(tensor_done, 1)
                    if REST <= s < N + REST:
                        r = s - REST
                        head, half, kb, q0 = tiles[r]
                        pe.wait_ge(vector_done, V.after(("arg", r), c))
                        for part in range(2):
                            last = nc.tensor.matmul(pacc[head][:, q0:HALF], triangles[:, 1, :], soft[:, part, r % NZ, q0:HALF],
                                                    start=False, stop=part == 1, skip_group_check=True)
                        last.then_inc(tensor_done, 1)
                    if TAIL <= s < N + TAIL:
                        r = s - TAIL
                        head, half, kb, q0 = tiles[r]
                        pe.wait_ge(pool_done, G.after(r, c))
                        for part in range(2):
                            last = nc.tensor.matmul(pacc[head][:, q0:HALF], triangles[:, 0, :], soft[:, part, r % NZ, q0:HALF],
                                                    start=kb == 4 * half + 3 and part == 0, stop=False, skip_group_check=True)
                        last.then_inc(tensor_done, 1)
                    if s >= Y:
                        r = s - Y
                        head, half, kb, q0 = tiles[r]
                        pe.wait_ge(scalar_done, A.after(("weights", r), c))
                        if r == 0:
                            pe.wait_ge(v_moved, c + 1)
                            pe.wait_ge(scalar_done, A.passes(c))
                        if half == 1 and kb == 7:
                            pe.wait_ge(scalar_done, A.after(("out", 0), c))
                        nc.tensor.matmul(py[64 * head:64 * head + 64, q0:HALF], v[:, kb, 64 * head:64 * head + 64],
                                         aT[:, r % NZ, q0:HALF], start=kb == 4 * half + 3, stop=kb == 0,
                                         skip_group_check=True).then_inc(tensor_done, 1)
                    if ahead:
                        project(c + 1, at_step.get(s, []), False)

            project(0, pieces, True)
            with pe.Fori(0, SB_HEADS // 2 - 1) as c:
                attend(c, True)
            attend(SB_HEADS // 2 - 1, False)

        @block.scalar
        def _(act):
            act.sem_inc(scalar_done, 1)
            nc.scalar.preload_act_table_set(LOG_EXP)
            act.sem_inc(taken, 1)

            def take(c, n, first):
                kind, part = units[n]
                act.wait_ge(projected, EP.after(units[n], c))
                if not first:
                    act.wait_ge(*((qk_moved, c * 2) if kind in "qk" else (v_moved, c)))
                if kind == "q":
                    nc.scalar.mul(qT_next[:, part * HALF:(part + 1) * HALF], pp[n % 2][:, :], SB_DIM ** -0.5).then_inc(taken, 1)
                elif kind == "k":
                    nc.scalar.copy(kT_next[:, part * HALF:(part + 1) * HALF], pp[n % 2][:, :]).then_inc(taken, 1)
                else:
                    nc.scalar.copy(v_next[:, 4 * part:4 * part + 4, :].rearrange("p b d -> p (b d)"), pp[n % 2][:, :]).then_inc(taken, 1)

            def attend(c, ahead):
                def out(half):
                    last = max(i for i, t in enumerate(tiles) if t[1] == half)
                    act.wait_ge(tensor_done, E.after(("y", last), c))
                    nc.scalar.copy(ysbT[:, bass.ds(c, 1), half * HALF:(half + 1) * HALF].rearrange("p c t -> p (c t)"),
                                   py[:, :]).then_inc(scalar_done, 1)

                for s in range(N + EXP):
                    if s < N:
                        q0 = tiles[s][3]
                        act.wait_ge(vector_done, V.after(("zd" if ("zd", s) in V.at else "zs", s), c))
                        nc.scalar.activation(mag[:, s % NZ, q0:HALF], zs[:, s % NZ, q0:HALF], ACT.Abs).then_inc(scalar_done, 1)
                        act.wait_ge(scalar_done, A.after(("mag", s), c))
                        nc.scalar.activation(mag[:, s % NZ, q0:HALF], mag[:, s % NZ, q0:HALF], ACT.Exp, scale=-1.0).then_inc(scalar_done, 1)
                        act.wait_ge(scalar_done, A.after(("exp", s), c))
                        nc.scalar.activation(mag[:, s % NZ, q0:HALF], mag[:, s % NZ, q0:HALF], ACT.Ln, bias=1.0).then_inc(scalar_done, 1)
                    if s >= EXP:
                        r = s - EXP
                        q0 = tiles[r][3]
                        act.wait_ge(vector_done, V.after(("arg", r), c))
                        if r >= NZ:
                            act.wait_ge(tensor_done, E.after(("y", r - NZ), c))
                        nc.scalar.activation(aT[:, r % NZ, q0:HALF], zs[:, r % NZ, q0:HALF], ACT.Exp).then_inc(scalar_done, 1)
                    if s - Y in ends:
                        out(ends[s - Y])
                    if ahead:
                        for n in range(6):
                            if whole_at[n] == s - 1:
                                take(c + 1, n, False)
                out(1)
                if ahead:
                    move(c + 1)

            def move(c):
                act.wait_ge(taken, AP.after(("v", 1), c))
                nc.scalar.copy(v[:, :, :], v_next[:, :, :]).then_inc(v_moved, 1)

            for n in range(6):
                take(0, n, True)
            move(0)
            with act.Fori(0, SB_HEADS // 2 - 1) as c:
                attend(c, True)
            attend(SB_HEADS // 2 - 1, False)

        @block.vector
        def _(dve):
            dve.sem_inc(vector_done, 1)
            for n, name in enumerate(("neg_from", "neg_before")):
                nc.vector.tensor_copy(triangles[:, n, :], core.const(name)).then_inc(triangles_set, 1)
            def move(c):
                dve.wait_ge(taken, AP.after(("k", 1), c))
                nc.vector.tensor_copy(qT[:, :], qT_next[:, :]).then_inc(qk_moved, 1)
                nc.vector.tensor_copy(kT[:, :], kT_next[:, :]).then_inc(qk_moved, 1)

            def attend(c, ahead):
                for s in range(N + TAIL):
                    if s < N:
                        q0 = tiles[s][3]
                        dve.wait_ge(tensor_done, E.after(("z", s), c))
                        dve.wait_ge(scalar_done, A.after(("weights", s - NZ), c) if s >= NZ else A.passes(c))
                        if diagonal[s]:
                            nc.vector.tensor_tensor(zs[:, s % NZ, q0:q0 + P], pz[s % 3][:, q0:q0 + P],
                                                    core.const("causal_bias"), ALU.add).then_inc(vector_done, 1)
                            if q0 + P < HALF:
                                nc.vector.tensor_copy(zs[:, s % NZ, q0 + P:HALF], pz[s % 3][:, q0 + P:HALF]).then_inc(vector_done, 1)
                        else:
                            nc.vector.tensor_copy(zs[:, s % NZ, :], pz[s % 3][:, :]).then_inc(vector_done, 1)
                    if SOFT <= s < N + SOFT:
                        r = s - SOFT
                        q0 = tiles[r][3]
                        dve.wait_ge(scalar_done, A.after(("ln", r), c))
                        if r >= NZ:
                            dve.wait_ge(tensor_done, E.after(("rest", r - NZ), c))
                        nc.vector.scalar_tensor_tensor(mag[:, r % NZ, q0:HALF], zs[:, r % NZ, q0:HALF], 0.0,
                                                       mag[:, r % NZ, q0:HALF], ALU.max, ALU.add).then_inc(vector_done, 1)
                        dve.wait_ge(vector_done, V.after(("soft", r), c))
                        nc.vector.tensor_copy(soft[:, 0, r % NZ, q0:HALF], mag[:, r % NZ, q0:HALF]).then_inc(vector_done, 1)
                    if s >= TAIL:
                        r = s - TAIL
                        q0 = tiles[r][3]
                        dve.wait_ge(tensor_done, E.after(("tail", r), c))
                        nc.vector.tensor_tensor(zs[:, r % NZ, q0:HALF], zs[:, r % NZ, q0:HALF],
                                                pacc[tiles[r][0]][:, q0:HALF], ALU.add).then_inc(vector_done, 1)
                if ahead:
                    move(c + 1)

            move(0)
            with dve.Fori(0, SB_HEADS // 2 - 1) as c:
                attend(c, True)
            attend(SB_HEADS // 2 - 1, False)

        @block.gpsimd
        def _(pool):
            pool.sem_inc(pool_done, 1)
            with pool.Fori(0, SB_HEADS // 2) as c:
                for r in range(N):
                    at = (r % NZ, slice(tiles[r][3], HALF))
                    pool.wait_ge(vector_done, V.after(("high", r), c))
                    nc.gpsimd.tensor_tensor(soft[:, 1, at[0], at[1]], mag[:, at[0], at[1]], soft[:, 0, at[0], at[1]].bitcast(F32), ALU.subtract).then_inc(pool_done, 1)


def hgrn2(nc, core, weights, lb_logits, norm_w, hT, yhgT, next_weights):
    NL = len(LEVELS)
    with ExitStack() as ctx:
        sb, ps, sem = stage_tools(nc, ctx, "hg")
        logits = sb("lb_logits", [P, HG_HEADS])
        shifted = sb("shifted", [P, HG_HEADS])
        gamma_of = sb("gamma", [P, 2, HG_HEADS])
        lower = sb("lower", [P, HG_HEADS])
        upper = sb("upper", [P, HG_HEADS])
        lb = sb("lb", [P, 2])
        nw = sb("norm_w", [P, 1])
        ln_c = sb("ln_c", [P, 2])
        e1 = sb("e1", [P, T])
        e2 = sb("e2", [P, T])
        q = sb("q", [P, T])
        key = sb("key", [P, T])
        logf = sb("logf", [P, T])
        b = sb("b", [P, TB, P])
        ebl = sb("chunk_decay", [P, TB])
        XR = 3
        x = sb("x", [P, XR, T])
        masked = sb("masked", [P, 2, T])
        eq = sb("eq", [P, T])
        q_raw = sb("q_raw", [P, T])
        g_raw = sb("g_raw", [P, T])
        scores = sb("scores", [P, TB, P])
        v = sb("v", [P, TB, P])
        gate = sb("gate", [P, TB, P])
        kd = sb("kd", [P, TB, P])
        kdn = sb("kdn", [P, TB, P])
        qd = sb("qd", [P, TB, P])
        state = sb("state", [P, TB, P])
        y = sb("y", [P, TB, P])
        ss = sb("ss", [P, 3 * TB])
        big = [ps(f"big{i}", [P, 2, HALF]) for i in range(4)]
        w, w_sem = weights.w, weights.loaded
        small_in = sem("small_in")
        nw_in = sem("norm_w_in")
        tensor_done, scalar_done, vector_done, pool_done = (sem("tensor_done"), sem("scalar_done"), sem("vector_done"), sem("pool_done"))
        projected, taken = sem("projected"), sem("taken")
        i_projected = sem("i_projected")

        E = Steps("g", "kdn", "same", ("level", 0), "dstate", *[("level", n) for n in range(1, NL)], "o", "yT")
        EF = Steps("f", "q")
        L = Steps("shifted", "recip", "gamma", "lower", "upper")
        V = Steps("lb", "one_minus_lb", "e1p", "f", "e2p", "key", "f_lb", "key_lb", "f_hi", "f_lo", "logf", "b",
                  "qp", "qr", "q", "kd_arg", "kd", "qd", ("diff", 0), ("diff", 1),
                  "same_masked", ("left", 0), ("right", 0),
                  *[step for n in range(NL) for step in [("left", n + 1), ("right", n + 1)] * (n + 1 < NL)
                    + [("diff", n + 2)] * (n + 2 < NL) + [("masked", n)]
                    + [("state", c) for c in range(1, TB)] * (n == 0)], "gp", "gr", "gate", "ss", "rstd", "y_rstd", "y")
        A = Steps("ln_hi", "ln_lo", "v", "exp_b", "kd_exp", "chunk_decay",
                  *[(s, n) for n in range(2) for s in ("decay_left", "decay_right")], "eg", "g_raw", "kdn",
                  *[(s, n) for n in range(2, NL) for s in ("decay_left", "decay_right")], "square", "std", "yT")
        AF = Steps("e1", "e2", "eq", "q_raw")
        G = Steps(*[("sum", n) for n in range(NL)])
        lnc_done, const_set = sem("ln_c_done"), sem("const_set")
        bound_done, bound_exp_done = sem("bound_done"), sem("bound_exp_done")
        block = ctx.enter_context(nc.Block())
        CUT, UP = 2.0 ** -40, 2.0 ** 60

        def flat(ap):
            return ap.rearrange("p b d -> p (b d)")

        @block.sync
        def _(sp):
            sp.dma_start(nw[:, :], norm_w).then_inc(nw_in, 16)
            sp.dma_start(logits[:, :], lb_logits).then_inc(small_in, 16)
            next_weights.load_first(sp)
            with sp.Fori(1, HG_HEADS) as h:
                sp.wait_ge(projected, EF.after("f", h - 1))
                weights.load(sp, 0, h)
                sp.wait_ge(projected, EF.after("q", h - 1))
                weights.load(sp, 1, h)
                sp.wait_ge(i_projected, h)
                weights.load(sp, 2, h)
                sp.wait_ge(tensor_done, E.after("g", h - 1))
                weights.load(sp, 3, h)

        @block.tensor
        def _(pe):
            pe.sem_inc(tensor_done, 1)
            pe.sem_inc(projected, 1)

            def project_ahead(h, pieces):
                for n, half, k in pieces:
                    if half == 0 and k == 0:
                        pe.wait_ge(w_sem[n], h * 16 + 16)
                    last = nc.tensor.matmul(big[2 + n][:, half, :], w[n][:, k, :], hT[:, k, half * HALF:(half + 1) * HALF],
                                            start=k == 0, stop=k == KC - 1)
                    if half == 1 and k == KC - 1:
                        last.then_inc(projected, 1)

            pieces = [(n, half, k) for n in range(2) for half in range(2) for k in range(KC)]

            def project_tokens(h, n):
                pe.wait_ge(w_sem[n], h * 16 + 16)
                for tb in range(TB):
                    for k in range(KC):
                        last = nc.tensor.matmul(big[n][:, tb // 4, (tb % 4) * P:(tb % 4 + 1) * P], hT[:, k, tb * P:(tb + 1) * P],
                                                w[n][:, k, :], start=k == 0, stop=k == KC - 1)
                return last

            def one_head(h, last_head):
                pe.wait_ge(scalar_done, A.passes(h))
                pe.wait_ge(vector_done, V.passes(h))
                pe.wait_ge(taken, AF.after("q_raw", h))
                project_tokens(h, 3).then_inc(tensor_done, 1)
                pe.wait_ge(scalar_done, A.after("v", h))
                if not last_head:
                    project_ahead(h + 1, pieces[:2 * KC])
                pe.wait_ge(vector_done, V.after("kd", h))
                for c in range(TB):
                    last = nc.tensor.transpose(big[1][:, c // 4, (c % 4) * P:(c % 4 + 1) * P], kd[:, c, :], core.const("ident"))
                last.then_inc(tensor_done, 1)
                pe.wait_ge(vector_done, V.after("q", h))
                for c in range(TB):
                    cs = slice(c * P, (c + 1) * P)
                    last = nc.tensor.matmul(big[0][:, c // 4, (c % 4) * P:(c % 4 + 1) * P], key[:, cs], q[:, cs], start=True, stop=True)
                last.then_inc(tensor_done, 1)
                for n in range(NL):
                    pe.wait_ge(vector_done, V.after(("right", n), h))
                    if n == 0:
                        pe.wait_ge(scalar_done, A.after("kdn", h))
                    else:
                        pe.wait_ge(vector_done, V.after("same_masked" if n == 1 else ("masked", n - 2), h))
                    for c in range(TB):
                        cs = slice(c * P, (c + 1) * P)
                        last = nc.tensor.matmul(big[(n + 1) % 2][:, c // 4, (c % 4) * P:(c % 4 + 1) * P], x[:, n % XR, cs], x[:, n % XR, cs],
                                                start=True, stop=True)
                    last.then_inc(tensor_done, 1)
                    if n == 0:
                        for c in range(TB):
                            last = nc.tensor.matmul(big[3][:, c // 4, (c % 4) * P:(c % 4 + 1) * P], kdn[:, c, :], v[:, c, :], start=True, stop=True)
                        last.then_inc(tensor_done, 1)
                    if n and not last_head:
                        if n == 1:
                            pe.wait_ge(vector_done, V.after(("state", TB - 1), h))
                        of_q = len(pieces) - 2 * KC
                        project_ahead(h + 1, pieces[2 * KC + (n - 1) * of_q // (NL - 1):2 * KC + n * of_q // (NL - 1)])
                pe.wait_ge(vector_done, V.after(("state", TB - 1), h))
                pe.wait_ge(pool_done, G.after(("sum", NL - 1), h))
                for c in range(TB):
                    o = big[0][:, c // 4, (c % 4) * P:(c % 4 + 1) * P]
                    last = nc.tensor.matmul(o, scores[:, c, :], v[:, c, :], start=True, stop=c == 0)
                    if c:
                        last = nc.tensor.matmul(o, qd[:, c, :], state[:, c, :], start=False, stop=True)
                last.then_inc(tensor_done, 1)
                if not last_head:
                    pe.wait_ge(taken, AF.after("e2", h + 1))
                    project_tokens(h + 1, 2).then_inc(i_projected, 1)
                pe.wait_ge(vector_done, V.after("y", h))
                for c in range(TB):
                    last = nc.tensor.transpose(big[1][:, c // 4, (c % 4) * P:(c % 4 + 1) * P], y[:, c, :], core.const("ident"))
                last.then_inc(tensor_done, 1)

            project_ahead(0, pieces)
            pe.wait_ge(taken, AF.after("e2"))
            project_tokens(0, 2).then_inc(i_projected, 1)
            with pe.Fori(0, HG_HEADS - 1) as h:
                one_head(h, False)
            one_head(HG_HEADS - 1, True)

        @block.scalar
        def _(act):
            act.sem_inc(scalar_done, 1)
            nc.scalar.preload_act_table_set(LOG_EXP)
            act.wait_ge(const_set, 1)
            nc.scalar.activation(ln_c[:, 1:2], ln_c[:, 0:1], ACT.Ln).then_inc(lnc_done, 1)
            act.wait_ge(bound_done, L.after("shifted"))
            nc.scalar.activation(gamma_of[:, 0, :], shifted[:, :], ACT.Exp).then_inc(bound_exp_done, 1)
            act.wait_ge(nw_in, 16)
            def take_f(h):
                act.wait_ge(projected, EF.after("f", h))
                nc.scalar.activation(e1[:, :], flat(big[2][:, :, :]), ACT.Exp, scale=-1.0).then_inc(taken, 1)
                nc.scalar.activation(e2[:, :], flat(big[2][:, :, :]), ACT.Exp).then_inc(taken, 1)

            def take_q(h):
                act.wait_ge(projected, EF.after("q", h))
                nc.scalar.activation(eq[:, :], flat(big[3][:, :, :]), ACT.Exp, scale=-1.0).then_inc(taken, 1)
                nc.scalar.copy(q_raw[:, :], flat(big[3][:, :, :])).then_inc(taken, 1)

            def decays(h, n):
                act.wait_ge(vector_done, V.after(("diff", n), h))
                xv = x[:, n % XR, :].rearrange("p (b s m) -> p b s m", s=2, m=LEVELS[n])
                nc.scalar.activation(xv[:, :, 0, :], xv[:, :, 0, :], ACT.Exp, scale=-1.0).then_inc(scalar_done, 1)
                nc.scalar.activation(xv[:, :, 1, :], xv[:, :, 1, :], ACT.Exp).then_inc(scalar_done, 1)

            def one_head(h, last_head):
                act.wait_ge(vector_done, V.after("f_lo", h))
                nc.scalar.activation(e1[:, :], e1[:, :], ACT.Ln).then_inc(scalar_done, 1)
                nc.scalar.activation(e2[:, :], e2[:, :], ACT.Ln, scale=UP).then_inc(scalar_done, 1)
                act.wait_ge(i_projected, h + 1)
                nc.scalar.copy(flat(v[:, :, :]), flat(big[2][:, :, :])).then_inc(scalar_done, 1)
                act.wait_ge(vector_done, V.after("b", h))
                nc.scalar.activation(flat(qd[:, :, :]), flat(b[:, :, :]), ACT.Exp).then_inc(scalar_done, 1)
                act.wait_ge(vector_done, V.after("kd_arg", h))
                nc.scalar.activation(flat(kd[:, :, :]), flat(kd[:, :, :]), ACT.Exp).then_inc(scalar_done, 1)
                nc.scalar.activation(ebl[:, :], b[:, :, P - 1], ACT.Exp).then_inc(scalar_done, 1)
                decays(h, 0)
                decays(h, 1)
                act.wait_ge(tensor_done, E.after("g", h))
                nc.scalar.activation(flat(gate[:, :, :]), flat(big[3][:, :, :]), ACT.Exp, scale=-1.0).then_inc(scalar_done, 1)
                nc.scalar.copy(g_raw[:, :], flat(big[3][:, :, :])).then_inc(scalar_done, 1)
                act.wait_ge(tensor_done, E.after("kdn", h))
                nc.scalar.copy(flat(kdn[:, :, :]), flat(big[1][:, :, :])).then_inc(scalar_done, 1)
                for n in range(2, NL):
                    decays(h, n)
                    if n == NL - 2 and not last_head:
                        take_f(h + 1)
                if not last_head:
                    take_q(h + 1)
                act.wait_ge(tensor_done, E.after("o", h))
                nc.scalar.activation(logf[:, :], flat(big[0][:, :, :]), ACT.Square).then_inc(scalar_done, 1)
                act.wait_ge(vector_done, V.after("ss", h))
                nc.scalar.activation(ss[:, TB:2 * TB], ss[:, 0:TB], ACT.Sqrt, scale=1.0 / HG_DIM, bias=core.eps[:, :]).then_inc(scalar_done, 1)
                act.wait_ge(tensor_done, E.after("yT", h))
                nc.scalar.activation(yhgT[:, bass.ds(h, 1), :].rearrange("p c t -> p (c t)"), flat(big[1][:, :, :]),
                                     ACT.Copy, scale=nw[:, :]).then_inc(scalar_done, 1)

            act.sem_inc(taken, 1)
            take_f(0)
            take_q(0)
            with act.Fori(0, HG_HEADS - 1) as h:
                one_head(h, False)
            one_head(HG_HEADS - 1, True)

        @block.vector
        def _(dve):
            dve.sem_inc(vector_done, 1)
            def chain(name, h):
                dve.wait_ge(vector_done, V.after(name, h))

            dve.sem_inc(bound_done, 1)
            nc.vector.memset(ln_c[:, 0:1], CUT * UP).then_inc(const_set, 1)
            dve.wait_ge(small_in, 16)
            nc.vector.tensor_tensor(shifted[:, :], logits[:, :], logits[:, :], ALU.subtract).then_inc(bound_done, 1)
            dve.wait_ge(bound_exp_done, 1)
            nc.vector.reciprocal(gamma_of[:, 1, :], gamma_of[:, 0, :]).then_inc(bound_done, 1)
            dve.wait_ge(bound_done, L.after("recip"))
            nc.vector.tensor_tensor(shifted[:, :], gamma_of[:, 0, :], gamma_of[:, 1, :], ALU.mult).then_inc(bound_done, 1)
            dve.wait_ge(bound_done, L.after("gamma"))
            nc.vector.tensor_tensor(lower[:, :], shifted[:, :], shifted[:, :], ALU.subtract).then_inc(bound_done, 1)
            dve.wait_ge(bound_done, L.after("lower"))
            nc.vector.tensor_scalar(upper[:, :], lower[:, :], -1.0, 1.0, ALU.mult, ALU.add).then_inc(bound_done, 1)
            dve.wait_ge(bound_done, L.after("upper"))
            dve.wait_ge(lnc_done, 1)
            with dve.Fori(0, HG_HEADS) as h:
                nc.vector.tensor_copy(lb[:, 0:1], lower[:, bass.ds(h, 1)]).then_inc(vector_done, 1)
                nc.vector.tensor_copy(lb[:, 1:2], upper[:, bass.ds(h, 1)]).then_inc(vector_done, 1)
                dve.wait_ge(taken, AF.after("e1", h))
                nc.vector.tensor_scalar(e1[:, :], e1[:, :], 1.0, None, ALU.add).then_inc(vector_done, 1)
                chain("e1p", h)
                nc.vector.reciprocal(logf[:, :], e1[:, :]).then_inc(vector_done, 1)
                dve.wait_ge(taken, AF.after("e2", h))
                nc.vector.tensor_scalar(e2[:, :], e2[:, :], 1.0, None, ALU.add).then_inc(vector_done, 1)
                chain("e2p", h)
                nc.vector.reciprocal(key[:, :], e2[:, :]).then_inc(vector_done, 1)
                chain("one_minus_lb", h)
                nc.vector.tensor_scalar(logf[:, :], logf[:, :], lb[:, 1:2], lb[:, 0:1], ALU.mult, ALU.add).then_inc(vector_done, 1)
                chain("key", h)
                nc.vector.tensor_scalar(key[:, :], key[:, :], lb[:, 1:2], None, ALU.mult).then_inc(vector_done, 1)
                chain("f_lb", h)
                nc.vector.tensor_scalar(e1[:, :], logf[:, :], CUT, None, ALU.max).then_inc(vector_done, 1)
                nc.vector.tensor_scalar(e2[:, :], logf[:, :], 1e-30, CUT, ALU.max, ALU.min).then_inc(vector_done, 1)
                dve.wait_ge(scalar_done, A.after("ln_lo", h))
                nc.vector.scalar_tensor_tensor(logf[:, :], e2[:, :], ln_c[:, 1:2], e1[:, :], ALU.subtract, ALU.add).then_inc(vector_done, 1)
                chain("logf", h)
                nc.vector.tensor_tensor_scan(flat(b[:, :, :]), core.consts[:, C_RESET:C_RESET + T], logf[:, :], 0.0,
                                             ALU.mult, ALU.add).then_inc(vector_done, 1)
                dve.wait_ge(taken, AF.after("q_raw", h))
                nc.vector.tensor_scalar(eq[:, :], eq[:, :], 1.0, None, ALU.add).then_inc(vector_done, 1)
                chain("qp", h)
                nc.vector.reciprocal(q[:, :], eq[:, :]).then_inc(vector_done, 1)
                chain("qr", h)
                nc.vector.scalar_tensor_tensor(q[:, :], q_raw[:, :], HG_DIM ** -0.5, q[:, :], ALU.mult, ALU.mult).then_inc(vector_done, 1)
                chain("b", h)
                nc.vector.tensor_tensor(kd[:, :, :], b[:, :, P - 1:P].broadcast_to([P, TB, P]), b[:, :, :], ALU.subtract).then_inc(vector_done, 1)
                dve.wait_ge(scalar_done, A.after("kd_exp", h))
                nc.vector.tensor_tensor(flat(kd[:, :, :]), flat(kd[:, :, :]), key[:, :], ALU.mult).then_inc(vector_done, 1)
                chain("q", h)
                nc.vector.tensor_tensor(flat(qd[:, :, :]), flat(qd[:, :, :]), q[:, :], ALU.mult).then_inc(vector_done, 1)
                def diff(n):
                    m = LEVELS[n]
                    xv = x[:, n % XR, :].rearrange("p (b s) -> p b s", s=2 * m)
                    bv = flat(b[:, :, :]).rearrange("p (b s) -> p b s", s=2 * m)
                    nc.vector.tensor_tensor(xv, bv, bv[:, :, m - 1:m].broadcast_to([P, T // (2 * m), 2 * m]), ALU.subtract).then_inc(vector_done, 1)

                def decayed(n):
                    m = LEVELS[n]
                    xs = x[:, n % XR, :].rearrange("p (b s m) -> p b s m", s=2, m=m)
                    ks = key[:, :].rearrange("p (b s m) -> p b s m", s=2, m=m)
                    qs = q[:, :].rearrange("p (b s m) -> p b s m", s=2, m=m)
                    dve.wait_ge(scalar_done, A.after(("decay_left", n), h))
                    nc.vector.tensor_tensor(xs[:, :, 0, :], xs[:, :, 0, :], ks[:, :, 0, :], ALU.mult).then_inc(vector_done, 1)
                    dve.wait_ge(scalar_done, A.after(("decay_right", n), h))
                    nc.vector.tensor_tensor(xs[:, :, 1, :], xs[:, :, 1, :], qs[:, :, 1, :], ALU.mult).then_inc(vector_done, 1)

                diff(0)
                diff(1)
                dve.wait_ge(tensor_done, E.after("same", h))
                nc.vector.tensor_tensor(scores[:, :, :], big[0][:, :, :].rearrange("p a (b t) -> p (a b) t", t=P),
                                        bc(core.level_mask(NL), 1, [P, TB, P]), ALU.mult).then_inc(vector_done, 1)
                decayed(0)
                for n in range(NL):
                    if n + 1 < NL:
                        decayed(n + 1)
                    if n + 2 < NL:
                        diff(n + 2)
                    dve.wait_ge(tensor_done, E.after(("level", n), h))
                    if n >= 2:
                        dve.wait_ge(pool_done, G.after(("sum", n - 2), h))
                    nc.vector.tensor_tensor(masked[:, n % 2, :].rearrange("p (b t) -> p b t", t=P),
                                            big[(n + 1) % 2][:, :, :].rearrange("p a (b t) -> p (a b) t", t=P),
                                            bc(core.level_mask(n), 1, [P, TB, P]), ALU.mult).then_inc(vector_done, 1)
                    if n == 0:
                        dve.wait_ge(tensor_done, E.after("dstate", h))
                        dve.wait_ge(scalar_done, A.after("chunk_decay", h))
                        for c in range(1, TB):
                            own = big[3][:, (c - 1) // 4, ((c - 1) % 4) * P:((c - 1) % 4 + 1) * P]
                            if c == 1:
                                nc.vector.tensor_copy(state[:, c, :], own).then_inc(vector_done, 1)
                            else:
                                chain(("state", c - 1), h)
                                nc.vector.scalar_tensor_tensor(state[:, c, :], state[:, c - 1, :], ebl[:, c - 1:c], own, ALU.mult, ALU.add).then_inc(vector_done, 1)
                gatef = flat(gate[:, :, :])
                dve.wait_ge(scalar_done, A.after("g_raw", h))
                nc.vector.tensor_scalar(gatef, gatef, 1.0, None, ALU.add).then_inc(vector_done, 1)
                chain("gp", h)
                nc.vector.reciprocal(gatef, gatef).then_inc(vector_done, 1)
                chain("gr", h)
                nc.vector.tensor_tensor(gatef, gatef, g_raw[:, :], ALU.mult).then_inc(vector_done, 1)
                dve.wait_ge(scalar_done, A.after("square", h))
                nc.vector.tensor_reduce(ss[:, 0:TB], logf[:, :].rearrange("p (b d) -> p b d", d=P), AXX, ALU.add).then_inc(vector_done, 1)
                dve.wait_ge(scalar_done, A.after("std", h))
                nc.vector.reciprocal(ss[:, 2 * TB:3 * TB], ss[:, TB:2 * TB]).then_inc(vector_done, 1)
                chain("rstd", h)
                nc.vector.tensor_tensor(y[:, :, :], big[0][:, :, :].rearrange("p a (b t) -> p (a b) t", t=P),
                                        bc(ss[:, 2 * TB:3 * TB], 2, [P, TB, P]), ALU.mult).then_inc(vector_done, 1)
                chain("y_rstd", h)
                nc.vector.tensor_tensor(y[:, :, :], y[:, :, :], gate[:, :, :], ALU.mult).then_inc(vector_done, 1)

        @block.gpsimd
        def _(pool):
            pool.sem_inc(pool_done, 1)
            with pool.Fori(0, HG_HEADS) as h:
                for n in range(NL):
                    if n:
                        pool.wait_ge(pool_done, G.after(("sum", n - 1), h))
                    pool.wait_ge(vector_done, V.after(("masked", n), h))
                    nc.gpsimd.tensor_tensor(flat(scores[:, :, :]), flat(scores[:, :, :]), masked[:, n % 2, :], ALU.add).then_inc(pool_done, 1)


class SsdWeights:

    def __init__(self, nc, ctx, w_in):
        self.w_in = kc_view(w_in)
        self.x, self.z, self.bc, self.dt = (ctx.enter_context(nc.sbuf_tensor(f"ssd_w{name}", [P, KC, columns], F32)) for name, columns in
                                            (("x", SSD_GW), ("z", SSD_GW), ("bc", 2 * SSD_STATE), ("dt", SSD_HEADS)))
        self.loaded = {n: ctx.enter_context(nc.semaphore(f"ssd_w{n}_loaded")) for n in ("x", "bc", "z", "dt")}

    def load(self, sp, g):
        sp.dma_start(self.x[:, :, :], self.w_in[:, :, bass.ds(g * SSD_GW + COL_X, SSD_GW)]).then_inc(self.loaded["x"], 16)
        for n, col in enumerate((COL_B, COL_C)):
            sp.dma_start(self.bc[:, :, n * SSD_STATE:(n + 1) * SSD_STATE],
                         self.w_in[:, :, bass.ds(g * SSD_STATE + col, SSD_STATE)]).then_inc(self.loaded["bc"], 16)
        sp.dma_start(self.z[:, :, :], self.w_in[:, :, bass.ds(g * SSD_GW + COL_Z, SSD_GW)]).then_inc(self.loaded["z"], 16)

    def load_first(self, sp):
        sp.dma_start(self.dt[:, :, :], self.w_in[:, :, COL_DT:COL_DT + SSD_HEADS]).then_inc(self.loaded["dt"], 16)
        self.load(sp, 0)


def ssd(nc, core, weights, conv_wb, head_rows, norm_w, hT, yssdT):
    HW, XC = SSD_HPG, SSD_GW // P
    GN = SSD_STATE
    NCV = XC + 1
    PAD = SSD_CONV - 1
    with ExitStack() as ctx:
        sb, ps, sem = stage_tools(nc, ctx, "ssd")
        wx, wz, wbc, wdt = weights.x, weights.z, weights.bc, weights.dt
        cw = sb("conv_w", [P, NCV, SSD_CONV + 1])
        cw_all = sb("conv_w_all", [P, SSD_GROUPS, NCV, SSD_CONV + 1])
        skip = sb("skip", [P, HW])
        rows_all = sb("rows_all", [P, 3, SSD_HEADS])
        nw = sb("norm_w", [P, SSD_GROUPS * XC])
        raw = sb("raw", [P, NCV, T + PAD])
        conv = sb("conv", [P, NCV, T])
        cT = sb("cT", [GN, T])
        sig = sb("sig", [P, 2 * XC, T])
        xs = sb("xs", [P, TB, SSD_GW])
        xdt = sig[:, 0:XC, :].rearrange("p u (b h d) -> p (u b) h d", h=HW, d=SSD_DIM)
        xdd = sig[:, XC:2 * XC, :].rearrange("p u (b h d) -> p (u b) h d", h=HW, d=SSD_DIM)
        dtT = raw[0:SSD_HEADS, 1, PAD:PAD + T]
        z_raw = [raw[:, i // 2, PAD + (i % 2) * HALF:PAD + (i % 2 + 1) * HALF] for i in range(4)]
        bn = sb("bn", [P, TB, GN])
        z = sb("z", [P, TB, SSD_GW])
        y = sb("y", [P, TB, HW, SSD_DIM])
        dt_all = sb("dt_all", [P, 3, TB, SSD_HEADS])
        a_all = sb("a_all", [P, TB, SSD_HEADS])
        decay_all = sb("decay_all", [P, 3, TB, SSD_HEADS])
        rate = sb("rate", [P, SSD_HEADS])
        dt = sb("dt", [P, TB, HW])
        a = sb("a", [P, TB, HW])
        decay = sb("decay", [P, 3, TB, HW])
        seg = sb("seg", [P, 2, HW, P])
        cbm = sb("cbm", [P, TB, P])
        sc = sb("sc", [P, 2, HW, P])
        state = sb("state", [GN, TB, SSD_GW])
        ss = sb("ss", [P, 3, TB])
        bank = [ps(f"bank{i}", [P, HALF]) for i in range(8)]
        w_sem = weights.loaded
        rows_in = sem("rows_in")
        tensor_done, scalar_done, vector_done = sem("tensor_done"), sem("scalar_done"), sem("vector_done")
        pads_set = sem("pads_set")
        dt_done = {n: sem(f"dt_{n}") for n in ("projected", "copied", "turned", "summed", "rate", "biased", "abs", "exp", "ln", "made", "a", "decays")}

        SMALL = 16 * (3 * SSD_GROUPS + 2)
        halves = [(u, half) for u in range(NCV) for half in range(2)]
        Z_AT = {1: 0, 2: 1, 5: 2, 6: 3}
        E = Steps(*[("in", u) for u in halves], ("z", 0), ("z", 1),
                  *[("xs", i) for i in range(4)], "cb0", "cb1", "bn",
                  *[("own", i) for i in range(4)],
                  ("seg", 0), *[s for c in range(1, TB) for s in [("seg", c), ("y", c - 1)] + [("z", c // 2 + 1)] * (c in (2, 4))], ("y", TB - 1), *[("yT", i) for i in range(XC)])
        def by_unit(taps, silu):
            return [s for u in range(NCV + 1) for s in (taps(u) if u < NCV else []) + (silu(u - 1) if u else [])]

        V = Steps("taps", "skip_row", "dt_row", "a_row", "decay_row",
                  *by_unit(lambda u: [("tap", u, j) for j in range(SSD_CONV)], lambda u: [("sp", u), ("sr", u), ("silu", u)]),
                  "cbm0", "cbm1", "xdt", "xdd",
                  *[s for c in range(1, TB) for s in (("state_decay", c), ("state", c))][1:],
                  *[("tri", 0, h) for h in range(HW)],
                  *[s for c in range(TB) for s in [("tri", c + 1, h) for h in range(HW) if c + 1 < TB] + [("sc", c)]
                    + [("y_off", c)] * (c > 0) + [("y", c)]
                    + [(s, Z_AT[c]) for s in ("zp", "zr", "z") if c in Z_AT]],
                  "skip", "y_skip", "gated", "square", "ss", "rstd", "y_norm")
        A = Steps(*by_unit(lambda u: [("in", (u, half)) for half in range(2)], lambda u: [("conv_exp", u)]),
                  *[(s, i) for i in range(2) for s in ("z_exp", "z_raw")],
                  *[("xs", i) for i in range(4)], "cT", "bn",
                  *[s for c in range(TB) for s in [("seg", c)] + [(s, c // 2 + 1) for s in ("z_exp", "z_raw")] * (c in (3, 5))], "std", *[("yT", i) for i in range(XC)])
        block = ctx.enter_context(nc.Block())

        @block.sync
        def _(sp):
            for g in range(SSD_GROUPS):
                sp.dma_start(cw_all[:, g, 0:XC, :], conv_wb[g * SSD_GW:(g + 1) * SSD_GW, :].rearrange("(u p) j -> p u j", p=P)).then_inc(rows_in, 16)
                for n in range(2):
                    row = SSD_W + (n * SSD_GROUPS + g) * GN
                    sp.dma_start(cw_all[n * GN:(n + 1) * GN, g, XC, :], conv_wb[row:row + GN, :]).then_inc(rows_in, 16)
            sp.dma_start(rows_all[:, :, :], head_rows.broadcast_to([P, 3, SSD_HEADS])).then_inc(rows_in, 16)
            sp.dma_start(nw[:, :], norm_w).then_inc(rows_in, 16)

            with sp.Fori(1, SSD_GROUPS) as g:
                sp.wait_ge(tensor_done, E.after(("z", 3), g - 1))
                weights.load(sp, g)

        @block.tensor
        def _(pe):
            pe.sem_inc(tensor_done, 1)
            pe.wait_ge(w_sem["dt"], 16)
            for half in range(2):
                for k in range(KC):
                    last = nc.tensor.matmul(bank[5 + 2 * half][0:SSD_HEADS, :], wdt[:, k, :], hT[:, k, half * HALF:(half + 1) * HALF],
                                            start=k == 0, stop=k == KC - 1)
                last.then_inc(dt_done["projected"], 1)
            pe.wait_ge(dt_done["copied"], 2)
            for tb in range(TB):
                last = nc.tensor.transpose(bank[7][:, tb * SSD_HEADS:(tb + 1) * SSD_HEADS], dtT[:, tb * P:(tb + 1) * P],
                                           core.const("ident")[0:SSD_HEADS, 0:SSD_HEADS])
            last.then_inc(dt_done["turned"], 1)
            pe.wait_ge(dt_done["a"], 1)
            for n, tri in enumerate(("upto", "beyond", "ones")):
                last = nc.tensor.matmul(bank[6][:, n * TB * SSD_HEADS:(n + 1) * TB * SSD_HEADS], core.const(tri),
                                        a_all[:, :, :].rearrange("p b h -> p (b h)"), start=True, stop=True)
            last.then_inc(dt_done["summed"], 1)
            with pe.Fori(0, SSD_GROUPS) as g:
                pe.wait_ge(scalar_done, A.passes(g))
                pe.wait_ge(vector_done, V.passes(g))
                for n, (u, half) in enumerate(halves):
                    if half == 0:
                        pe.wait_ge(w_sem["x" if u < XC else "bc"], g * 16 + 16 if u < XC else g * 32 + 32)
                    for k in range(KC):
                        w = wx[:, k, u * P:(u + 1) * P] if u < XC else wbc[:, k, :]
                        last = nc.tensor.matmul(bank[n][:, :], w, hT[:, k, half * HALF:(half + 1) * HALF], start=k == 0, stop=k == KC - 1)
                    last.then_inc(tensor_done, 1)
                pe.wait_ge(w_sem["z"], g * 16 + 16)
                def project_z(i, tb):
                    for k in range(KC):
                        last = nc.tensor.matmul(bank[1 + i % 2][:, (tb % 2) * SSD_GW:(tb % 2 + 1) * SSD_GW], hT[:, k, tb * P:(tb + 1) * P],
                                                wz[:, k, :], start=k == 0, stop=k == KC - 1)
                    if tb % 2:
                        last.then_inc(tensor_done, 1)

                for i in range(2):
                    pe.wait_ge(scalar_done, A.after(("in", halves[1 + i]), g))
                    project_z(i, 2 * i)
                    project_z(i, 2 * i + 1)
                for i in range(4):
                    if i == 0:
                        pe.wait_ge(vector_done, V.after(("silu", XC - 1), g))
                    if i >= 2:
                        pe.wait_ge(scalar_done, A.after(("xs", i - 2), g))
                    for tb in (2 * i, 2 * i + 1):
                        for u in range(XC):
                            at = (tb % 2) * SSD_GW + u * P
                            last = nc.tensor.transpose(bank[6 + i % 2][:, at:at + P], conv[:, u, tb * P:(tb + 1) * P], core.const("ident"))
                    last.then_inc(tensor_done, 1)
                pe.wait_ge(vector_done, V.after(("silu", XC), g))
                pe.wait_ge(scalar_done, A.after("cT", g))
                for i in range(2):
                    for c in range(4 * i, 4 * i + 4):
                        last = nc.tensor.matmul(bank[6 + i][:, (c % 4) * P:(c % 4 + 1) * P], conv[0:GN, XC, c * P:(c + 1) * P],
                                                cT[:, c * P:(c + 1) * P], start=True, stop=True)
                    last.then_inc(tensor_done, 1)
                for tb in range(TB):
                    last = nc.tensor.transpose(bank[0][:, tb * GN:(tb + 1) * GN], conv[0:GN, XC, tb * P:(tb + 1) * P], core.const("ident")[0:GN, 0:GN])
                last.then_inc(tensor_done, 1)
                pe.wait_ge(vector_done, V.after("xdd", g))
                pe.wait_ge(scalar_done, A.after("bn", g))
                for i in range(4):
                    for c in (2 * i, 2 * i + 1):
                        last = nc.tensor.matmul(bank[1 + i][0:GN, (c % 2) * SSD_GW:(c % 2 + 1) * SSD_GW], bn[:, c, :],
                                                xdd[:, c, :, :].rearrange("p h d -> p (h d)"), start=True, stop=True)
                    last.then_inc(tensor_done, 1)
                for c in range(TB + 1):
                    if c < TB:
                        if c >= 2:
                            pe.wait_ge(scalar_done, A.after(("seg", c - 2), g))
                        pe.wait_ge(vector_done, V.after(("tri", c, HW - 1), g))
                        for h in range(HW):
                            last = nc.tensor.matmul(bank[(0, 5)[c % 2]][:, h * P:(h + 1) * P], seg[:, c % 2, h, :], core.const("upto"), start=True, stop=True)
                        last.then_inc(tensor_done, 1)
                    if c >= 1:
                        r = c - 1
                        pe.wait_ge(vector_done, V.after(("sc", r), g))
                        if r >= 2:
                            pe.wait_ge(vector_done, V.after(("y", r - 2), g))
                        yb = bank[6 + r % 2]
                        for h in range(HW):
                            last = nc.tensor.matmul(yb[:, h * SSD_DIM:(h + 1) * SSD_DIM], sc[:, r % 2, h, :], xdt[:, r, h, :], start=True, stop=True)
                        if r >= 1:
                            last = nc.tensor.matmul(yb[:, SSD_GW:2 * SSD_GW], cT[:, r * P:(r + 1) * P], state[:, r, :], start=True, stop=True)
                        last.then_inc(tensor_done, 1)
                    if 1 <= c <= 4:
                        project_z((c + 3) // 2, c + 3)
                pe.wait_ge(vector_done, V.after("y_norm", g))
                pe.wait_ge(scalar_done, A.after(("z_raw", 3), g))
                for u in range(XC):
                    for tb in range(TB):
                        last = nc.tensor.transpose(bank[1 + 2 * u + tb // 4][:, (tb % 4) * P:(tb % 4 + 1) * P],
                                                   y[:, tb, 2 * u:2 * u + 2, :].rearrange("p h d -> p (h d)"), core.const("ident"))
                    last.then_inc(tensor_done, 1)

        @block.scalar
        def _(act):
            act.sem_inc(scalar_done, 1)
            nc.scalar.preload_act_table_set(LOG_EXP)
            act.wait_ge(pads_set, 1)
            act.wait_ge(rows_in, SMALL)
            for half in range(2):
                act.wait_ge(dt_done["projected"], half + 1)
                nc.scalar.copy(dtT[:, half * HALF:(half + 1) * HALF], bank[5 + 2 * half][0:SSD_HEADS, :]).then_inc(dt_done["copied"], 1)
            nc.scalar.activation(rate[:, :], rows_all[:, 1, :], ACT.Exp).then_inc(dt_done["rate"], 1)
            act.wait_ge(dt_done["biased"], 1)
            nc.scalar.activation(dt_all[:, 1, :, :], dt_all[:, 0, :, :], ACT.Abs).then_inc(dt_done["abs"], 1)
            act.wait_ge(dt_done["abs"], 1)
            nc.scalar.activation(dt_all[:, 1, :, :], dt_all[:, 1, :, :], ACT.Exp, scale=-1.0).then_inc(dt_done["exp"], 1)
            act.wait_ge(dt_done["exp"], 1)
            nc.scalar.activation(dt_all[:, 1, :, :], dt_all[:, 1, :, :], ACT.Ln, bias=1.0).then_inc(dt_done["ln"], 1)
            act.wait_ge(dt_done["summed"], 1)
            nc.scalar.activation(decay_all[:, :, :, :].rearrange("p s b h -> p (s b h)"), bank[6][:, 0:3 * TB * SSD_HEADS], ACT.Exp).then_inc(dt_done["decays"], 1)
            with act.Fori(0, SSD_GROUPS) as g:
                for u in range(NCV + 1):
                    for half in range(2):
                        if u < NCV:
                            act.wait_ge(tensor_done, E.after(("in", (u, half)), g))
                            nc.scalar.copy(raw[:, u, PAD + half * HALF:PAD + (half + 1) * HALF], bank[2 * u + half][:, :]).then_inc(scalar_done, 1)
                    if u:
                        act.wait_ge(vector_done, V.after(("tap", u - 1, SSD_CONV - 1), g))
                        nc.scalar.activation(sig[:, u - 1, :], conv[:, u - 1, :], ACT.Exp, scale=-1.0).then_inc(scalar_done, 1)

                def take_z(i):
                    act.wait_ge(tensor_done, E.after(("z", i), g))
                    quarter = slice(2 * i, 2 * i + 2)
                    nc.scalar.activation(z[:, quarter, :].rearrange("p b d -> p (b d)"), bank[1 + i % 2][:, :], ACT.Exp, scale=-1.0).then_inc(scalar_done, 1)
                    nc.scalar.copy(z_raw[i], bank[1 + i % 2][:, :]).then_inc(scalar_done, 1)

                for i in range(2):
                    take_z(i)
                for i in range(4):
                    act.wait_ge(tensor_done, E.after(("xs", i), g))
                    nc.scalar.copy(xs[:, 2 * i:2 * i + 2, :].rearrange("p b d -> p (b d)"), bank[6 + i % 2][:, :]).then_inc(scalar_done, 1)
                act.wait_ge(vector_done, V.after(("silu", XC), g))
                nc.scalar.copy(cT[:, :], conv[GN:2 * GN, XC, :]).then_inc(scalar_done, 1)
                act.wait_ge(tensor_done, E.after("bn", g))
                nc.scalar.copy(bn[:, :, :].rearrange("p b n -> p (b n)"), bank[0][:, :]).then_inc(scalar_done, 1)
                for c in range(TB):
                    act.wait_ge(tensor_done, E.after(("seg", c), g))
                    if c >= 2:
                        act.wait_ge(tensor_done, E.after(("y", c - 2), g))
                    nc.scalar.activation(sc[:, c % 2, :, :].rearrange("p h t -> p (h t)"), bank[(0, 5)[c % 2]][:, :], ACT.Exp).then_inc(scalar_done, 1)
                    if c in (3, 5):
                        take_z(c // 2 + 1)
                act.wait_ge(vector_done, V.after("ss", g))
                nc.scalar.activation(ss[:, 1, :], ss[:, 0, :], ACT.Sqrt, scale=1.0 / SSD_GW, bias=core.eps[:, :]).then_inc(scalar_done, 1)
                for u in range(XC):
                    act.wait_ge(tensor_done, E.after(("yT", u), g))
                    for half in range(2):
                        last = nc.scalar.activation(yssdT[:, bass.ds(g * XC + u, 1), half * HALF:(half + 1) * HALF].rearrange("p c t -> p (c t)"),
                                                    bank[1 + 2 * u + half][:, :], ACT.Copy, scale=nw[:, bass.ds(g * XC + u, 1)])
                    last.then_inc(scalar_done, 1)

        @block.vector
        def _(dve):
            dve.sem_inc(vector_done, 1)
            nc.vector.memset(raw[:, :, 0:PAD], 0.0).then_inc(pads_set, 1)
            dve.wait_ge(rows_in, SMALL)
            dve.wait_ge(dt_done["turned"], 1)
            nc.vector.tensor_tensor(dt_all[:, 0, :, :], bank[7][:, 0:TB * SSD_HEADS].rearrange("p (b h) -> p b h", h=SSD_HEADS),
                                    bc(rows_all[:, 0, :], 1, [P, TB, SSD_HEADS]), ALU.add).then_inc(dt_done["biased"], 1)
            dve.wait_ge(dt_done["ln"], 1)
            nc.vector.scalar_tensor_tensor(dt_all[:, 2, :, :], dt_all[:, 0, :, :], 0.0, dt_all[:, 1, :, :], ALU.max, ALU.add).then_inc(dt_done["made"], 1)
            dve.wait_ge(dt_done["made"], 1)
            dve.wait_ge(dt_done["rate"], 1)
            nc.vector.scalar_tensor_tensor(a_all[:, :, :], dt_all[:, 2, :, :], -1.0, bc(rate[:, :], 1, [P, TB, SSD_HEADS]), ALU.mult, ALU.mult).then_inc(dt_done["a"], 1)
            dve.wait_ge(dt_done["a"], 1)
            dve.wait_ge(dt_done["decays"], 1)
            with dve.Fori(0, SSD_GROUPS) as g:
                def chain(name):
                    dve.wait_ge(vector_done, V.after(name, g))

                nc.vector.tensor_copy(cw[:, :, :], cw_all[:, bass.ds(g, 1), :, :].rearrange("p g u j -> p (g u) j")).then_inc(vector_done, 1)
                heads = bass.ds(g * HW, HW)
                nc.vector.tensor_copy(skip[:, :], rows_all[:, 2, heads]).then_inc(vector_done, 1)
                nc.vector.tensor_copy(dt[:, :, :], dt_all[:, 2, :, heads]).then_inc(vector_done, 1)
                nc.vector.tensor_copy(a[:, :, :], a_all[:, :, heads]).then_inc(vector_done, 1)
                nc.vector.tensor_copy(decay[:, :, :, :].rearrange("p s b h -> p (s b) h"),
                                      decay_all[:, :, :, heads].rearrange("p s b h -> p (s b) h")).then_inc(vector_done, 1)
                chain("decay_row")
                for u in range(NCV + 1):
                    if u < NCV:
                        dve.wait_ge(scalar_done, A.after(("in", (u, 1)), g))
                        nc.vector.tensor_scalar(conv[:, u, :], raw[:, u, 0:T], cw[:, u, 0:1], cw[:, u, SSD_CONV:SSD_CONV + 1],
                                                ALU.mult, ALU.add).then_inc(vector_done, 1)
                        for j in range(1, SSD_CONV):
                            chain(("tap", u, j - 1))
                            nc.vector.scalar_tensor_tensor(conv[:, u, :], raw[:, u, j:j + T], cw[:, u, j:j + 1], conv[:, u, :],
                                                           ALU.mult, ALU.add).then_inc(vector_done, 1)
                    if u:
                        r = u - 1
                        dve.wait_ge(scalar_done, A.after(("conv_exp", r), g))
                        nc.vector.tensor_scalar(sig[:, r, :], sig[:, r, :], 1.0, None, ALU.add).then_inc(vector_done, 1)
                        chain(("sp", r))
                        nc.vector.reciprocal(sig[:, r, :], sig[:, r, :]).then_inc(vector_done, 1)
                        chain(("sr", r))
                        nc.vector.tensor_tensor(conv[:, r, :], conv[:, r, :], sig[:, r, :], ALU.mult).then_inc(vector_done, 1)
                for i in range(2):
                    dve.wait_ge(tensor_done, E.after(f"cb{i}", g))
                    nc.vector.tensor_tensor(cbm[:, 4 * i:4 * i + 4, :], bank[6 + i][:, :].rearrange("p (c t) -> p c t", t=P),
                                            bc(core.const("upto"), 1, [P, 4, P]), ALU.mult).then_inc(vector_done, 1)
                dve.wait_ge(scalar_done, A.after(("xs", 3), g))
                nc.vector.tensor_tensor(xdt[:, :, :, :].rearrange("p b h d -> p (b h) d"), xs[:, :, :].rearrange("p b (h d) -> p (b h) d", d=SSD_DIM),
                                        bc(dt[:, :, :].rearrange("p b h -> p (b h)"), 2, [P, TB * HW, SSD_DIM]), ALU.mult).then_inc(vector_done, 1)
                chain("xdt")
                nc.vector.tensor_tensor(xdd[:, :, :, :].rearrange("p b h d -> p (b h) d"), xdt[:, :, :, :].rearrange("p b h d -> p (b h) d"),
                                        bc(decay[:, 1, :, :].rearrange("p b h -> p (b h)"), 2, [P, TB * HW, SSD_DIM]), ALU.mult).then_inc(vector_done, 1)
                for c in range(1, TB):
                    own = bank[1 + (c - 1) // 2][0:GN, ((c - 1) % 2) * SSD_GW:((c - 1) % 2 + 1) * SSD_GW]
                    dve.wait_ge(tensor_done, E.after(("own", (c - 1) // 2), g))
                    if c == 1:
                        nc.vector.tensor_copy(state[:, c, :], own).then_inc(vector_done, 1)
                    else:
                        chain(("state", c - 1))
                        nc.vector.tensor_tensor(state[:, c, :].rearrange("p (h d) -> p h d", d=SSD_DIM),
                                                state[:, c - 1, :].rearrange("p (h d) -> p h d", d=SSD_DIM),
                                                bc(decay[0:GN, 2, c - 1, :], 2, [GN, HW, SSD_DIM]), ALU.mult).then_inc(vector_done, 1)
                        chain(("state_decay", c))
                        nc.vector.tensor_tensor(state[:, c, :], state[:, c, :], own, ALU.add).then_inc(vector_done, 1)

                def gate_z(i):
                    quarter = slice(2 * i, 2 * i + 2)
                    dve.wait_ge(scalar_done, A.after(("z_raw", i), g))
                    nc.vector.tensor_scalar(z[:, quarter, :], z[:, quarter, :], 1.0, None, ALU.add).then_inc(vector_done, 1)
                    chain(("zp", i))
                    nc.vector.reciprocal(z[:, quarter, :], z[:, quarter, :]).then_inc(vector_done, 1)
                    chain(("zr", i))
                    nc.vector.tensor_tensor(z[:, quarter, :].rearrange("p b d -> p (b d)"), z[:, quarter, :].rearrange("p b d -> p (b d)"), z_raw[i], ALU.mult).then_inc(vector_done, 1)

                def below_diagonal(c):
                    if c >= 2:
                        dve.wait_ge(tensor_done, E.after(("seg", c - 2), g))
                    for h in range(HW):
                        nc.vector.tensor_scalar(seg[:, c % 2, h, :], core.const("beyond"), a[:, c, h:h + 1], None, ALU.mult).then_inc(vector_done, 1)

                below_diagonal(0)
                for c in range(TB):
                    if c + 1 < TB:
                        below_diagonal(c + 1)
                    dve.wait_ge(scalar_done, A.after(("seg", c), g))
                    nc.vector.tensor_tensor(sc[:, c % 2, :, :], sc[:, c % 2, :, :], bc(cbm[:, c, :], 1, [P, HW, P]), ALU.mult).then_inc(vector_done, 1)
                    dve.wait_ge(tensor_done, E.after(("y", c), g))
                    yb = bank[6 + c % 2]
                    if c:
                        nc.vector.tensor_tensor(y[:, c, :, :], yb[:, SSD_GW:2 * SSD_GW].rearrange("p (h d) -> p h d", d=SSD_DIM),
                                                bc(decay[:, 0, c, :], 2, [P, HW, SSD_DIM]), ALU.mult).then_inc(vector_done, 1)
                        chain(("y_off", c))
                        nc.vector.tensor_tensor(y[:, c, :, :], y[:, c, :, :], yb[:, 0:SSD_GW].rearrange("p (h d) -> p h d", d=SSD_DIM), ALU.add).then_inc(vector_done, 1)
                    else:
                        nc.vector.tensor_copy(y[:, c, :, :], yb[:, 0:SSD_GW].rearrange("p (h d) -> p h d", d=SSD_DIM)).then_inc(vector_done, 1)
                    if c in Z_AT:
                        gate_z(Z_AT[c])
                nc.vector.tensor_tensor(xdd[:, :, :, :], xs[:, :, :].rearrange("p b (h d) -> p b h d", d=SSD_DIM),
                                        skip[:, :].unsqueeze(1).unsqueeze(3).broadcast_to([P, TB, HW, SSD_DIM]), ALU.mult).then_inc(vector_done, 1)
                chain("skip")
                nc.vector.tensor_tensor(y[:, :, :, :], y[:, :, :, :], xdd[:, :, :, :], ALU.add).then_inc(vector_done, 1)
                yf = y[:, :, :, :].rearrange("p b h d -> p b (h d)")
                chain("y_skip")
                nc.vector.tensor_tensor(yf, yf, z[:, :, :], ALU.mult).then_inc(vector_done, 1)
                chain("gated")
                nc.vector.tensor_tensor(xdd[:, :, :, :].rearrange("p b h d -> p b (h d)"), yf, yf, ALU.mult).then_inc(vector_done, 1)
                chain("square")
                nc.vector.tensor_reduce(ss[:, 0, :], xdd[:, :, :, :].rearrange("p b h d -> p b (h d)"), AXX, ALU.add).then_inc(vector_done, 1)
                dve.wait_ge(scalar_done, A.after("std", g))
                nc.vector.reciprocal(ss[:, 2, :], ss[:, 1, :]).then_inc(vector_done, 1)
                chain("rstd")
                nc.vector.tensor_tensor(yf, yf, bc(ss[:, 2, :], 2, [P, TB, SSD_GW]), ALU.mult).then_inc(vector_done, 1)


def merge(nc, core, w_in, branch_w, hT, yT):
    NB, YC = 3, 4
    with ExitStack() as ctx:
        sb, ps, sem = stage_tools(nc, ctx, "mg")
        h = sb("h_parts", [P, 2, KC, T], F32R)
        w_whole = sb("wg", [P, 2, KC, P])
        wg = sb("wg_parts", [P, 2, 2, KC, P], F32R)
        wb = sb("wb", [P, 2, YC, P])
        RING = 4
        sig = sb("sig", [P, RING, HALF])
        part = sb("part", [P, 2, HALF])
        pg = [ps(f"pg{i}", [P, HALF]) for i in range(RING)]
        pb = [ps(f"pb{i}", [P, HALF]) for i in range(RING)]
        wg_in = [sem(f"wg{j}_in") for j in range(2)]
        wb_in = [sem(f"wb{j}_in") for j in range(2)]
        h_high, h_cut = sem("h_high"), sem("h_cut")
        tensor_done, scalar_done, vector_done, pool_done = (sem("tensor_done"), sem("scalar_done"), sem("vector_done"), sem("pool_done"))
        tiles = [(j, n) for j in range(2) for n in range(NB)]
        NT = len(tiles)
        units = [(j, n, half) for j, n in tiles for half in range(2)]
        E = Steps(*[(s, u) for u in units for s in ("gate", "branch")], open_passes=1)
        A = Steps(("high", 0), *[s for t in range(NT) for s in [("high", t + 1)] * (t + 1 < NT) + [units[2 * t], units[2 * t + 1]]])
        V = Steps(*[(s, u) for u in units for s in ("plus", "recip", "product") + ("sum",) * (u[1] > 0)])
        G = Steps(*range(NT))
        block = ctx.enter_context(nc.Block())
        wv_ = kc_view(w_in)
        wbv = branch_w.rearrange("n (k p) c -> n p k c", p=P)

        def two_before(i, t):
            return ((t - 2) % NT, i if t >= 2 else i - 1)

        @block.sync
        def _(sp):
            with sp.Fori(0, KC // 2) as i:
                for t, (j, n) in enumerate(tiles):
                    before, its_pass = two_before(i, t)
                    sp.wait_ge(tensor_done, E.after(("branch", units[2 * before + 1]), its_pass))
                    sp.dma_start(w_whole[:, t % 2, :, :], wv_[:, :, bass.ds(i * 2 * P + (COL_G + n * D + j * P), P)]).then_inc(wg_in[t % 2], 16)
                    sp.dma_start(wb[:, t % 2, :, :], wbv[n, :, :, bass.ds(i * 2 * P + j * P, P)]).then_inc(wb_in[t % 2], 16)

        @block.tensor
        def _(pe):
            pe.sem_inc(tensor_done, E.opening)
            pe.wait_ge(h_cut, KC)
            with pe.Fori(0, KC // 2) as i:
                for x, (j, n, half) in enumerate(units):
                    ts = slice(half * HALF, (half + 1) * HALF)
                    r, t = x % RING, x // 2
                    if half == 0:
                        pe.wait_ge(pool_done, G.after(t, i))
                    pe.wait_ge(vector_done, V.after(("product", units[x - RING]), i) if x >= RING else V.passes(i))
                    for k in range(KC):
                        last = product_of_parts(nc, pg[r][:, :], wg[:, t % 2, 0, k, :], wg[:, t % 2, 1, k, :], h[:, 0, k, ts], h[:, 1, k, ts],
                                                k == 0, k == KC - 1)
                    last.then_inc(tensor_done, 1)
                    if half == 0:
                        pe.wait_ge(wb_in[t % 2], i * (16 * NT // 2) + (t // 2 * 16 + 16))
                    for k in range(YC):
                        last = nc.tensor.matmul(pb[r][:, :], wb[:, t % 2, k, :], yT[n][:, k, ts], start=k == 0, stop=k == YC - 1)
                    last.then_inc(tensor_done, 1)

        @block.scalar
        def _(act):
            act.sem_inc(scalar_done, 1)
            for k in range(KC):
                nc.scalar.copy(h[:, 0, k, :], hT[:, k, :]).then_inc(h_high, 1)
            with act.Fori(0, KC // 2) as i:
                def high(t):
                    act.wait_ge(wg_in[t % 2], i * (16 * NT // 2) + (t // 2 * 16 + 16))
                    before, its_pass = two_before(i, t)
                    act.wait_ge(tensor_done, E.after(("gate", units[2 * before + 1]), its_pass))
                    nc.scalar.copy(wg[:, t % 2, 0, :, :], w_whole[:, t % 2, :, :]).then_inc(scalar_done, 1)

                high(0)
                for x, u in enumerate(units):
                    if x % 2 == 0 and x // 2 + 1 < NT:
                        high(x // 2 + 1)
                    act.wait_ge(tensor_done, E.after(("gate", u), i))
                    act.wait_ge(vector_done, V.after(("product", units[x - RING]), i) if x >= RING else V.passes(i))
                    nc.scalar.activation(sig[:, x % RING, :], pg[x % RING][:, :], ACT.Exp, scale=-1.0).then_inc(scalar_done, 1)

        @block.vector
        def _(dve):
            dve.sem_inc(vector_done, 1)
            for k in range(KC):
                dve.wait_ge(h_high, k + 1)
                nc.vector.tensor_tensor(h[:, 1, k, :], hT[:, k, :], h[:, 0, k, :].bitcast(F32), ALU.subtract).then_inc(h_cut, 1)
            dve.wait_ge(h_cut, KC)
            with dve.Fori(0, KC // 2) as i:
                for x, u in enumerate(units):
                    j, n, half = u
                    r = x % RING
                    dve.wait_ge(scalar_done, A.after(u, i))
                    nc.vector.tensor_scalar(sig[:, r, :], sig[:, r, :], 1.0, None, ALU.add).then_inc(vector_done, 1)
                    dve.wait_ge(vector_done, V.after(("plus", u), i))
                    nc.vector.reciprocal(sig[:, r, :], sig[:, r, :]).then_inc(vector_done, 1)
                    dve.wait_ge(vector_done, V.after(("recip", u), i))
                    dve.wait_ge(tensor_done, E.after(("branch", u), i))
                    merged = hT[:, bass.ds(i * 2 + j, 1), half * HALF:(half + 1) * HALF].rearrange("p c t -> p (c t)")
                    nc.vector.tensor_tensor(part[:, half, :] if n else merged, sig[:, r, :], pb[r][:, :], ALU.mult).then_inc(vector_done, 1)
                    if n:
                        dve.wait_ge(vector_done, V.after(("product", u), i))
                        nc.vector.tensor_tensor(merged, merged, part[:, half, :], ALU.add).then_inc(vector_done, 1)

        @block.gpsimd
        def _(pool):
            pool.sem_inc(pool_done, G.opening)
            with pool.Fori(0, KC // 2) as i:
                for t in range(NT):
                    pool.wait_ge(scalar_done, A.after(("high", t), i))
                    nc.gpsimd.tensor_tensor(wg[:, t % 2, 1, :, :], w_whole[:, t % 2, :, :], wg[:, t % 2, 0, :, :].bitcast(F32), ALU.subtract).then_inc(pool_done, 1)


def output_and_norm(nc, core, x, w_out, norm_w, mergedT, acc, h2T, next_weights):
    with ExitStack() as ctx:
        sb, ps, sem = stage_tools(nc, ctx, "ou")
        w_whole = sb("w", [P, 2, D])
        wo = sb("w_parts", [P, 2, KC, D], F32R)
        mt = sb("merged_parts", [P, 2, 2, KC, P], F32R)
        xt = sb("x", [P, 2, D])
        squares = sb("squares", [P, D])
        xn = sb("xn", [P, 2, D])
        stat = sb("stat", [P, 2, 3])
        wcol = sb("wcol", [P, KC])
        po = [ps(f"po{i}", [P, 2, HALF]) for i in range(2)]
        turned = [ps(f"turned{i}", [P, KC, P]) for i in range(2)]
        w_sem = [sem(f"w{i}_in") for i in range(2)]
        x_in = [sem(f"x{i}_in") for i in range(2)]
        norm_in = sem("norm_in")
        tensor_done, scalar_done, vector_done, pool_done = (sem("tensor_done"), sem("scalar_done"), sem("vector_done"), sem("pool_done"))
        E = Steps(*[s for b in range(TB + 1) for s in [("out", b)] * (b < TB) + [("turned", b - 1)] * (b > 0)])
        first_cuts = [("m", 0), ("w", 0), ("w", 1), ("m", 1)] + [("w", k) for k in range(2, KC)]
        A = Steps(*first_cuts, *[s for b in range(TB) for s in [("squares", b), ("std", b)] + [("m", b + 2)] * (b + 2 < TB)])
        G = Steps(*first_cuts, *[("m", b) for b in range(2, TB)])
        V = Steps(*[(s, b) for b in range(TB) for s in ("sum", "rstd", "xn", "h0", "h1")])
        block = ctx.enter_context(nc.Block())
        xv = x.rearrange("(b p) d -> p b d", p=P)
        wov = kc_view(w_out)

        @block.sync
        def _(sp):
            sp.dma_start(wcol[:, :], norm_w).then_inc(norm_in, 16)
            for k in range(KC):
                if k >= 2:
                    sp.wait_ge(pool_done, G.after(("w", k - 2)))
                sp.dma_start(w_whole[:, k % 2, :], wov[:, k, :]).then_inc(w_sem[k % 2], 16)
                if k < 2:
                    sp.dma_start(xt[:, k, :], xv[:, k, :]).then_inc(x_in[k], 16)
            for b in range(2, TB):
                sp.wait_ge(vector_done, V.after(("sum", b - 2)))
                sp.dma_start(xt[:, b % 2, :], xv[:, b, :]).then_inc(x_in[b % 2], 16)
            next_weights.load(sp, 0)

        @block.tensor
        def _(pe):
            pe.sem_inc(tensor_done, 1)
            for b in range(TB + 1):
                if b < TB:
                    pe.wait_ge(pool_done, G.after(("m", b)))
                    if b >= 2:
                        pe.wait_ge(vector_done, V.after(("sum", b - 2)))
                    for k in range(KC):
                        if b == 0:
                            pe.wait_ge(pool_done, G.after(("w", k)))
                        for half in range(2):
                            span = slice(half * HALF, (half + 1) * HALF)
                            last = product_of_parts(nc, po[b % 2][:, half, :], mt[:, b % 2, 0, k, :], mt[:, b % 2, 1, k, :],
                                                    wo[:, 0, k, span], wo[:, 1, k, span], k == 0, k == KC - 1)
                    last.then_inc(tensor_done, 1)
                if b > 0:
                    r = b - 1
                    pe.wait_ge(vector_done, V.after(("xn", r)))
                    if r >= 2:
                        pe.wait_ge(vector_done, V.after(("h1", r - 2)))
                    for k in range(KC):
                        last = nc.tensor.transpose(turned[r % 2][:, k, :], xn[:, r % 2, k * P:(k + 1) * P], core.const("ident"))
                    last.then_inc(tensor_done, 1)

        @block.scalar
        def _(act):
            act.sem_inc(scalar_done, 1)

            def high(kind, n):
                if kind == "w":
                    act.wait_ge(w_sem[n % 2], 16 * (n // 2 + 1))
                    nc.scalar.copy(wo[:, 0, n, :], w_whole[:, n % 2, :]).then_inc(scalar_done, 1)
                else:
                    if n >= 2:
                        act.wait_ge(tensor_done, E.after(("out", n - 2)))
                    nc.scalar.copy(mt[:, n % 2, 0, :, :], mergedT[:, :, n * P:(n + 1) * P]).then_inc(scalar_done, 1)

            for kind, n in first_cuts:
                high(kind, n)
            for b in range(TB):
                act.wait_ge(vector_done, V.after(("sum", b)))
                nc.scalar.activation(squares[:, :], acc[:, b, :], ACT.Square, accum_out=stat[:, b % 2, 0:1]).then_inc(scalar_done, 1)
                act.wait_ge(scalar_done, A.after(("squares", b)))
                nc.scalar.activation(stat[:, b % 2, 1:2], stat[:, b % 2, 0:1], ACT.Sqrt, scale=1.0 / D, bias=core.eps[:, :]).then_inc(scalar_done, 1)
                if b + 2 < TB:
                    high("m", b + 2)

        @block.vector
        def _(dve):
            dve.sem_inc(vector_done, 1)
            dve.wait_ge(norm_in, 16)
            for b in range(TB):
                dve.wait_ge(x_in[b % 2], 16 * (b // 2 + 1))
                dve.wait_ge(tensor_done, E.after(("out", b)))
                nc.vector.tensor_tensor(acc[:, b, :], xt[:, b % 2, :], po[b % 2][:, :, :].rearrange("p a d -> p (a d)"), ALU.add).then_inc(vector_done, 1)
                dve.wait_ge(scalar_done, A.after(("std", b)))
                nc.vector.reciprocal(stat[:, b % 2, 2:3], stat[:, b % 2, 1:2]).then_inc(vector_done, 1)
                if b >= 2:
                    dve.wait_ge(tensor_done, E.after(("turned", b - 2)))
                dve.wait_ge(vector_done, V.after(("rstd", b)))
                nc.vector.tensor_scalar(xn[:, b % 2, :], acc[:, b, :], stat[:, b % 2, 2:3], None, ALU.mult).then_inc(vector_done, 1)
                dve.wait_ge(tensor_done, E.after(("turned", b)))
                for n in range(2):
                    ks = slice(4 * n, 4 * n + 4)
                    nc.vector.tensor_tensor(h2T[:, ks, b * P:(b + 1) * P], turned[b % 2][:, ks, :], bc(wcol[:, ks], 2, [P, 4, P]), ALU.mult).then_inc(vector_done, 1)

        @block.gpsimd
        def _(pool):
            pool.sem_inc(pool_done, 1)
            for kind, n in first_cuts + [("m", b) for b in range(2, TB)]:
                pool.wait_ge(scalar_done, A.after((kind, n)))
                if kind == "w":
                    nc.gpsimd.tensor_tensor(wo[:, 1, n, :], w_whole[:, n % 2, :], wo[:, 0, n, :].bitcast(F32), ALU.subtract).then_inc(pool_done, 1)
                else:
                    nc.gpsimd.tensor_tensor(mt[:, n % 2, 1, :, :], mergedT[:, :, n * P:(n + 1) * P], mt[:, n % 2, 0, :, :].bitcast(F32), ALU.subtract).then_inc(pool_done, 1)


def norm_output(nc, norm_row, acc, out):
    with ExitStack() as ctx:
        sb, ps, sem = stage_tools(nc, ctx, "no")
        wrow = sb("w", [P, D])
        squares = sb("squares", [P, D])
        stat = sb("stat", [P, 3, TB])
        scaled = sb("scaled", [P, 2, D])
        eps = sb("eps", [P, 1])
        eps_set = sem("eps_set")
        w_in_sem = sem("w_in")
        out_sem = [sem(f"out{i}") for i in range(2)]
        scalar_done, vector_done = sem("scalar_done"), sem("vector_done")
        A = Steps(*[(s, b) for b in range(TB) for s in ("squares", "std")])
        V = Steps(*[(s, b) for b in range(TB) for s in ("rstd", "out")])
        block = ctx.enter_context(nc.Block())

        @block.sync
        def _(sp):
            sp.dma_start(wrow[:, :], norm_row.broadcast_to([P, D])).then_inc(w_in_sem, 16)
            for b in range(TB):
                sp.wait_ge(vector_done, V.after(("out", b)))
                sp.dma_start(out[b * P:(b + 1) * P, :], scaled[:, b % 2, :]).then_inc(out_sem[b % 2], 16)
            for i in range(2):
                sp.wait_ge(out_sem[i], 16 * TB // 2)

        @block.scalar
        def _(act):
            act.sem_inc(scalar_done, 1)
            act.wait_ge(eps_set, 1)
            for b in range(TB):
                nc.scalar.activation(squares[:, :], acc[:, b, :], ACT.Square, accum_out=stat[:, 0, b:b + 1]).then_inc(scalar_done, 1)
                act.wait_ge(scalar_done, A.after(("squares", b)))
                nc.scalar.activation(stat[:, 1, b:b + 1], stat[:, 0, b:b + 1], ACT.Sqrt, scale=1.0 / D, bias=eps[:, :]).then_inc(scalar_done, 1)

        @block.vector
        def _(dve):
            dve.sem_inc(vector_done, 1)
            nc.vector.memset(eps[:, :], EPS).then_inc(eps_set, 1)
            dve.wait_ge(w_in_sem, 16)
            for b in range(TB):
                dve.wait_ge(scalar_done, A.after(("std", b)))
                nc.vector.reciprocal(stat[:, 2, b:b + 1], stat[:, 1, b:b + 1]).then_inc(vector_done, 1)
                dve.wait_ge(vector_done, V.after(("rstd", b)))
                if b >= 2:
                    dve.wait_ge(out_sem[b % 2], 16 * (b // 2))
                nc.vector.scalar_tensor_tensor(scaled[:, b % 2, :], acc[:, b, :], stat[:, 2, b:b + 1], wrow[:, :], ALU.mult, ALU.mult).then_inc(vector_done, 1)


class SelectWeights:

    def __init__(self, nc, ctx, w_q, keysT, room):
        self.w_q, self.keysT = kc_view(w_q), keysT
        self.w = room[:, 0:2, :].rearrange("p a (k c) -> p (a k) c", c=2 * P)
        self.keys = room[:, 2, 0:2 * KEYS].rearrange("p (s k) -> p s k", s=2)
        self.w_loaded = ctx.enter_context(nc.semaphore("select_w_loaded"))
        self.keys_loaded = ctx.enter_context(nc.semaphore("select_keys_loaded"))

    def load(self, sp, h):
        sp.dma_start(self.w, self.w_q[:, :, bass.ds(h * 2 * P, 2 * P)]).then_inc(self.w_loaded, 16)
        sp.dma_start(self.keys, self.keysT[bass.ds(h * 2, 2), :, :].rearrange("s d k -> d s k")).then_inc(self.keys_loaded, 16)


def peer_select(nc, core, weights, h2T, slot_row, slot_col, slot_gate):
    K = TOPK
    LAST = 7
    LOWEST = -3.0e38
    with ExitStack() as ctx:
        sb, ps, sem = stage_tools(nc, ctx, "se")
        w, keys, w_sem, keys_sem = weights.w, weights.keys, weights.w_loaded, weights.keys_loaded
        qT = sb("qT", [P, 2, T])
        s = sb("s", [P, 2, TB, 2, KEYS])
        rest = sb("rest", [P, 3, 2, KEYS])
        pace = sb("pace", [P, 1])
        pool_pace = sb("pool_pace", [P, 1])
        val = sb("val", [P, TB, 2, K])
        idx = sb("idx", [P, TB, 2, K], U32)
        pair = sb("pair", [P, 3, K * K])
        pair_rest = sb("pair_rest", [P, 3, K * K])
        top = sb("top", [P, TB, K])
        pos = sb("pos", [P, TB, K], U32)
        part = sb("part", [P, 2, TB * K], U32)
        partf = sb("partf", [P, 2, TB * K], BF16)
        idxf = sb("idxf", [P, 2, K, TB], BF16)
        hit = sb("hit", [P, 2, K, TB * K], BF16)
        rank_rows = sb("rank_rows", [P, K, TB * K], BF16)
        ex = sb("ex", [P, TB, K])
        total = sb("total", [P, 2, TB])
        pq = [ps(f"pq{i}", [P, HALF]) for i in range(4)]
        psc = [ps(f"psc{i}", [P, 2, 2, KEYS]) for i in range(4)]
        exp_done, rank_rows_set = sem("exp_done"), sem("rank_rows_set")
        tensor_done, scalar_done, vector_done, pool_done = (sem("tensor_done"), sem("scalar_done"), sem("vector_done"), sem("pool_done"))
        E = Steps(*[("q", i) for i in range(4)], *[("score", i) for i in range(4)])
        A = Steps(*[("q", i) for i in range(4)], *[("score", i) for i in range(4)])
        V = Steps(*[("rank", step) for step in range(TB + LAST)],
                  "shifted", "part0", "part1", "partf", "idxf", "equal0", "equal1", "sum", "recip", "gate")
        G = Steps(*[(step, p) for step in ("hit", K // 2, K // 4, K // 8, 1) for p in range(2)])
        block = ctx.enter_context(nc.Block())

        @block.sync
        def _(sp):
            with sp.Fori(1, PEER_HEADS) as h:
                sp.wait_ge(tensor_done, E.passes(h))
                weights.load(sp, h)

        @block.tensor
        def _(pe):
            pe.sem_inc(tensor_done, 1)
            with pe.Fori(0, PEER_HEADS) as h:
                pe.wait_ge(w_sem, h * 16 + 16)
                pe.wait_ge(scalar_done, A.passes(h))
                for i in range(4):
                    p, half = i // 2, i % 2
                    for k in range(KC):
                        last = nc.tensor.matmul(pq[i][:, :], w[:, k, p * P:(p + 1) * P], h2T[:, k, half * HALF:(half + 1) * HALF],
                                                start=k == 0, stop=k == KC - 1)
                    last.then_inc(tensor_done, 1)
                pe.wait_ge(keys_sem, h * 16 + 16)
                pe.wait_ge(scalar_done, A.after(("q", 3), h))
                for i in range(4):
                    for tb in (2 * i, 2 * i + 1):
                        for p in range(2):
                            last = nc.tensor.matmul(psc[i][:, tb % 2, p, :], qT[:, p, tb * P:(tb + 1) * P], keys[:, p, :], start=True, stop=True)
                    last.then_inc(tensor_done, 1)

        @block.scalar
        def _(act):
            act.sem_inc(scalar_done, 1)
            nc.scalar.preload_act_table_set(LOG_EXP)
            def scores(h, parity, first):
                for i in range(4):
                    act.wait_ge(tensor_done, E.after(("q", i), h))
                    nc.scalar.copy(qT[:, i // 2, (i % 2) * HALF:(i % 2 + 1) * HALF], pq[i][:, :]).then_inc(scalar_done, 1)
                if not first:
                    act.wait_ge(vector_done, V.after(("rank", TB + LAST - 1), h - 2))
                for i in range(4):
                    act.wait_ge(tensor_done, E.after(("score", i), h))
                    nc.scalar.copy(s[:, parity, 2 * i:2 * i + 2, :, :].rearrange("p b s k -> p (b s k)"),
                                   psc[i][:, :, :, :].rearrange("p b s k -> p (b s k)")).then_inc(scalar_done, 1)

            def exponentials(h):
                act.wait_ge(vector_done, V.after("shifted", h))
                nc.scalar.activation(ex[:, :, :], ex[:, :, :], ACT.Exp).then_inc(exp_done, 1)

            scores(0, 0, True)
            scores(1, 1, True)
            exponentials(0)
            with act.Fori(1, PEER_HEADS // 2) as i:
                scores(i * 2, 0, False)
                exponentials(i * 2 - 1)
                scores(i * 2 + 1, 1, False)
                exponentials(i * 2)
            exponentials(PEER_HEADS - 1)
        @block.vector
        def _(dve):
            dve.sem_inc(vector_done, 1)
            nc.vector.tensor_copy(rank_rows[:, :, :], bc(core.const("iota")[:, 0:K], 2, [P, K, TB * K])).then_inc(rank_rows_set, 1)
            dve.wait_ge(rank_rows_set, 1)

            def rank(h, parity):
                def chain(name):
                    dve.wait_ge(vector_done, V.after(name, h))

                for step in range(TB + LAST):
                    if step < TB and step % 2 == 0:
                        dve.wait_ge(scalar_done, A.after(("score", step // 2), h))
                    dve.wait_ge(vector_done, V.after(("rank", step - 1), h) if step else V.passes(h))
                    last = nc.vector.memset(pace[:, :], 0.0)
                    for p in range(2):
                        if step < TB:
                            last = nc.vector.max(val[:, step, p, 0:8], s[:, parity, step, p, :])
                        if 0 <= (tb := step - 1) < TB:
                            nc.vector.max_index(idx[:, tb, p, 0:8], val[:, tb, p, 0:8], s[:, parity, tb, p, :])
                            last = nc.vector.match_replace(rest[:, tb % 3, p, :], val[:, tb, p, 0:8], s[:, parity, tb, p, :], LOWEST)
                        if 0 <= (tb := step - 2) < TB:
                            last = nc.vector.max(val[:, tb, p, 8:16], rest[:, tb % 3, p, :])
                        if 0 <= (tb := step - 3) < TB:
                            last = nc.vector.max_index(idx[:, tb, p, 8:16], val[:, tb, p, 8:16], rest[:, tb % 3, p, :])
                    if 0 <= (tb := step - 3) < TB:
                        last = nc.vector.tensor_tensor(pair[:, tb % 3, :].rearrange("p (a b) -> p a b", b=K), bc(val[:, tb, 0, :], 2, [P, K, K]),
                                                       bc(val[:, tb, 1, :], 1, [P, K, K]), ALU.add)
                    if 0 <= (tb := step - 4) < TB:
                        last = nc.vector.max(top[:, tb, 0:8], pair[:, tb % 3, :])
                    if 0 <= (tb := step - 5) < TB:
                        nc.vector.max_index(pos[:, tb, 0:8], top[:, tb, 0:8], pair[:, tb % 3, :])
                        last = nc.vector.match_replace(pair_rest[:, tb % 3, :], top[:, tb, 0:8], pair[:, tb % 3, :], LOWEST)
                    if 0 <= (tb := step - 6) < TB:
                        last = nc.vector.max(top[:, tb, 8:16], pair_rest[:, tb % 3, :])
                    if 0 <= (tb := step - 7) < TB:
                        last = nc.vector.max_index(pos[:, tb, 8:16], top[:, tb, 8:16], pair_rest[:, tb % 3, :])
                    last.then_inc(vector_done, 1)
                chain(("rank", TB + LAST - 1))
                nc.vector.tensor_tensor(ex[:, :, :], top[:, :, :], top[:, :, 0:1].broadcast_to([P, TB, K]), ALU.subtract).then_inc(vector_done, 1)
                posf = pos[:, :, :].rearrange("p b k -> p (b k)")
                nc.vector.tensor_scalar(part[:, 0, :], posf, 4, None, ALU.logical_shift_right).then_inc(vector_done, 1)
                nc.vector.tensor_scalar(part[:, 1, :], posf, K - 1, None, ALU.bitwise_and).then_inc(vector_done, 1)
                chain("part1")
                nc.vector.tensor_copy(partf[:, :, :], part[:, :, :]).then_inc(vector_done, 1)
                dve.wait_ge(pool_done, G.passes(h))
                nc.vector.tensor_copy(idxf[:, :, :, :], idx[:, :, :, :].rearrange("p b s r -> p s r b")).then_inc(vector_done, 1)
                chain("idxf")
                for p in range(2):
                    nc.vector.tensor_tensor(hit[:, p, :, :], rank_rows[:, :, :], bc(partf[:, p, :], 1, [P, K, TB * K]), ALU.is_equal).then_inc(vector_done, 1)
                dve.wait_ge(exp_done, h + 1)
                nc.vector.tensor_reduce(total[:, 0, :], ex[:, :, :], AXX, ALU.add).then_inc(vector_done, 1)
                chain("sum")
                nc.vector.reciprocal(total[:, 1, :], total[:, 0, :]).then_inc(vector_done, 1)
                chain("recip")
                nc.vector.tensor_tensor(slot_gate[:, :, bass.ds(h * K, K)], ex[:, :, :], bc(total[:, 1, :], 2, [P, TB, K]), ALU.mult).then_inc(vector_done, 1)

            with dve.Fori(0, PEER_HEADS // 2) as i:
                rank(i * 2, 0)
                rank(i * 2 + 1, 1)

        @block.gpsimd
        def _(pool):
            pool.sem_inc(pool_done, 1)
            nc.gpsimd.memset(pool_pace[:, :], 0.0)
            with pool.Fori(0, PEER_HEADS) as h:
                for p in range(2):
                    pool.wait_ge(vector_done, V.after(f"equal{p}", h))
                    hit_by_block = hit[:, p, :, :].rearrange("p r (b k) -> p r b k", k=K)
                    nc.gpsimd.tensor_tensor(hit_by_block, hit_by_block, bc(idxf[:, p, :, :], 3, [P, K, TB, K]), ALU.mult).then_inc(pool_done, 1)
                wide = "hit"
                for m in (K // 2, K // 4, K // 8):
                    for p in range(2):
                        pool.wait_ge(pool_done, G.after((wide, p), h))
                        nc.gpsimd.tensor_tensor(hit[:, p, 0:m, :], hit[:, p, 0:m, :], hit[:, p, m:2 * m, :], ALU.add).then_inc(pool_done, 1)
                    wide = m
                pool.wait_ge(pool_done, G.after((wide, 1), h))
                nc.gpsimd.tensor_tensor(pool_pace[:, :], pool_pace[:, :], pool_pace[:, :], ALU.add)
                for p, out in enumerate((slot_row, slot_col)):
                    by_block = hit[:, p, 0:2, :].rearrange("p r (b k) -> p r b k", k=K)
                    nc.gpsimd.tensor_tensor(out[:, :, bass.ds(h * K, K)], by_block[:, 0, :, :], by_block[:, 1, :, :], ALU.add).then_inc(pool_done, 1)


def gate_matrix(nc, core, slot_row, slot_col, slot_gate, gates):
    PER, RING, BLOCK = 4, 4, 64
    TURNS = BLOCK // (PER * RING)
    NB = T // BLOCK
    with ExitStack() as ctx:
        sb, ps, sem = stage_tools(nc, ctx, "gm")
        rowT = sb("rowT", [P, T])
        colT = sb("colT", [P, T])
        gateT = sb("gateT", [P, T])
        hot_row = sb("hot_row", [P, RING, PER, KEYS])
        hot_col = sb("hot_col", [P, RING, PER, KEYS])
        staged = sb("staged", [P, 2, KEYS, BLOCK])
        pt = [ps(f"pt{i}", [P, 2, HALF]) for i in range(2)]
        pg = [ps(f"pg{i}", [P, PER, KEYS]) for i in range(RING)]
        turned, copied = sem("turned"), sem("copied")
        hot = [sem(f"hot{r}") for r in range(RING)]
        weighted = [sem(f"weighted{r}") for r in range(RING)]
        multiplied = [sem(f"multiplied{r}") for r in range(RING)]
        collected = [sem(f"collected{r}") for r in range(RING)]
        stored = [sem(f"stored{i}") for i in range(2)]
        block = ctx.enter_context(nc.Block())
        tables = ((slot_row, rowT), (slot_col, colT), (slot_gate, gateT))

        def turn_of(i, half, j):
            return i * (2 * TURNS) + (j + half * TURNS)

        @block.tensor
        def _(pe):
            for n, (table, _) in enumerate(tables):
                if n == 2:
                    pe.wait_ge(copied, 1)
                for tb in range(TB):
                    last = nc.tensor.transpose(pt[n % 2][:, tb // 4, (tb % 4) * P:(tb % 4 + 1) * P], table[:, tb, :], core.const("ident"))
                last.then_inc(turned, 1)
            for r in range(RING):
                pe.sem_inc(multiplied[r], 1)
            with pe.Fori(0, NB // 2) as i:
                for half in range(2):
                    with pe.Fori(0, TURNS) as j:
                        for r in range(RING):
                            n = turn_of(i, half, j)
                            pe.wait_ge(weighted[r], n + 1)
                            pe.wait_ge(collected[r], n + 1)
                            for x in range(PER):
                                last = nc.tensor.matmul(pg[r][:, x, :], hot_col[:, r, x, :], hot_row[:, r, x, :], start=True, stop=True)
                            last.then_inc(multiplied[r], 1)

        @block.vector
        def _(dve):
            dve.wait_ge(copied, 3)
            iota = bc(core.const("iota"), 1, [P, PER, KEYS])
            with dve.Fori(0, NB // 2) as i:
                for half in range(2):
                    with dve.Fori(0, TURNS) as j:
                        for r in range(RING):
                            n = turn_of(i, half, j)
                            dve.wait_ge(multiplied[r], n + 1)
                            for hot_one, index in ((hot_row, rowT), (hot_col, colT)):
                                t = bass.ds(n * (RING * PER) + r * PER, PER)
                                last = nc.vector.tensor_tensor(hot_one[:, r, :, :], iota, bc(index[:, t], 2, [P, PER, KEYS]), ALU.is_equal)
                            last.then_inc(hot[r], 1)

        @block.gpsimd
        def _(pool):
            pool.wait_ge(copied, 3)
            with pool.Fori(0, NB // 2) as i:
                for half in range(2):
                    with pool.Fori(0, TURNS) as j:
                        for r in range(RING):
                            n = turn_of(i, half, j)
                            pool.wait_ge(hot[r], n + 1)
                            gate = gateT[:, bass.ds(n * (RING * PER) + r * PER, PER)]
                            nc.gpsimd.tensor_tensor(hot_col[:, r, :, :], hot_col[:, r, :, :], bc(gate, 2, [P, PER, KEYS]), ALU.mult).then_inc(weighted[r], 1)

        @block.scalar
        def _(act):
            for n, (_, table) in enumerate(tables):
                act.wait_ge(turned, n + 1)
                nc.scalar.copy(table[:, :], pt[n % 2][:, :, :].rearrange("p a t -> p (a t)")).then_inc(copied, 1)
            for r in range(RING):
                act.sem_inc(collected[r], 1)
            with act.Fori(0, NB // 2) as i:
                for half in range(2):
                    act.wait_ge(stored[half], i * 16 + 16)
                    with act.Fori(0, TURNS) as j:
                        for r in range(RING):
                            act.wait_ge(multiplied[r], turn_of(i, half, j) + 2)
                            nc.scalar.copy(staged[:, half, :, bass.ds(j * (RING * PER) + r * PER, PER)].rearrange("p k t -> p t k"),
                                           pg[r][:, :, :]).then_inc(collected[r], 1)

        @block.sync
        def _(sp):
            for half in range(2):
                sp.sem_inc(stored[half], 16)
            with sp.Fori(0, NB // 2) as i:
                for half in range(2):
                    for r in range(RING):
                        sp.wait_ge(collected[r], i * (2 * TURNS) + ((half + 1) * TURNS + 1))
                    sp.dma_start(gates[bass.ds(i * 2 + half, 1), :, :].rearrange("b p n -> (b p) n"),
                                 staged[:, half, :, :].rearrange("p k t -> p (k t)")).then_inc(stored[half], 16)
            for half in range(2):
                sp.wait_ge(stored[half], 16 * (NB // 2 + 1))


def peer_experts(nc, uT, v, gates, h2T, acc):
    EG, BLOCK = 2, 64
    NG = KEYS // EG
    NB = T // BLOCK
    UNITS, RING = TB * 2, 4
    with ExitStack() as ctx:
        sb, ps, sem = stage_tools(nc, ctx, "pe")
        h2 = sb("h2_parts", [P, 2, KC, T], F32R)
        ut = sb("u_parts", [P, 2, EG, D], F32R)
        vt = sb("v_parts", [P, 2, EG, D], F32R)
        wt = sb("weight_parts", [P, 2, 2, EG, T], F32R)
        u_whole, v_whole, g_whole, w_whole = (h2T[:, EG * j:EG * (j + 1), :] for j in range(4))
        gt = g_whole.rearrange("p e (b t) -> p (e b) t", t=EG * BLOCK)
        pu = [ps(f"pu{i}", [P, 2, HALF]) for i in range(2)]
        pv = [ps(f"pv{i}", [P, HALF]) for i in range(RING)]
        u_in, v_in, g_in = sem("u_in"), sem("v_in"), sem("g_in")
        h_high, h_cut = sem("h_high"), sem("h_cut")
        u_high, u_cut, v_high, v_cut = sem("u_high"), sem("u_cut"), sem("v_high"), sem("v_cut")
        up_done, gelu_done, down_done = sem("up_done"), sem("gelu_done"), sem("down_done")
        gated, w_high, w_cut = sem("gated"), sem("w_high"), sem("w_cut")
        added = [sem(f"added{i}") for i in range(RING)]
        block = ctx.enter_context(nc.Block())
        gv = gates.rearrange("b p n -> p b n")

        @block.sync
        def _(sp):
            def load(n, first):
                sp.wait_ge(*((h_cut, EG) if first else (u_cut, n)))
                sp.dma_start(u_whole, uT[bass.ds(n * EG, EG), :, :].rearrange("e p n -> p e n")).then_inc(u_in, 16)
                sp.wait_ge(*((h_cut, 3 * EG) if first else (gated, n * EG)))
                sp.dma_start(gt, gv[:, :, bass.ds(n * (EG * BLOCK), EG * BLOCK)]).then_inc(g_in, 16)
                if not first:
                    sp.wait_ge(v_cut, n)
                sp.dma_start(v_whole, v[bass.ds(n * EG * P, EG * P), :].rearrange("(e p) d -> p e d", p=P)).then_inc(v_in, 16)

            load(0, True)
            with sp.Fori(1, NG) as n:
                load(n, False)

        def schedule(eng, up, down):
            up(0, 0, True)
            with eng.Fori(0, NG // 2 - 1) as i:
                for s in range(2):
                    up(i * 2 + (s + 1), 1 - s, False)
                    down(i * 2 + s, s, 2)
            up(NG - 1, 1, False)
            down(NG - 2, 0, 1)
            down(NG - 1, 1, 0)

        @block.tensor
        def _(pe):
            def up(n, s, first):
                pe.wait_ge(u_cut, n + 1)
                for e in range(EG):
                    if not first:
                        pe.wait_ge(gelu_done, (n - 1) * EG + (e + 1))
                    for k in range(KC):
                        if first and e == 0:
                            pe.wait_ge(h_cut, k + 1)
                        for half in range(2):
                            span = slice(half * HALF, (half + 1) * HALF)
                            last = product_of_parts(nc, pu[e][:, half, :], ut[:, 0, e, k * P:(k + 1) * P], ut[:, 1, e, k * P:(k + 1) * P],
                                                    h2[:, 0, k, span], h2[:, 1, k, span], k == 0, k == KC - 1)
                    last.then_inc(up_done, 1)

            def down(n, s, after):
                pe.wait_ge(v_cut, n + 1)
                pe.wait_ge(w_cut, n * EG + EG)
                for x in range(UNITS):
                    tb, half = x // 2, x % 2
                    tok, span = slice(tb * P, (tb + 1) * P), slice(half * HALF, (half + 1) * HALF)
                    pe.wait_ge(added[x % RING], n * (UNITS // RING) + (x // RING + 1))
                    for e in range(EG):
                        last = product_of_parts(nc, pv[x % RING][:, :], wt[:, 0, s, e, tok], wt[:, 1, s, e, tok],
                                                vt[:, 0, e, span], vt[:, 1, e, span], e == 0, e == EG - 1)
                    last.then_inc(down_done, 1)

            schedule(pe, up, down)

        @block.scalar
        def _(act):
            def high_u(n, first):
                act.wait_ge(u_in, n * 16 + 16)
                if not first:
                    act.wait_ge(up_done, n * EG)
                nc.scalar.copy(ut[:, 0, :, :], u_whole).then_inc(u_high, 1)

            def high_v(n, first):
                act.wait_ge(v_in, n * 16 + 16)
                if not first:
                    act.wait_ge(down_done, n * UNITS)
                nc.scalar.copy(vt[:, 0, :, :], v_whole).then_inc(v_high, 1)

            def up(n, s, first):
                for e in range(EG):
                    act.wait_ge(up_done, n * EG + (e + 1))
                    if not first:
                        act.wait_ge(w_cut, (n - 1) * EG + (e + 1))
                    nc.scalar.activation(w_whole[:, e, :], pu[e][:, :, :].rearrange("p a t -> p (a t)"), ACT.Gelu).then_inc(gelu_done, 1)
                if first:
                    high_u(1, False)

            def down(n, s, after):
                if after > 1:
                    high_u(n + 2, False)
                if after > 0:
                    high_v(n + 1, False)

            for k in range(KC):
                nc.scalar.copy(h2[:, 0, k, :], h2T[:, k, :]).then_inc(h_high, 1)
            high_u(0, True)
            high_v(0, True)
            schedule(act, up, down)

        @block.vector
        def _(dve):
            def up(n, s, first):
                dve.wait_ge(g_in, n * 16 + 16)
                for e in range(EG):
                    dve.wait_ge(gelu_done, n * EG + (e + 1))
                    whole = w_whole[:, e, :].rearrange("p (b t) -> p b t", t=BLOCK)
                    nc.vector.tensor_tensor(whole, whole, gt[:, :, e * BLOCK:(e + 1) * BLOCK], ALU.mult).then_inc(gated, 1)
                    dve.wait_ge(gated, n * EG + (e + 1))
                    nc.vector.tensor_copy(wt[:, 0, s, e, :], w_whole[:, e, :]).then_inc(w_high, 1)
                    dve.wait_ge(w_high, n * EG + (e + 1))
                    nc.vector.tensor_tensor(wt[:, 1, s, e, :], w_whole[:, e, :], wt[:, 0, s, e, :].bitcast(F32), ALU.subtract).then_inc(w_cut, 1)

            def down(n, s, after):
                for x in range(UNITS):
                    a = acc[:, x // 2, (x % 2) * HALF:(x % 2 + 1) * HALF]
                    dve.wait_ge(down_done, n * UNITS + (x + 1))
                    nc.vector.tensor_tensor(a, a, pv[x % RING][:, :], ALU.add).then_inc(added[x % RING], 1)

            for r in range(RING):
                dve.sem_inc(added[r], 1)
            for k in range(KC):
                dve.wait_ge(h_high, k + 1)
                nc.vector.tensor_tensor(h2[:, 1, k, :], h2T[:, k, :], h2[:, 0, k, :].bitcast(F32), ALU.subtract).then_inc(h_cut, 1)
            schedule(dve, up, down)

        @block.gpsimd
        def _(pool):
            def rest(cut, high, parts, whole, n):
                pool.wait_ge(high, n + 1)
                nc.gpsimd.tensor_tensor(parts[:, 1, :, :], whole, parts[:, 0, :, :].bitcast(F32), ALU.subtract).then_inc(cut, 1)

            def rest_u(n):
                rest(u_cut, u_high, ut, u_whole, n)

            def rest_v(n):
                rest(v_cut, v_high, vt, v_whole, n)

            rest_u(0)
            rest_v(0)
            rest_u(1)
            with pool.Fori(0, NG - 2) as n:
                rest_u(n + 2)
                rest_v(n + 1)
            rest_v(NG - 1)


def packed_consts():
    import numpy as np

    r, c = np.arange(P)[:, None], np.arange(P)[None, :]
    mats = {
        "ident": r == c,
        "neg_from": -1.0 * (r >= c),
        "neg_before": -1.0 * (r < c),
        "causal_bias": NEG * (r >= c),
        "upto": r <= c,
        "beyond": r > c,
        "ones": np.ones((P, P)),
        "iota": c + 0 * r,
    }
    parts = [mats[name] for name in CONSTS]
    for m in LEVELS:
        parts.append((r // (2 * m) == c // (2 * m)) & (r % (2 * m) < m) & (c % (2 * m) >= m))
    parts.append(r == c)
    t = np.arange(T)[None, :]
    parts.append((t % P != 0) + 0 * r)
    return np.ascontiguousarray(np.concatenate([np.asarray(m, np.float32) for m in parts], axis=1))


def hybrid_layer(nc, a, gates, out):
    with ExitStack() as ctx:
        def sb(stack, name, shape):
            return stack.enter_context(nc.sbuf_tensor(name, shape, F32))

        hT = mergedT = h2T = sb(ctx, "hT_h2T", [P, KC, T])
        y_sb_hg = acc = sb(ctx, "y_acc", [P, KC, T])
        ysbT, yhgT = y_sb_hg[:, 0:KC // 2, :], y_sb_hg[:, KC // 2:KC, :]
        with ExitStack() as upto_gates:
            core = Core(nc, upto_gates)
            yssdT = sb(upto_gates, "yssdT", [P, KC // 2, T])
            select_weights = SelectWeights(nc, upto_gates, a["peer_w_q"], a["keysT"], yssdT)
            with ExitStack() as mixer:
                sb_weights = Weights(nc, mixer, "sb_w", a["w_in"], yhgT, (COL_Q, COL_K, COL_V))
                hg_weights = Weights(nc, mixer, "hg_w", a["w_in"], yssdT, (COL_HF, COL_HQ, COL_HI, COL_HG))
                norm_input(nc, core, a["x"], a["norm1_w"], a["consts"], hT, sb_weights)
                stick_breaking(nc, core, sb_weights, hT, ysbT, hg_weights)
                with ExitStack() as recurrences:
                    ssd_weights = SsdWeights(nc, recurrences, a["w_in"])
                    hgrn2(nc, core, hg_weights, a["lb_logits"], a["hg_norm_w"], hT, yhgT, ssd_weights)
                    ssd(nc, core, ssd_weights, a["conv_wb"], a["ssd_rows"], a["ssd_norm_w"], hT, yssdT)
                merge(nc, core, a["w_in"], a["branch_w"], hT, [ysbT, yhgT, yssdT])
                output_and_norm(nc, core, a["x"], a["w_out"], a["norm2_w"], mergedT, acc, h2T, select_weights)
            slots = [sb(upto_gates, name, [P, TB, P]) for name in ("slot_row", "slot_col", "slot_gate")]
            peer_select(nc, core, select_weights, h2T, *slots)
            gate_matrix(nc, core, *slots, gates)
        peer_experts(nc, a["uT"], a["v"], gates, h2T, acc)
        norm_output(nc, a["final_norm_w"], acc, out)


def columns(w):
    return w.reshape(-1, P).T


def kernel(x, norm1_w, w_in, hg_lb_logits, hg_norm_w, ssd_conv_w, ssd_conv_b, ssd_dt_bias, ssd_a_log, ssd_d, ssd_norm_w,
           w_branch_sb, w_branch_hg, w_branch_ssd, w_out, norm2_w, peer_w_q, peer_sub_keys, peer_u, peer_v, final_norm_w):
    import concourse.bacc as bacc
    import numpy as np
    from concourse.bass_utils import run_bass_kernel_spmd

    laid_out = {
        "x": x[0],
        "norm1_w": columns(norm1_w[0]),
        "w_in": w_in[0],
        "lb_logits": columns(hg_lb_logits[0]),
        "hg_norm_w": columns(hg_norm_w[0]),
        "conv_wb": np.concatenate([ssd_conv_w[0].T, ssd_conv_b[0][:, None]], axis=1),
        "ssd_rows": np.stack([ssd_dt_bias[0], ssd_a_log[0], ssd_d[0]])[None],
        "ssd_norm_w": columns(ssd_norm_w[0]),
        "branch_w": np.concatenate([w_branch_sb, w_branch_hg, w_branch_ssd]),
        "w_out": w_out[0],
        "norm2_w": columns(norm2_w[0]),
        "peer_w_q": peer_w_q[0],
        "keysT": peer_sub_keys[0].reshape(2 * PEER_HEADS, KEYS, P).transpose(0, 2, 1),
        "uT": peer_u[0].reshape(KEYS, KEYS, KC, P).transpose(0, 3, 2, 1).reshape(KEYS, P, D),
        "v": peer_v[0],
        "final_norm_w": final_norm_w[None],
        "consts": packed_consts(),
    }
    laid_out = {name: np.ascontiguousarray(value) for name, value in laid_out.items()}
    nc = bacc.Bacc("TRN2", target_bir_lowering=False, num_devices=1)
    aps = {name: nc.dram_tensor(f"{name}_dram", value.shape, mybir.dt.from_np(value.dtype), kind="ExternalInput").ap()
           for name, value in laid_out.items()}
    gates = nc.dram_tensor("gates_dram", (T // 64, P, KEYS * 64), F32, kind="Internal").ap()
    out = nc.dram_tensor("out_dram", (T, D), F32, kind="ExternalOutput").ap()
    hybrid_layer(nc, aps, gates, out)
    result = run_bass_kernel_spmd(nc, [{f"{name}_dram": value for name, value in laid_out.items()}], core_ids=[0])
    return result.results[0]["out_dram"].reshape(1, T, D)
```
